# Optimizing a Trainium2 kernel written in Bass

```python
import math
import jax, jax.numpy as jnp
from jax import lax
import numpy as np
import jax
import jax.numpy as jnp

D_MODEL = 1024
BATCH = 1
SEQ = 256
DEPTH = 2

D_MIX = D_MODEL
SSD_INNER = D_MIX // 2
SSD_HEAD_DIM = 64
SSD_HEADS = SSD_INNER // SSD_HEAD_DIM
SSD_GROUPS = 2
SSD_STATE = 128
SSD_CONV = 4
SSD_CHUNK = 128
SSD_XBC = SSD_INNER + 2 * SSD_GROUPS * SSD_STATE
POOL_WIDTH = D_MIX // 4
POOL_GROUPS = 4
POOL_GROUP_DIM = POOL_WIDTH // POOL_GROUPS
ATTN_WIDTH = D_MIX - SSD_INNER - POOL_WIDTH
ATTN_HEAD_DIM = 64
ATTN_HEADS = ATTN_WIDTH // ATTN_HEAD_DIM
ROPE_DIM = ATTN_HEAD_DIM // 4
ROPE_THETA = 500000.0
MOBA_BLOCK = 256
MOBA_TOPK = 3
MOBA_QCHUNK = 64
D_FF = 2816
RMS_EPS = 1e-6

OFF_Z = 0
OFF_XBC = OFF_Z + SSD_INNER
OFF_DT = OFF_XBC + SSD_XBC
OFF_POOL = OFF_DT + SSD_HEADS
OFF_Q = OFF_POOL + POOL_WIDTH
OFF_K = OFF_Q + ATTN_WIDTH
OFF_V = OFF_K + ATTN_WIDTH
IN_COLS = OFF_V + ATTN_WIDTH


def _rmsnorm(x, g):
    x32 = x.astype(jnp.float32)
    y = x32 * lax.rsqrt(jnp.mean(x32 * x32, axis=-1, keepdims=True) + RMS_EPS)
    return y.astype(x.dtype) * g

def _swiglu(h, wg, wu, wd):
    return (jax.nn.silu(h @ wg) * (h @ wu)) @ wd

def _partial_rope(t, pos):
    half = ROPE_DIM // 2
    inv_freq = ROPE_THETA ** (-jnp.arange(0, ROPE_DIM, 2, dtype=jnp.float32) / ROPE_DIM)
    ang = pos[:, None] * inv_freq[None, :]
    cos = jnp.cos(ang)[None, :, None, :]
    sin = jnp.sin(ang)[None, :, None, :]
    t32 = t[..., :ROPE_DIM].astype(jnp.float32)
    x1, x2 = t32[..., :half], t32[..., half:]
    rot = jnp.concatenate([x1 * cos - x2 * sin, x2 * cos + x1 * sin], axis=-1).astype(t.dtype)
    return jnp.concatenate([rot, t[..., ROPE_DIM:]], axis=-1)

def _ssd_chunked(xdt, dA, Bm, Cm):
    b, S, H, P = xdt.shape
    G = SSD_GROUPS
    HG = H // G
    N = Bm.shape[-1]
    L = SSD_CHUNK
    nc = S // L
    x = xdt.reshape(b, nc, L, G, HG, P)
    a = dA.reshape(b, nc, L, G, HG).transpose(0, 3, 4, 1, 2)
    Bc = Bm.reshape(b, nc, L, G, N)
    Cc = Cm.reshape(b, nc, L, G, N)
    a_cs = jnp.cumsum(a, axis=-1)
    causal = jnp.tril(jnp.ones((L, L), dtype=bool))
    seg = jnp.exp(jnp.where(causal, a_cs[..., :, None] - a_cs[..., None, :], -jnp.inf))
    cb = jnp.einsum('bclgn,bcsgn->bgcls', Cc, Bc)
    y_diag = jnp.einsum('bgcls,bghcls,bcsghp->bclghp', cb, seg, x)
    decay_in = jnp.exp(a_cs[..., -1:] - a_cs)
    states = jnp.einsum('bclgn,bghcl,bclghp->bcghpn', Bc, decay_in, x)
    chunk_decay = jnp.exp(a_cs[..., -1])

    def step(h, inp):
        st, dec = inp
        return h * dec[..., None, None] + st, h

    h0 = jnp.zeros(states.shape[:1] + states.shape[2:], states.dtype)
    _, prev = lax.scan(step, h0, (jnp.moveaxis(states, 1, 0), jnp.moveaxis(chunk_decay, -1, 0)))
    prev = jnp.moveaxis(prev, 0, 1)
    y_off = jnp.einsum('bclgn,bcghpn,bghcl->bclghp', Cc, prev, jnp.exp(a_cs))
    return (y_diag + y_off).reshape(b, S, H, P)

def _ssd_mixer(z, xbc, dt_raw, conv_w, conv_b, dt_bias, a_log, d_skip, norm_g):
    b, S, C = xbc.shape
    xbc = lax.conv_general_dilated(
        xbc, conv_w[:, None, :], window_strides=(1,), padding=[(SSD_CONV - 1, 0)],
        dimension_numbers=('NWC', 'WIO', 'NWC'), feature_group_count=C)
    xbc = jax.nn.silu(xbc + conv_b)
    gn = SSD_GROUPS * SSD_STATE
    xs = xbc[..., :SSD_INNER].reshape(b, S, SSD_HEADS, SSD_HEAD_DIM)
    Bm = xbc[..., SSD_INNER:SSD_INNER + gn].reshape(b, S, SSD_GROUPS, SSD_STATE)
    Cm = xbc[..., SSD_INNER + gn:].reshape(b, S, SSD_GROUPS, SSD_STATE)
    dt = jax.nn.softplus((dt_raw + dt_bias).astype(jnp.float32))
    A = -jnp.exp(a_log.astype(jnp.float32))
    y = _ssd_chunked(xs * dt[..., None], dt * A, Bm, Cm)
    y = y + d_skip[:, None] * xs
    y = y.reshape(b, S, SSD_INNER).astype(z.dtype)
    return _rmsnorm(y * jax.nn.silu(z), norm_g)

def _pool_mixer(u, pool_w, pool_scale):
    S = u.shape[1]
    c = jnp.cumsum(u.astype(jnp.float32), axis=1)
    t = jnp.arange(1, S + 1, dtype=jnp.float32)
    outs = []
    for g in range(POOL_GROUPS):
        w = 2 ** (g + 1)
        sl = slice(g * POOL_GROUP_DIM, (g + 1) * POOL_GROUP_DIM)
        cg = c[..., sl]
        shifted = jnp.pad(cg, ((0, 0), (w, 0), (0, 0)))[:, :S]
        mean = (cg - shifted) / jnp.minimum(t, float(w))[None, :, None]
        outs.append(jnp.einsum('bsc,cd->bsd', (mean - u[..., sl]).astype(u.dtype), pool_w[g]))
    return jnp.concatenate(outs, axis=-1) * pool_scale

def _moba_attention(q, k, v):
    b, S, H, Dh = q.shape
    q = q.transpose(0, 2, 1, 3)
    k = k.transpose(0, 2, 1, 3)
    v = v.transpose(0, 2, 1, 3)
    nb = -(-S // MOBA_BLOCK)
    sp = nb * MOBA_BLOCK
    topk = min(MOBA_TOPK, nb)
    pad = ((0, 0), (0, 0), (0, sp - S), (0, 0))
    k_pad = jnp.pad(k, pad)
    v_pad = jnp.pad(v, pad)
    kb = k_pad.reshape(b, H, nb, MOBA_BLOCK, Dh)
    vb = v_pad.reshape(b, H, nb, MOBA_BLOCK, Dh)
    k_mean = jnp.mean(kb.astype(jnp.float32), axis=3)
    gate = jnp.einsum('bhsd,bhnd->bhsn', q.astype(jnp.float32), k_mean)
    q_blk = jnp.arange(S) // MOBA_BLOCK
    past = jnp.arange(nb)[None, :] < q_blk[:, None]
    gate = jnp.where(past, gate, -jnp.inf)
    _, sel = lax.top_k(gate, topk)
    sel_valid = sel < q_blk[None, None, :, None]
    nq = S // MOBA_QCHUNK

    def chunks(t):
        return jnp.moveaxis(t.reshape((b, H, nq, MOBA_QCHUNK) + t.shape[3:]), 2, 0)

    bidx = jnp.arange(b)[:, None, None, None]
    hidx = jnp.arange(H)[None, :, None, None]
    scale = Dh ** -0.5

    def attend(args):
        qi, si, vi, ci = args
        start = ci * MOBA_QCHUNK
        q_pos = start + jnp.arange(MOBA_QCHUNK)
        kg = kb[bidx, hidx, si]
        vg = vb[bidx, hidx, si]
        s_sel = jnp.einsum('bhqd,bhqkjd->bhqkj', qi, kg).astype(jnp.float32) * scale
        s_sel = jnp.where(vi[..., None], s_sel, -jnp.inf).reshape(b, H, MOBA_QCHUNK, topk * MOBA_BLOCK)
        own = (start // MOBA_BLOCK) * MOBA_BLOCK
        ko = lax.dynamic_slice_in_dim(k_pad, own, MOBA_BLOCK, axis=2)
        vo = lax.dynamic_slice_in_dim(v_pad, own, MOBA_BLOCK, axis=2)
        s_own = jnp.einsum('bhqd,bhjd->bhqj', qi, ko).astype(jnp.float32) * scale
        k_pos = own + jnp.arange(MOBA_BLOCK)
        s_own = jnp.where(k_pos[None, :] <= q_pos[:, None], s_own, -jnp.inf)
        p = jax.nn.softmax(jnp.concatenate([s_sel, s_own], axis=-1), axis=-1).astype(v.dtype)
        p_sel = p[..., :topk * MOBA_BLOCK].reshape(b, H, MOBA_QCHUNK, topk, MOBA_BLOCK)
        return (jnp.einsum('bhqkj,bhqkjd->bhqd', p_sel, vg)
                + jnp.einsum('bhqj,bhjd->bhqd', p[..., topk * MOBA_BLOCK:], vo))

    out = lax.map(attend, (chunks(q), chunks(sel), chunks(sel_valid), jnp.arange(nq)))
    out = jnp.moveaxis(out, 0, 2).reshape(b, H, S, Dh)
    return out.transpose(0, 2, 1, 3).reshape(b, S, H * Dh)

def _hybrid_mixer(h, w_in, conv_w, conv_b, dt_bias, a_log, d_skip, ssd_norm, pool_w, pool_scale, w_out):
    b, S, _ = h.shape
    proj = h @ w_in
    z = proj[..., OFF_Z:OFF_XBC]
    xbc = proj[..., OFF_XBC:OFF_DT]
    dt_raw = proj[..., OFF_DT:OFF_POOL]
    u = proj[..., OFF_POOL:OFF_Q]
    pos = jnp.arange(S, dtype=jnp.float32)
    q = _partial_rope(proj[..., OFF_Q:OFF_K].reshape(b, S, ATTN_HEADS, ATTN_HEAD_DIM), pos)
    k = _partial_rope(proj[..., OFF_K:OFF_V].reshape(b, S, ATTN_HEADS, ATTN_HEAD_DIM), pos)
    v = proj[..., OFF_V:IN_COLS].reshape(b, S, ATTN_HEADS, ATTN_HEAD_DIM)
    y_ssd = _ssd_mixer(z, xbc, dt_raw, conv_w, conv_b, dt_bias, a_log, d_skip, ssd_norm)
    y_pool = _pool_mixer(u, pool_w, pool_scale).astype(h.dtype)
    y_attn = _moba_attention(q, k, v)
    return jnp.concatenate([y_ssd, y_pool, y_attn], axis=-1) @ w_out

def first_inputs(seed: int = 0) -> dict:
    key = jax.random.key(seed)
    ks = jax.random.split(key, 24)
    f32 = jnp.float32

    def nrm(k, shape, fan_in):
        return jax.random.normal(k, shape, f32) * fan_in ** -0.5

    def gain(k, shape):
        return 1.0 + 0.05 * jax.random.normal(k, shape, f32)

    u_dt = jax.random.uniform(ks[9], (DEPTH, SSD_HEADS), f32)
    dt0 = jnp.exp(u_dt * (math.log(0.1) - math.log(0.001)) + math.log(0.001))
    dt_bias = dt0 + jnp.log(-jnp.expm1(-dt0))
    a_log = jnp.log(jax.random.uniform(ks[10], (DEPTH, SSD_HEADS), f32, 1.0, 16.0))
    return {
        "x": jax.random.normal(ks[0], (BATCH, SEQ, D_MODEL), f32),
        "ff1_norm_pre": gain(ks[1], (DEPTH, D_MODEL)),
        "ff1_w_gate": nrm(ks[2], (DEPTH, D_MODEL, D_FF), D_MODEL),
        "ff1_w_up": nrm(ks[3], (DEPTH, D_MODEL, D_FF), D_MODEL),
        "ff1_w_down": nrm(ks[4], (DEPTH, D_FF, D_MODEL), D_FF),
        "ff1_norm_post": gain(ks[5], (DEPTH, D_MODEL)),
        "mix_norm_pre": gain(ks[6], (DEPTH, D_MODEL)),
        "w_in": nrm(ks[7], (DEPTH, D_MODEL, IN_COLS), D_MODEL),
        "conv_w": nrm(ks[8], (DEPTH, SSD_CONV, SSD_XBC), SSD_CONV),
        "conv_b": 0.01 * jax.random.normal(ks[11], (DEPTH, SSD_XBC), f32),
        "dt_bias": dt_bias,
        "a_log": a_log,
        "d_skip": gain(ks[12], (DEPTH, SSD_HEADS)),
        "ssd_norm": gain(ks[13], (DEPTH, SSD_INNER)),
        "pool_w": nrm(ks[14], (DEPTH, POOL_GROUPS, POOL_GROUP_DIM, POOL_GROUP_DIM), POOL_GROUP_DIM),
        "pool_scale": gain(ks[15], (DEPTH, POOL_WIDTH)),
        "w_out": nrm(ks[16], (DEPTH, D_MIX, D_MODEL), D_MIX),
        "mix_norm_post": gain(ks[17], (DEPTH, D_MODEL)),
        "ff2_norm_pre": gain(ks[18], (DEPTH, D_MODEL)),
        "ff2_w_gate": nrm(ks[19], (DEPTH, D_MODEL, D_FF), D_MODEL),
        "ff2_w_up": nrm(ks[20], (DEPTH, D_MODEL, D_FF), D_MODEL),
        "ff2_w_down": nrm(ks[21], (DEPTH, D_FF, D_MODEL), D_FF),
        "ff2_norm_post": gain(ks[22], (DEPTH, D_MODEL)),
    }

def first_block(x, ff1_norm_pre, ff1_w_gate, ff1_w_up, ff1_w_down, ff1_norm_post,
              mix_norm_pre, w_in, conv_w, conv_b, dt_bias, a_log, d_skip, ssd_norm,
              pool_w, pool_scale, w_out, mix_norm_post,
              ff2_norm_pre, ff2_w_gate, ff2_w_up, ff2_w_down, ff2_norm_post):
    h = x
    for l in range(DEPTH):
        f = _swiglu(_rmsnorm(h, ff1_norm_pre[l]), ff1_w_gate[l], ff1_w_up[l], ff1_w_down[l])
        h = h + 0.5 * _rmsnorm(f, ff1_norm_post[l])
        m = _hybrid_mixer(_rmsnorm(h, mix_norm_pre[l]), w_in[l], conv_w[l], conv_b[l], dt_bias[l],
                          a_log[l], d_skip[l], ssd_norm[l], pool_w[l], pool_scale[l], w_out[l])
        h = h + _rmsnorm(m, mix_norm_post[l])
        f = _swiglu(_rmsnorm(h, ff2_norm_pre[l]), ff2_w_gate[l], ff2_w_up[l], ff2_w_down[l])
        h = h + 0.5 * _rmsnorm(f, ff2_norm_post[l])
    return h


GRID_W = 64
CTX_LEN = 256
HEAD_DIM = 64
N_HEADS_A = 8
N_KV_A = 2
N_HEADS_B = 8
N_KV_B = 2
G_A = N_HEADS_A // N_KV_A
G_B = N_HEADS_B // N_KV_B
QA = N_HEADS_A * HEAD_DIM
KVA = N_KV_A * HEAD_DIM
QB = N_HEADS_B * HEAD_DIM
KVB = N_KV_B * HEAD_DIM
IN_PROJ_WIDTH = QA + 2 * KVA + QB + 2 * KVB
IN_SPLITS = (QA, QA + KVA, QA + 2 * KVA, QA + 2 * KVA + QB, QA + 2 * KVA + QB + KVB)
MIX_OUT_WIDTH = QA + QB
WINDOW = 128
Q_BLOCK = 128
ROPE_THETA_2 = 10000.0
ATTN_SCALE = HEAD_DIM ** -0.5
CONV_WIDTH = 3
N_EXPERTS = 8
TOP_K = 2
D_FF_EXPERT = 3584
N_ADA = 6
EPS = 1e-6
N_ATTN_LAYERS = (DEPTH + 1) // 2
N_CONV_LAYERS = DEPTH // 2


def rms_norm(x, g):
    xf = x.astype(jnp.float32)
    y = xf * lax.rsqrt(jnp.mean(xf * xf, axis=-1, keepdims=True) + EPS)
    return (y * g.astype(jnp.float32)).astype(x.dtype)

def axial_rope_tables(n_tokens):
    rows = n_tokens // GRID_W
    row, col = jnp.meshgrid(jnp.arange(rows, dtype=jnp.float32), jnp.arange(GRID_W, dtype=jnp.float32), indexing='ij')
    half = HEAD_DIM // 2
    inv_freq = ROPE_THETA_2 ** (-jnp.arange(0, half, 2, dtype=jnp.float32) / half)
    ang = jnp.concatenate([row.reshape(-1, 1) * inv_freq, col.reshape(-1, 1) * inv_freq], axis=-1)
    return jnp.cos(ang), jnp.sin(ang)

def apply_rope(x, cos, sin):
    shape = (cos.shape[0],) + (1,) * (x.ndim - 3) + (cos.shape[1],)
    cs, sn = cos.reshape(shape), sin.reshape(shape)
    xr = x.astype(jnp.float32).reshape(x.shape[:-1] + (HEAD_DIM // 2, 2))
    x0, x1 = xr[..., 0], xr[..., 1]
    out = jnp.stack([x0 * cs - x1 * sn, x0 * sn + x1 * cs], axis=-1)
    return out.reshape(x.shape).astype(x.dtype)

def softmax_with_sink(s, sink):
    sk = sink.astype(jnp.float32)[:, :, None, None]
    m = jnp.maximum(jnp.max(s, axis=-1, keepdims=True), sk)
    p = jnp.exp(s - m)
    return p / (jnp.sum(p, axis=-1, keepdims=True) + jnp.exp(sk - m))

def project_heads(h, w_in, qn_a, kn_a, qn_b, kn_b):
    bsz, n, _ = h.shape
    qa, ka, va, qb, kb, vb = jnp.split(h @ w_in, IN_SPLITS, axis=-1)
    qa = rms_norm(qa.reshape(bsz, n, N_KV_A, G_A, HEAD_DIM), qn_a)
    ka = rms_norm(ka.reshape(bsz, n, N_KV_A, HEAD_DIM), kn_a)
    va = va.reshape(bsz, n, N_KV_A, HEAD_DIM)
    qb = rms_norm(qb.reshape(bsz, n, N_KV_B, G_B, HEAD_DIM), qn_b)
    kb = rms_norm(kb.reshape(bsz, n, N_KV_B, HEAD_DIM), kn_b)
    vb = vb.reshape(bsz, n, N_KV_B, HEAD_DIM)
    return qa, ka, va, qb, kb, vb

def context_attention(q, k, v, sink):
    s = jnp.einsum('bqhgd,bkhd->bhgqk', q, k).astype(jnp.float32) * ATTN_SCALE
    p = jax.nn.softmax(s, axis=-1) if sink is None else softmax_with_sink(s, sink)
    return jnp.einsum('bhgqk,bkhd->bqhgd', p.astype(v.dtype), v)

def global_attention(q, k_lat, v_lat, k_ctx, v_ctx):
    bsz, n = q.shape[:2]
    nb = n // Q_BLOCK
    k = jnp.concatenate([k_ctx, k_lat], axis=1)
    v = jnp.concatenate([v_ctx, v_lat], axis=1)
    qb = jnp.moveaxis(q.reshape((bsz, nb, Q_BLOCK) + q.shape[2:]), 1, 0)

    def block(q_blk):
        s = jnp.einsum('bqhgd,bkhd->bhgqk', q_blk, k).astype(jnp.float32) * ATTN_SCALE
        p = jax.nn.softmax(s, axis=-1)
        return jnp.einsum('bhgqk,bkhd->bqhgd', p.astype(v.dtype), v)

    out = lax.map(block, qb)
    return jnp.moveaxis(out, 0, 1).reshape(q.shape)

def window_attention(q, k_lat, v_lat, k_ctx, v_ctx, sink):
    bsz, n = q.shape[:2]
    nb = n // Q_BLOCK
    span = Q_BLOCK + 2 * WINDOW
    pad = ((0, 0), (WINDOW, WINDOW), (0, 0), (0, 0))
    kp = jnp.pad(k_lat, pad)
    vp = jnp.pad(v_lat, pad)
    qb = jnp.moveaxis(q.reshape((bsz, nb, Q_BLOCK) + q.shape[2:]), 1, 0)
    rel = jnp.arange(Q_BLOCK)[:, None] - jnp.arange(span)[None, :] + WINDOW
    band = jnp.abs(rel) <= WINDOW
    s_ctx_all = None

    def block(args):
        bi, q_blk = args
        start = bi * Q_BLOCK
        kb = lax.dynamic_slice_in_dim(kp, start, span, axis=1)
        vb = lax.dynamic_slice_in_dim(vp, start, span, axis=1)
        kpos = start - WINDOW + jnp.arange(span)
        valid = band & ((kpos >= 0) & (kpos < n))[None, :]
        s_loc = jnp.einsum('bqhgd,bkhd->bhgqk', q_blk, kb).astype(jnp.float32) * ATTN_SCALE
        s_loc = jnp.where(valid, s_loc, -jnp.inf)
        s_ctx = jnp.einsum('bqhgd,bkhd->bhgqk', q_blk, k_ctx).astype(jnp.float32) * ATTN_SCALE
        p = softmax_with_sink(jnp.concatenate([s_ctx, s_loc], axis=-1), sink)
        vv = jnp.concatenate([v_ctx, vb], axis=1)
        return jnp.einsum('bhgqk,bkhd->bqhgd', p.astype(vv.dtype), vv)

    out = lax.map(block, (jnp.arange(nb), qb))
    return jnp.moveaxis(out, 0, 1).reshape(q.shape)

def attn_mixer(h_lat, h_ctx, w_in, w_out, qn_a, kn_a, qn_b, kn_b, sink, cos, sin, with_ctx_out):
    bsz, n = h_lat.shape[:2]
    qa_l, ka_l, va_l, qb_l, kb_l, vb_l = project_heads(h_lat, w_in, qn_a, kn_a, qn_b, kn_b)
    qa_c, ka_c, va_c, qb_c, kb_c, vb_c = project_heads(h_ctx, w_in, qn_a, kn_a, qn_b, kn_b)
    qa_l, ka_l, qb_l, kb_l = [apply_rope(t, cos, sin) for t in (qa_l, ka_l, qb_l, kb_l)]
    sink = sink.reshape(N_KV_B, G_B)
    o_a = global_attention(qa_l, ka_l, va_l, ka_c, va_c).reshape(bsz, n, QA)
    o_b = window_attention(qb_l, kb_l, vb_l, kb_c, vb_c, sink).reshape(bsz, n, QB)
    out_lat = jnp.concatenate([o_a, o_b], axis=-1) @ w_out
    if not with_ctx_out:
        return out_lat, None
    n_ctx = h_ctx.shape[1]
    oa_c = context_attention(qa_c, ka_c, va_c, None).reshape(bsz, n_ctx, QA)
    ob_c = context_attention(qb_c, kb_c, vb_c, sink).reshape(bsz, n_ctx, QB)
    out_ctx = jnp.concatenate([oa_c, ob_c], axis=-1) @ w_out
    return out_lat, out_ctx

def short_conv_mixer(h, w_in, conv_w, w_out):
    n = h.shape[1]
    b_gate, c_gate, u = jnp.split(h @ w_in, 3, axis=-1)
    z = c_gate * u
    r = CONV_WIDTH // 2
    zp = jnp.pad(z, ((0, 0), (r, r), (0, 0)))
    conv = zp[:, 0:n] * conv_w[0]
    for j in range(1, CONV_WIDTH):
        conv = conv + zp[:, j:j + n] * conv_w[j]
    return (b_gate * conv) @ w_out

def swiglu(h, w_gate, w_up, w_down):
    return (jax.nn.silu(h @ w_gate) * (h @ w_up)) @ w_down

def moe_swiglu(h, router_w, w_gate, w_up, w_down):
    logits = (h @ router_w).astype(jnp.float32)
    top_vals, top_idx = lax.top_k(logits, TOP_K)
    weights = jax.nn.softmax(top_vals, axis=-1)
    gates = jnp.sum(jax.nn.one_hot(top_idx, N_EXPERTS, dtype=jnp.float32) * weights[..., None], axis=-2)
    gates = gates.astype(h.dtype)
    out = gates[..., 0:1] * swiglu(h, w_gate[0], w_up[0], w_down[0])
    for e in range(1, N_EXPERTS):
        out = out + gates[..., e:e + 1] * swiglu(h, w_gate[e], w_up[e], w_down[e])
    return out

def second_inputs(seed: int = 0) -> dict:
    key = jax.random.key(seed)
    ks = jax.random.split(key, 25)
    f32 = jnp.float32
    D = D_MODEL
    NE, NO = N_ATTN_LAYERS, N_CONV_LAYERS

    def nrm(k, shape, scale):
        return jax.random.normal(k, shape, f32) * scale

    return {
        'x': nrm(ks[0], (BATCH, SEQ, D), 1.0),
        'c': nrm(ks[1], (BATCH, D), 1.0),
        'ctx': nrm(ks[2], (BATCH, CTX_LEN, D), 1.0),
        'c_ctx': nrm(ks[3], (D,), 1.0),
        'ada_w': nrm(ks[4], (DEPTH, D, N_ADA * D), 0.5 * D ** -0.5),
        'ada_b': nrm(ks[5], (DEPTH, N_ADA * D), 0.01),
        'norm1_g': 1.0 + nrm(ks[6], (DEPTH, D), 0.05),
        'norm2_g': 1.0 + nrm(ks[7], (DEPTH, D), 0.05),
        'attn_w_in': nrm(ks[8], (NE, D, IN_PROJ_WIDTH), D ** -0.5),
        'attn_w_out': nrm(ks[9], (NE, MIX_OUT_WIDTH, D), MIX_OUT_WIDTH ** -0.5),
        'qnorm_a': 1.0 + nrm(ks[10], (NE, HEAD_DIM), 0.05),
        'knorm_a': 1.0 + nrm(ks[11], (NE, HEAD_DIM), 0.05),
        'qnorm_b': 1.0 + nrm(ks[12], (NE, HEAD_DIM), 0.05),
        'knorm_b': 1.0 + nrm(ks[13], (NE, HEAD_DIM), 0.05),
        'sink_b': nrm(ks[14], (NE, N_HEADS_B), 0.5),
        'ffn_w_gate': nrm(ks[15], (NE, D, D_FF), D ** -0.5),
        'ffn_w_up': nrm(ks[16], (NE, D, D_FF), D ** -0.5),
        'ffn_w_down': nrm(ks[17], (NE, D_FF, D), D_FF ** -0.5),
        'conv_w_in': nrm(ks[18], (NO, D, 3 * D), D ** -0.5),
        'conv_w': nrm(ks[19], (NO, CONV_WIDTH, D), CONV_WIDTH ** -0.5),
        'conv_w_out': nrm(ks[20], (NO, D, D), D ** -0.5),
        'router_w': nrm(ks[21], (NO, D, N_EXPERTS), D ** -0.5),
        'moe_w_gate': nrm(ks[22], (NO, N_EXPERTS, D, D_FF_EXPERT), D ** -0.5),
        'moe_w_up': nrm(ks[23], (NO, N_EXPERTS, D, D_FF_EXPERT), D ** -0.5),
        'moe_w_down': nrm(ks[24], (NO, N_EXPERTS, D_FF_EXPERT, D), D_FF_EXPERT ** -0.5),
    }

def second_block(x, c, ctx, c_ctx, ada_w, ada_b, norm1_g, norm2_g, attn_w_in, attn_w_out, qnorm_a, knorm_a, qnorm_b, knorm_b, sink_b, ffn_w_gate, ffn_w_up, ffn_w_down, conv_w_in, conv_w, conv_w_out, router_w, moe_w_gate, moe_w_up, moe_w_down):
    n_tok = x.shape[1]
    cos, sin = axial_rope_tables(n_tok)
    silu_c = jax.nn.silu(c)
    silu_cc = jax.nn.silu(c_ctx)
    xc = ctx
    for layer in range(DEPTH):
        i = layer // 2
        ctx_needed = any(j % 2 == 0 for j in range(layer + 1, DEPTH))
        sh1, sc1, g1, sh2, sc2, g2 = jnp.split((silu_c @ ada_w[layer] + ada_b[layer])[:, None, :], N_ADA, axis=-1)
        csh1, csc1, cg1, csh2, csc2, cg2 = jnp.split(silu_cc @ ada_w[layer] + ada_b[layer], N_ADA, axis=-1)

        h = rms_norm(x, norm1_g[layer]) * (1 + sc1) + sh1
        if layer % 2 == 0:
            hc = rms_norm(xc, norm1_g[layer]) * (1 + csc1) + csh1
            mix, mix_c = attn_mixer(h, hc, attn_w_in[i], attn_w_out[i], qnorm_a[i], knorm_a[i], qnorm_b[i], knorm_b[i], sink_b[i], cos, sin, ctx_needed)
        else:
            mix = short_conv_mixer(h, conv_w_in[i], conv_w[i], conv_w_out[i])
            if ctx_needed:
                hc = rms_norm(xc, norm1_g[layer]) * (1 + csc1) + csh1
                mix_c = short_conv_mixer(hc, conv_w_in[i], conv_w[i], conv_w_out[i])
        x = x + g1 * mix
        if ctx_needed:
            xc = xc + cg1 * mix_c

        if layer % 2 == 0:
            ffn = lambda t: swiglu(t, ffn_w_gate[i], ffn_w_up[i], ffn_w_down[i])
        else:
            ffn = lambda t: moe_swiglu(t, router_w[i], moe_w_gate[i], moe_w_up[i], moe_w_down[i])
        h = rms_norm(x, norm2_g[layer]) * (1 + sc2) + sh2
        x = x + g2 * ffn(h)
        if ctx_needed:
            hc = rms_norm(xc, norm2_g[layer]) * (1 + csc2) + csh2
            xc = xc + cg2 * ffn(hc)
    return x


def setup_inputs(seed=0):
    out = dict(first_inputs(seed))
    for name, value in second_inputs(seed + 1).items():
        if name != "x":
            out[name + "_2"] = value
    return out


def reference(
    x, ff1_norm_pre, ff1_w_gate, ff1_w_up, ff1_w_down, ff1_norm_post, mix_norm_pre, w_in,
    conv_w, conv_b, dt_bias, a_log, d_skip, ssd_norm, pool_w, pool_scale, w_out, mix_norm_post,
    ff2_norm_pre, ff2_w_gate, ff2_w_up, ff2_w_down, ff2_norm_post, c_2, ctx_2, c_ctx_2, ada_w_2,
    ada_b_2, norm1_g_2, norm2_g_2, attn_w_in_2, attn_w_out_2, qnorm_a_2, knorm_a_2, qnorm_b_2,
    knorm_b_2, sink_b_2, ffn_w_gate_2, ffn_w_up_2, ffn_w_down_2, conv_w_in_2, conv_w_2,
    conv_w_out_2, router_w_2, moe_w_gate_2, moe_w_up_2, moe_w_down_2,
):
    x = first_block(
        x, ff1_norm_pre, ff1_w_gate, ff1_w_up, ff1_w_down, ff1_norm_post, mix_norm_pre, w_in,
        conv_w, conv_b, dt_bias, a_log, d_skip, ssd_norm, pool_w, pool_scale, w_out,
        mix_norm_post, ff2_norm_pre, ff2_w_gate, ff2_w_up, ff2_w_down, ff2_norm_post,
    )
    return second_block(
        x, c_2, ctx_2, c_ctx_2, ada_w_2, ada_b_2, norm1_g_2, norm2_g_2, attn_w_in_2,
        attn_w_out_2, qnorm_a_2, knorm_a_2, qnorm_b_2, knorm_b_2, sink_b_2, ffn_w_gate_2,
        ffn_w_up_2, ffn_w_down_2, conv_w_in_2, conv_w_2, conv_w_out_2, router_w_2, moe_w_gate_2,
        moe_w_up_2, moe_w_down_2,
    )


_drawn_inputs = setup_inputs


def setup_inputs(seed=0):
    import zlib

    import numpy as np

    out = dict(_drawn_inputs(seed))
    spreads = {}
    factors = {'conv_b': 4.274,
     'ctx_2': 6.201,
     'ada_b_2': 4.182,
     'norm1_g_2': 3.318,
     'norm2_g_2': 3.616,
     'qnorm_a_2': 8.0,
     'knorm_a_2': 8.0,
     'qnorm_b_2': 8.0,
     'knorm_b_2': 8.0,
     'sink_b_2': 8.0}
    for name, (base, spread) in spreads.items():
        noise = np.random.default_rng([zlib.crc32(name.encode()), seed]).standard_normal(out[name].shape)
        drawn = base * np.exp(spread * noise) if base else spread * noise
        out[name] = jnp.asarray(drawn.astype(out[name].dtype))
    for name, factor in factors.items():
        out[name] = (out[name] * factor).astype(out[name].dtype)
    return out
```

```python
from contextlib import ExitStack, contextmanager

import numpy as np

import concourse.bass as bass
from concourse import mybir

F32 = mybir.dt.float32
F32R = mybir.dt.float32r
ACT = mybir.ActivationFunctionType
ALU = mybir.AluOpType
AX = mybir.AxisListType.X

P = 128
S = 256
NT = S // P
D = 1024
KD = D // P
DEPTH = 2
F1 = 2816
FE = 3584
NE = 8
FC = 256
FB = FC // P
N1 = F1 // FC
NX = FE // FC
NM = NE * NX
GC = 512
PIECE = 2048
EPS = 1e-6
NEG = -1e30

SSD_IN, HEADS, HP = 512, 8, 64
OFF_XBC, OFF_DT, OFF_U, OFF_Q, OFF_K, OFF_V = 512, 1536, 1544, 1800, 2056, 2312
PAD = 16
CPAD = 3
ADA = 6 * D
NADA = ADA // GC

PER_TURN = {'act_ff1': {'a_done': 2,
             'a_free': 2,
             'd_free': 2,
             'gu0': 2,
             'raw0': 32,
             'raw1': 32,
             'raw2': 32,
             't_psum': 2},
 'act_ff2': {'a_done': 2,
             'a_free': 2,
             'd_free': 2,
             'gu0': 2,
             'raw0': 32,
             'raw1': 32,
             'raw2': 32,
             't_psum': 2},
 'act_ffn': {'a_done': 2,
             'a_free': 2,
             'd_free': 2,
             'gu0': 2,
             'raw0': 32,
             'raw1': 32,
             'raw2': 32,
             't_psum': 2},
 'act_layer': {'a_done': 30,
               'a_free': 30,
               'act_step': 11,
               'amax': 4,
               'arg': 2,
               'd_free': 22,
               'gated': 1,
               'gu0': 22,
               'mix_par': 144,
               'ms': 7,
               'pT_psum': 4,
               'pool_psum': 1,
               'qk_psum': 1,
               'raw0': 480,
               'raw1': 480,
               'raw2': 352,
               'res_ready': 3,
               'scale': 4,
               't_psum': 22,
               'taps_bc': 1,
               'taps_xs': 1,
               'xt_psum': 8,
               'y_done': 22},
 'act_moe': {'a_done': 2,
             'a_free': 2,
             'd_free': 2,
             'gu0': 2,
             'raw0': 32,
             'raw1': 32,
             'raw2': 32,
             't_psum': 2},
 'dve_ada0': {'ada_bias0': 16, 'ada_bias1': 16, 'ada_used1': 2},
 'dve_ada1': {'ada_bias0': 16, 'ada_bias1': 16, 'ada_used1': 2},
 'dve_ff1': {'hi': 6, 'ht_hi': 2, 'sg0': 2, 'sg1': 2},
 'dve_ff2': {'hi': 6, 'ht_hi': 2, 'sg0': 2, 'sg1': 2},
 'dve_ffn': {'hi': 6, 'ht_hi': 2, 'sg0': 2, 'sg1': 2},
 'dve_layer': {'a_done': 30,
               'acs_psum': 2,
               'bc_out': 1,
               'cb_psum': 1,
               'decay': 2,
               'dt_psum': 1,
               'dve_step': 34,
               'gain': 80,
               'gain_one': 1,
               'gain_row': 48,
               'hi': 82,
               'ht_hi': 22,
               'kv_out': 1,
               'mix_par': 144,
               'pT_psum': 4,
               'pool_out': 1,
               'probs': 4,
               'pv_psum': 4,
               'root': 7,
               'scores': 4,
               'sg0': 22,
               'sg1': 22,
               'soft': 1,
               'ssd_psum': 2,
               'ssq': 7,
               'x_hi': 8,
               'xs_out': 1,
               'xs_psum': 1,
               'y_done': 22},
 'dve_moe': {'hi': 6, 'ht_hi': 2, 'sg0': 2, 'sg1': 2},
 'pe_ada0': {'ada_psum_free': 2, 'raw0': 32, 'raw1': 32},
 'pe_ada1': {'ada_psum_free': 2, 'raw0': 32, 'raw1': 32},
 'pe_ff1': {'h0': 2, 'h1': 2, 'ht': 2, 'split0': 2, 'split1': 2, 'split2': 2},
 'pe_ff2': {'h0': 2, 'h1': 2, 'ht': 2, 'split0': 2, 'split1': 2, 'split2': 2},
 'pe_ffn': {'h0': 2, 'h1': 2, 'ht': 2, 'split0': 2, 'split1': 2, 'split2': 2},
 'pe_layer': {'acs_rows': 1,
              'arg': 2,
              'bc_out': 1,
              'conv_bc': 1,
              'conv_xs': 1,
              'dtc': 1,
              'h0': 22,
              'h1': 22,
              'ht': 22,
              'kv_out': 1,
              'mix_par': 144,
              'pT': 4,
              'pool_out': 1,
              'pooled': 1,
              'probs': 4,
              'qkT': 1,
              'roped': 1,
              'seg': 2,
              'split0': 30,
              'split1': 30,
              'split2': 22,
              'uq_out': 1,
              'x_lo': 8,
              'xdt': 1,
              'xn_ready': 4,
              'xs_out': 1,
              'z_out': 1},
 'pe_moe': {'h0': 2, 'h1': 2, 'ht': 2, 'split0': 2, 'split1': 2, 'split2': 2},
 'pool_ada0': {'ada_bias_free': 2, 'ada_row': 2, 'ada_stored0': 16, 'ada_stored1': 16},
 'pool_ada1': {'ada_bias_free': 2, 'ada_row': 2, 'ada_stored0': 16, 'ada_stored1': 16},
 'pool_layer': {'pool_step': 9, 'res_ready': 3, 'uq_out': 1, 'x_lo': 8},
 'sp_ada0': {'ada_used0': 1, 'ada_used1': 1},
 'sp_ada1': {'ada_used0': 1, 'ada_used1': 1},
 'sp_ff1': {'split0': 1, 'split1': 1, 'split2': 1},
 'sp_ff2': {'split0': 1, 'split1': 1, 'split2': 1},
 'sp_ffn': {'split0': 1, 'split1': 1, 'split2': 1},
 'sp_layer': {'split0': 30, 'split1': 30, 'split2': 22},
 'sp_moe': {'split0': 14, 'split1': 14, 'split2': 14},
 'sp_moe0': {'split0': 1, 'split1': 1, 'split2': 1},
 'sp_moec': {'split0': 1, 'split1': 1, 'split2': 1}}
PER_TURN_SEEN = {}


class Seen:

    def __init__(self):
        self.count = {}
        self.loops = []

    def __call__(self, name, events=1):
        self.count[name] = self.count.get(name, 0) + events
        value = self.count[name]
        for turn, label in self.loops:
            per = PER_TURN.get(label, {}).get(name, 0)
            if per:
                value = turn * per + value
        return value

    @contextmanager
    def loop(self, engine, label, turns, start=0):
        before = dict(self.count)
        with engine.Fori(start, start + turns) as i:
            self.loops.append((i - start if start else i, label))
            yield i
            self.loops.pop()
        per = {k: v - before.get(k, 0) for k, v in self.count.items() if v != before.get(k, 0)}
        PER_TURN_SEEN[label] = per
        for k, v in per.items():
            self.count[k] = before.get(k, 0) + v * turns


def build(nc, T, out, mods, stop=None):
    ctx = ExitStack()
    with ctx:
        def sb(name, shape, dt=F32):
            return ctx.enter_context(nc.sbuf_tensor(name, shape, dt))

        sems = {}

        class Sems:
            def __getitem__(self, name):
                if name not in sems:
                    sems[name] = ctx.enter_context(nc.semaphore(name))
                return sems[name]
        sem = Sems()

        raw = sb("raw", [P, 3, PIECE])
        a_hi, a_lo = sb("a_hi", [P, 2, 2, PIECE], F32R), sb("a_lo", [P, 2, 2, PIECE], F32R)
        d_hi, d_lo = sb("d_hi", [P, PIECE], F32R), sb("d_lo", [P, PIECE], F32R)
        x_hi, x_lo = sb("x_hi", [P, KD, S], F32R), sb("x_lo", [P, KD, S], F32R)
        ht_hi, ht_lo = sb("ht_hi", [P, FB, S], F32R), sb("ht_lo", [P, FB, S], F32R)
        res = sb("res", [P, NT, D])
        xn = sb("xn", [P, NT, D])
        mod = sb("mod", [P, KD, S])
        gbc = sb("gbc", [P, D])
        gcol = sb("gcol", [P, 4, KD])
        sg = sb("sg", [P, NT, FC])
        hb = sb("hb", [P, NT, FC])
        st = sb("st", [P, 2, NT])
        ident = sb("ident", [P, P])
        cmask = sb("cmask", [P, 2 * P + P])
        qmask = sb("qmask", [P, 3 * P])
        epsc = sb("epsc", [P, 1])
        small = sb("small", [P, 256])
        ARENA = 9504
        arena = sb("arena", [P, ARENA])
        psum = ctx.enter_context(nc.psum_tensor("psum", [P, 8, 512], F32))
        Y = psum[:, 0:4, :].rearrange("p (t h) n -> p t (h n)", t=NT)
        TB, MB = psum[:, 6, :], psum[:, 7, :]

        def f(ap):
            return ap.bitcast(F32)

        def area(at, *shape):
            n = int(np.prod(shape))
            assert at + n <= ARENA, (at, n)
            ap = arena[:, at:at + n]
            if len(shape) == 2:
                ap = ap.rearrange("p (a b) -> p a b", b=shape[1])
            if len(shape) == 3:
                ap = ap.rearrange("p (a b c) -> p a b c", b=shape[1], c=shape[2])
            return ap

        zs = area(0, NT, SSD_IN)
        xT = area(1024, 8, CPAD + S + 1)
        arg = area(1024, 4, 384)
        cT = mod
        xdt = area(3104, NT, SSD_IN)
        xsd = area(4128, NT, SSD_IN)
        qk = area(5152, NT, 512)
        vv = area(6176, NT, 256)
        qkT = area(6688, 4, S)
        prob = area(7712, 384)
        pT = area(8096, 384)
        dts = area(8480, 4 * S)[0:HEADS]
        uw = [sb(f"uw{i}", [P, 2, PAD + S]) for i in range(2)]
        um, pm = hb, sg
        poolw = sb("poolw", [P, 2, P])
        convw = small[:, 0:32].rearrange("p (j c) -> p j c", c=8)
        convb = small[:, 32:40]
        dskip = small[:, 40:48]
        dtb, alog = small[0:8, 48:49], small[0:8, 49:50]
        dtc = small[:, 52:68].rearrange("p (t h) -> p t h", h=8)
        nacs = small[:, 68:84].rearrange("p (t h) -> p t h", h=8)
        qstat = small[:, 84:108].rearrange("p (c h t) -> p c h t", c=3, t=NT)
        rope = sb("rope", [P, NT, 16])
        rcnt = sb("rcnt", [P, 2, S])

        cs = sb("cs", [P, KD, 2])
        qq = area(0, NT, 1024)
        kk = area(2048, 4, 256)
        vk = area(3072, 4, 256)
        qT = area(4096, 8, S)
        kT = area(6144, 2, 512)
        prob2 = area(7168, 2, 512)
        pT2 = area(8192, 2, 512)
        ctxr = area(4096, NT, D)
        band = hb
        rope2 = sg[:, 0, 0:128].rearrange("p (t n) -> p t n", t=NT)
        qkg = sg[:, 1, :].rearrange("p (i n) -> p i n", n=64)
        rms = small[:, 160:208]
        nsink = small[:, 148:156]
        sm2 = sb("sm2", [P, 4, 32])
        cg = area(0, 4, S)
        zT = area(1024, 4, S + 2)
        acc = area(2056, 4, S)
        convw2 = small[:, 210:234].rearrange("p (j c) -> p j c", c=8)
        lg = area(0, 8, NT, NE)
        gexp = area(256, NT, NM)
        CONV_UNITS = [1024, 2048, 0, 1536, 2560, 512]

        block = ctx.enter_context(nc.Block())

        def colsof(row):
            return row.rearrange("(k p) -> p k", p=P)

        def kview(w):
            return w.rearrange("(k p) n -> p k n", p=P)

        IN_UNITS = [(OFF_DT, 8), (1024, 512), (512, 512), (OFF_U, 512), (OFF_K, 512), (0, 512)]

        @block.sync
        def _(sp):
            seen = Seen()

            def piece(j, src, dst, first):
                if not first:
                    sp.wait_ge(sem[f"split{j}"], seen(f"split{j}"))
                    sp.sem_inc(sem["sp_past_wait"], 1)
                sp.dma_start(dst, src).then_inc(sem[f"raw{j}"], 16)

            def plain(w, c0, n, first=False):
                v = kview(w)
                for j in range(2):
                    dst = raw[:, j, 0:4 * n].rearrange("p (k n) -> p k n", n=n)
                    piece(j, v[:, 4 * j:4 * j + 4, bass.ds(c0, n)], dst, first)

            def gate_up(wg, wu, c0, first=False):
                for j, w in enumerate((wg, wu)):
                    piece(j, kview(w)[:, :, bass.ds(c0, FC)],
                          raw[:, j, :].rearrange("p (k n) -> p k n", n=FC), first)

            def down(wd, c0, first=False):
                piece(2, wd[bass.ds(c0, FC), :].rearrange("(b p) n -> p b n", p=P),
                      raw[:, 2, :].rearrange("p (b n) -> p b n", n=D), first)

            def ffn(label, wg, wu, wd, first, after):
                gate_up(wg, wu, 0, first)
                gate_up(wg, wu, FC)
                down(wd, 0, first)
                with seen.loop(sp, label, N1 - 2) as i:
                    gate_up(wg, wu, i * FC + 2 * FC)
                    down(wd, i * FC + FC)
                if after:
                    after()
                down(wd, (N1 - 1) * FC)

            for l in range(DEPTH):
                with seen.loop(sp, f"sp_ada{l}", NADA) as i:
                    for j in range(2):
                        sp.wait_ge(sem[f"ada_used{j}"], seen(f"ada_used{j}"))
                        sp.sem_inc(sem["sp_past_wait"], 1)
                        sp.dma_start(raw[:, j, :].rearrange("p (k n) -> p k n", n=GC),
                                     kview(T["ada_w_2"][l])[:, 4 * j:4 * j + 4, bass.ds(i * GC, GC)]
                                     ).then_inc(sem[f"raw{j}"], 16)
            for j in range(2):
                sp.wait_ge(sem[f"ada_used{j}"], seen(f"ada_used{j}"))

            def layer(l):
                W = {k: T[k][l] for k in ("ff1_w_gate", "ff1_w_up", "ff1_w_down", "w_in", "w_out",
                                          "ff2_w_gate", "ff2_w_up", "ff2_w_down")}
                ffn("sp_ff1", W["ff1_w_gate"], W["ff1_w_up"], W["ff1_w_down"], False,
                    lambda: plain(W["w_in"], *IN_UNITS[0]))
                for u in IN_UNITS[1:]:
                    plain(W["w_in"], *u)
                plain(W["w_out"], 0, GC)
                plain(W["w_out"], GC, GC)
                ffn("sp_ff2", W["ff2_w_gate"], W["ff2_w_up"], W["ff2_w_down"], False, None)

            with seen.loop(sp, "sp_layer", DEPTH) as l:
                layer(l)
            wi = T["attn_w_in_2"][0]
            if stop == "first":
                plain(wi, 512, 512)
                sp.wait_ge(sem["final"], 1)
                for t in range(NT):
                    sp.dma_start(out[0, t * P:(t + 1) * P, :], res[:, t, :]).then_inc(sem["stored"], 16)
                sp.wait_ge(sem["stored"], 32)
                return
            plain(wi, 512, 256)
            plain(wi, 1280, 256)
            for c in range(3):
                plain(wi, c * GC, GC)
            for c in range(2):
                plain(T["attn_w_out_2"][0], c * GC, GC)
            ffn("sp_ffn", T["ffn_w_gate_2"][0], T["ffn_w_up_2"][0], T["ffn_w_down_2"][0], False,
                lambda: plain(T["conv_w_in_2"][0], CONV_UNITS[0], GC))
            for c0 in CONV_UNITS[1:]:
                plain(T["conv_w_in_2"][0], c0, GC)
            for c in range(2):
                plain(T["conv_w_out_2"][0], c * GC, GC)
            plain(T["router_w_2"][0], 0, NE)
            mg, mu = T["moe_w_gate_2"][0], T["moe_w_up_2"][0]
            md = T["moe_w_down_2"][0].rearrange("e f d -> (e f) d")
            gate_up(mg[0], mu[0], 0)
            with seen.loop(sp, "sp_moe0", NX - 1) as c:
                gate_up(mg[0], mu[0], c * FC + FC)
                down(md, c * FC)
            with seen.loop(sp, "sp_moe", NE - 1) as e:
                gate_up(mg[e + 1], mu[e + 1], 0)
                down(md, e * FE + (NX - 1) * FC)
                with seen.loop(sp, "sp_moec", NX - 1) as c:
                    gate_up(mg[e + 1], mu[e + 1], c * FC + FC)
                    down(md, e * FE + (FE + c * FC))
            down(md, (NM - 1) * FC)
            sp.wait_ge(sem["final"], 1)
            for t in range(NT):
                sp.dma_start(out[0, t * P:(t + 1) * P, :], res[:, t, :]).then_inc(sem["stored"], 16)
            sp.wait_ge(sem["stored"], 32)

        @block.gpsimd
        def _(pool):
            seen = Seen()
            seen.count["ada_row"] = 2
            M = mods

            def bc(row, n=P):
                return row.unsqueeze(0).broadcast_to([n, row.shape[0]])

            def load(dst, src, name="consts"):
                pool.dma_start(dst, src, allow_slow_non_contiguous=True).then_inc(sem[name], 16)

            nc.gpsimd.memset(uw[0][:], 0.0).then_inc(sem["pool_zero"], 1)
            nc.gpsimd.memset(uw[1][:], 0.0).then_inc(sem["pool_zero"], 1)
            nc.gpsimd.memset(poolw[:], 0.0).then_inc(sem["pool_zero"], 1)
            nc.gpsimd.memset(gcol[:], 0.0).then_inc(sem["pool_zero"], 1)
            nc.gpsimd.memset(epsc[:], EPS).then_inc(sem["pool_zero"], 1)
            CONSTS = [(ident[:], T["c_ident"]), (cmask[:, 0:S], T["c_cmask"]), (qmask[:], T["c_qmask"]),
                      (rope[:], T["c_rope"]), (rcnt[:], T["c_rcnt"]),
                      (res[:], T["x"][0].rearrange("(t p) n -> p t n", p=P)),
                      (small[:, 128:136], colsof(T["c_ctx_2"])), (small[:, 136:144], colsof(T["c_2"][0]))]
            for dst, src in CONSTS:
                load(dst, src)
            pool.wait_ge(sem["consts"], 16 * len(CONSTS))
            pool.wait_ge(sem["pool_zero"], 5)
            pool.sem_inc(sem["consts_in"], 1)

            ab = arena[0:2, 0:2 * GC].rearrange("p (a n) -> p a n", n=GC)
            ao = arena[0:2, 2 * GC:4 * GC].rearrange("p (a n) -> p a n", n=GC)
            for l in range(DEPTH):
                with seen.loop(pool, f"pool_ada{l}", NADA // 2) as i:
                    for q in range(2):
                        pool.wait_ge(sem["ada_row"], seen("ada_bias_free"))
                        pool.sem_inc(sem["pool_past_wait"], 1)
                        pool.dma_start(ab[:, q, :], T["ada_b_2"][l][bass.ds(i * 2 * GC + q * GC, GC)].unsqueeze(0)
                                       .broadcast_to([2, GC])).then_inc(sem[f"ada_bias{q}"], 16)
                    for q in range(2):
                        pool.wait_ge(sem["ada_row"], seen("ada_row"))
                        pool.sem_inc(sem["pool_past_wait"], 1)
                        pool.dma_start(M[l, :, bass.ds(i * 2 * GC + q * GC, GC)], ao[:, q, :]
                                       ).then_inc(sem[f"ada_stored{q}"], 16)
                    for q in range(2):
                        pool.wait_ge(sem[f"ada_stored{q}"], seen(f"ada_stored{q}", 16))

            def gains_in(first=False):
                pool.wait_ge(sem["x_lo"], seen("x_lo", 2))
                pool.sem_inc(sem["pool_past_wait"], 1)

            def columns(cols):
                gains_in()
                for n, (i, src) in enumerate(cols):
                    pool.dma_start(gcol[:, i, 0:src.shape[1]], src, allow_slow_non_contiguous=True).then_inc(sem["gain"], 16)

            def row(src):
                pool.wait_ge(sem["res_ready"], seen("res_ready"))
                pool.sem_inc(sem["pool_past_wait"], 1)
                pool.dma_start(gbc[:], bc(src)).then_inc(sem["gain_row"], 16)

            def pool_branch(l):
                W = T["pool_w"][l]
                pool.wait_ge(sem["uq_out"], seen("uq_out"))
                pool.sem_inc(sem["pool_past_wait"], 1)
                n = PAD + S
                a, b = uw

                def link(ins):
                    ins.then_inc(sem["pool_step"], 1)
                    pool.wait_ge(sem["pool_step"], seen("pool_step"))
                src, dst = a, b
                link(nc.gpsimd.tensor_copy(um[:], a[:, :, PAD:n]))
                for g in range(4):
                    w = 1 << g
                    lo = 2 * w - 1
                    link(nc.gpsimd.tensor_tensor(dst[:, :, lo:n], src[:, :, lo:n], src[:, :, lo - w:n - w], ALU.add))
                    rows = slice(64 * (g % 2), 64 * (g % 2) + 64)
                    c = g // 2
                    link(nc.gpsimd.tensor_tensor(pm[rows, c, :], dst[rows, c, PAD:n],
                                                 rcnt[rows, c, :], ALU.mult))
                    src, dst = dst, src
                nc.gpsimd.tensor_tensor(um[:], pm[:], um[:], ALU.subtract).then_inc(sem["pooled"], 1)

            def mixer_loads(l):
                for dst, src in [(convw, T["conv_w"][l].rearrange("j (c p) -> p j c", p=P)),
                                 (convb, T["conv_b"][l].rearrange("(c p) -> p c", p=P)),
                                 (dskip, bc(T["d_skip"][l])), (dtb, T["dt_bias"][l].unsqueeze(1)),
                                 (alog, T["a_log"][l].unsqueeze(1))] + [
                                 (poolw[64 * (g % 2):64 * (g % 2) + 64, g // 2, 64 * (g % 2):64 * (g % 2) + 64],
                                  T["pool_w"][l, g]) for g in range(4)]:
                    pool.dma_start(dst, src, allow_slow_non_contiguous=True).then_inc(sem["mix_par"], 16)

            with seen.loop(pool, "pool_layer", DEPTH) as l:
                mixer_loads(l)
                columns([(0, colsof(T["ff1_norm_pre"][l]))])
                row(T["ff1_norm_post"][l])
                columns([(0, colsof(T["mix_norm_pre"][l]))])
                row(T["mix_norm_post"][l])
                pool_branch(l)
                gains_in()
                pool.dma_start(gcol[:, 0, 0:4], colsof(T["ssd_norm"][l]), allow_slow_non_contiguous=True).then_inc(sem["gain"], 16)
                pool.dma_start(gcol[:, 0, 4:6], colsof(T["pool_scale"][l]), allow_slow_non_contiguous=True).then_inc(sem["gain"], 16)
                nc.gpsimd.memset(gcol[:, 0, 6:8], 1.0).then_inc(sem["gain_one"], 1)
                columns([(0, colsof(T["ff2_norm_pre"][l]))])
                row(T["ff2_norm_post"][l])
            if stop != "first":
                def part(l, r, i):
                    return M[l, r, i * D:(i + 1) * D]
                G1, G2 = T["norm1_g_2"], T["norm2_g_2"]
                columns([(0, colsof(G1[0])), (1, colsof(part(0, 0, 0))), (2, colsof(part(0, 0, 1)))])
                row(part(0, 1, 2))
                for dst, src in [(ctxr, T["ctx_2"][0].rearrange("(t p) n -> p t n", p=P)), (band[:], T["c_band"]),
                                 (rope2, T["c_rope2"]), (nsink, bc(T["sink_b_2"][0])),
                                 (convw2, T["conv_w_2"][0].rearrange("j (c p) -> p j c", p=P))] + [
                                 (qkg[:, i, :], bc(T[n][0])) for i, n in enumerate(
                                     ("qnorm_a_2", "qnorm_b_2", "knorm_a_2", "knorm_b_2"))]:
                    pool.dma_start(dst, src, allow_slow_non_contiguous=True).then_inc(sem["att_in"], 16)
                columns([(0, colsof(G1[0])), (1, colsof(part(0, 1, 0))), (2, colsof(part(0, 1, 1)))])
                gains_in()
                nc.gpsimd.memset(gcol[:, 1:3, :], 0.0).then_inc(sem["pool_zero"], 1)
                nc.gpsimd.memset(gcol[:, 0, :], 1.0).then_inc(sem["gain_one"], 1)
                for l, i, g in ((0, 3, G2), (1, 0, G1), (1, 3, G2)):
                    columns([(0, colsof(g[l])), (1, colsof(part(l, 1, i))), (2, colsof(part(l, 1, i + 1)))])
                    row(part(l, 1, i + 2))
                    if (l, i) == (1, 0):
                        seen("x_lo", 2)

        @block.tensor
        def _(pe):
            seen = Seen()
            seen.count.update({"split0": 1, "split1": 1, "split2": 1, "x_lo": 2})
            pe.sem_inc(sem["a_done"], 2)
            pe.sem_inc(sem["d_done"], 1)
            pe.sem_inc(sem["ada_used0"], 1)
            pe.sem_inc(sem["ada_used1"], 1)
            par = [0]

            def mm3(o, xh, xl, wh, wl, start, stop_):
                pe.matmul(o, xh, wh, start=start, stop=False, skip_group_check=True)
                pe.matmul(o, xh, wl, start=False, stop=False, skip_group_check=True)
                return pe.matmul(o, xl, wh, start=False, stop=stop_, skip_group_check=True)

            def split_in():
                for j in range(2):
                    pe.wait_ge(sem[f"split{j}"], seen(f"split{j}"))

            def wview(n):
                b = par[0]
                return [w[:, b, :, 0:4 * n].rearrange("p j (k n) -> p j k n", n=n) for w in (a_hi, a_lo)]

            def plain_tok(outs, n, c0=0, w=None, last=True):
                w = w or n
                wh, wl = wview(n)
                for t in range(NT):
                    for k in range(KD):
                        ins = mm3(outs[t], x_hi[:, k, t * P:(t + 1) * P], x_lo[:, k, t * P:(t + 1) * P],
                                  wh[:, k // 4, k % 4, c0:c0 + w], wl[:, k // 4, k % 4, c0:c0 + w],
                                  k == 0, k == KD - 1)
                if last:
                    ins.then_inc(sem["a_done"], 1)
                    par[0] ^= 1

            def plain_tr(outs, n, last=True):
                wh, wl = wview(n)
                m = min(P, n)
                for c, o in enumerate(outs):
                    for k in range(KD):
                        a, b = (w[:, k // 4, k % 4, c * P:c * P + m] for w in (wh, wl))
                        pe.matmul(o, a, x_hi[:, k, :], start=k == 0, stop=False, skip_group_check=True)
                        pe.matmul(o, b, x_hi[:, k, :], start=False, stop=False, skip_group_check=True)
                        ins = pe.matmul(o, a, x_lo[:, k, :], start=False, stop=k == KD - 1, skip_group_check=True)
                if last:
                    ins.then_inc(sem["a_done"], 1)
                    par[0] ^= 1

            def halves(bank):
                return [psum[:, b, h * S:(h + 1) * S] for b in bank for h in range(2)]

            def gate_up():
                split_in()
                b = par[0]
                for t in range(NT):
                    for k in range(KD):
                        wh, wl = (w[:, b, :, k * FC:(k + 1) * FC] for w in (a_hi, a_lo))
                        ins = mm3(psum[:, 4 + t, :].rearrange("p (a n) -> p a n", n=FC),
                                  x_hi[:, k, t * P:(t + 1) * P], x_lo[:, k, t * P:(t + 1) * P],
                                  wh, wl, k == 0, k == KD - 1)
                    ins.then_inc(sem["a_done"] if t else sem["gu0"], 1)
                par[0] ^= 1

            def down(first, last):
                pe.wait_ge(sem["split2"], seen("split2"))
                pe.wait_ge(sem["ht"], seen("ht"))
                for t in range(NT):
                    for h in range(2):
                        for b in range(FB):
                            wh, wl = (w[:, b * D + h * 512:b * D + h * 512 + 512] for w in (d_hi, d_lo))
                            ins = mm3(psum[:, 2 * t + h, :], ht_hi[:, b, t * P:(t + 1) * P],
                                      ht_lo[:, b, t * P:(t + 1) * P], wh, wl,
                                      first and b == 0, last and b == FB - 1)
                ins.then_inc(sem["d_done"], 1)

            def turn_hidden():
                for t in range(NT):
                    pe.wait_ge(sem[f"h{t}"], seen(f"h{t}"))
                    for b in range(FB):
                        ins = pe.transpose(TB[:, b * S + t * P:b * S + (t + 1) * P], hb[:, t, b * P:(b + 1) * P], ident[:])
                ins.then_inc(sem["t_psum"], 1)

            def ffn(label, n):
                gate_up(); turn_hidden()
                gate_up(); down(True, False); turn_hidden()
                with seen.loop(pe, label, (n - 3) // 2):
                    for _ in range(2):
                        gate_up(); down(False, False); turn_hidden()
                for _ in range(1 + (n - 3) % 2):
                    gate_up(); down(False, False); turn_hidden()
                down(False, True)

            def to_x():
                pe.wait_ge(sem["xn_ready"], seen("xn_ready"))
                for k in range(KD):
                    for t in range(NT):
                        ins = pe.transpose(psum[:, k // 2, (k % 2) * S + t * P:(k % 2) * S + (t + 1) * P],
                                           xn[:, t, k * P:(k + 1) * P], ident[:])
                    if k % 4 == 3:
                        ins.then_inc(sem["xt_psum"], 1)
                pe.wait_ge(sem["x_lo"], seen("x_lo", 2))

            def event(name):
                pe.wait_ge(sem[name], seen(name))

            def mixer():
                split_in(); plain_tr([MB[0:8, 0:S]], 8)
                split_in(); plain_tr(halves((4, 5)), GC)
                split_in(); plain_tr(halves((0, 1)), GC)
                split_in(); plain_tr(halves((2,)), GC, last=False)
                plain_tok([psum[:, 3, t * 256:(t + 1) * 256] for t in range(NT)], GC, 256, 256)
                event("bc_out")
                split_in(); plain_tok([psum[:, 4 + t, :] for t in range(NT)], GC)
                event("xs_out")
                split_in(); plain_tok([psum[:, t, :] for t in range(NT)], GC)
                event("acs_rows")
                pe.sem_inc(sem["pe_past_wait"], 1)
                for i in range(2):
                    for t in range(NT):
                        ins = pe.transpose(TB[:, (i * 2 + t) * 8:(i * 2 + t) * 8 + 8],
                                           dts[:, i * S + t * P:i * S + (t + 1) * P], ident[0:8, 0:8])
                ins.then_inc(sem["dt_psum"], 1)
                event("pooled")
                pe.wait_ge(sem["mix_par"], seen("mix_par", 16 * 9))
                for t in range(NT):
                    for c in range(2):
                        ins = pe.matmul(MB[:, t * S + c * P:t * S + (c + 1) * P], um[:, c, t * P:(t + 1) * P],
                                        poolw[:, c, :], start=True, stop=True)
                ins.then_inc(sem["pool_psum"], 1)
                event("conv_bc"); event("dtc"); event("pool_out")
                for g, o in ((0, TB), (1, MB)):
                    pe.matmul(o[:, 0:S], cT[:, 4 + g, 0:P], cT[:, 6 + g, :], start=True, stop=True)
                    ins = pe.matmul(o[:, S:S + P], cT[:, 4 + g, P:S], cT[:, 6 + g, P:S], start=True, stop=True)
                ins.then_inc(sem["cb_psum"], 1)
                event("uq_out")
                for g in range(2):
                    if g:
                        event("arg")
                    for h in range(4):
                        ins = pe.matmul(psum[:, 2 + h // 2, (h % 2) * S:(h % 2) * S + S], ident[0:8, 4 * g + h:4 * g + h + 1].broadcast_to([8, P]),
                                        dts[:, S:2 * S], start=True, stop=True)
                    ins.then_inc(sem["acs_psum"], 1)
                    if g == 0:
                        event("z_out"); event("conv_xs")
                        for t in range(NT):
                            for c in range(4):
                                ins = pe.transpose(psum[:, t, c * P:(c + 1) * P], cT[:, c, t * P:(t + 1) * P], ident[:])
                        ins.then_inc(sem["xs_psum"], 1)
                        event("kv_out"); event("xdt")
                    event("seg")
                    for h in range(4):
                        o = 64 * (4 * g + h)
                        pe.matmul(psum[:, 4, o:o + 64], arg[:, h, 0:P], xdt[:, 0, o:o + 64], start=True, stop=True)
                        pe.matmul(psum[:, 5, o:o + 64], arg[:, h, P:S], xdt[:, 0, o:o + 64], start=True, stop=False)
                        ins = pe.matmul(psum[:, 5, o:o + 64], arg[:, h, S:S + P], xdt[:, 1, o:o + 64], start=False, stop=True)
                    ins.then_inc(sem["ssd_psum"], 1)
                event("roped"); event("arg")
                for a in range(4):
                    for t in range(NT):
                        ins = pe.transpose(psum[:, 2 + a // 2, (a % 2) * S + t * P:(a % 2) * S + (t + 1) * P],
                                           qk[:, t, a * P:(a + 1) * P], ident[:])
                ins.then_inc(sem["qk_psum"], 1)
                event("qkT")
                for h in range(4):
                    r = slice(64 * (h % 2), 64 * (h % 2) + 64)
                    pe.matmul(psum[:, h, 0:P], qkT[r, h // 2, 0:P], qkT[r, 2 + h // 2, 0:P], start=True, stop=True)
                    ins = pe.matmul(psum[:, h, P:3 * P], qkT[r, h // 2, P:S], qkT[r, 2 + h // 2, :], start=True, stop=True)
                    ins.then_inc(sem["scores"], 1)
                for h in range(4):
                    event("probs")
                    for i in range(3):
                        ins = pe.transpose(TB[:, i * P:(i + 1) * P], prob[:, i * P:(i + 1) * P], ident[:])
                    ins.then_inc(sem["pT_psum"], 1)
                    event("pT")
                    v = vv[:, :, h * 64:h * 64 + 64]
                    pe.matmul(MB[:, h * 64:h * 64 + 64], pT[:, 0:P], v[:, 0], start=True, stop=True)
                    pe.matmul(MB[:, 256 + h * 64:320 + h * 64], pT[:, P:2 * P], v[:, 0], start=True, stop=False)
                    ins = pe.matmul(MB[:, 256 + h * 64:320 + h * 64], pT[:, 2 * P:3 * P], v[:, 1], start=False, stop=True)
                    ins.then_inc(sem["pv_psum"], 1)
                to_x()
                for c in range(2):
                    split_in()
                    plain_tok([psum[:, 2 * t + c, :] for t in range(NT)], GC)

            event("silu_c")
            for l in range(DEPTH):
                with seen.loop(pe, f"pe_ada{l}", NADA // 2):
                    for q in range(2):
                        pe.wait_ge(sem["ada_row"], seen("ada_psum_free"))
                        for j in range(2):
                            pe.wait_ge(sem[f"raw{j}"], seen(f"raw{j}", 16))
                            for k in range(4):
                                ins = pe.matmul(psum[0:2, q, :], cs[:, 4 * j + k, :], raw[:, j, k * GC:(k + 1) * GC],
                                                start=4 * j + k == 0, stop=4 * j + k == KD - 1)
                            ins.then_inc(sem[f"ada_used{j}"], 1)

            with seen.loop(pe, "pe_layer", DEPTH):
                to_x(); ffn("pe_ff1", N1)
                to_x(); mixer()
                to_x(); ffn("pe_ff2", N1)
            if stop != "first":
                tok = [[psum[:, b + t, 0:256] for t in range(NT)] for b in (4, 6)]
                to_x()
                for o in tok:
                    split_in(); plain_tok(o, 256)
                to_x()
                event("ctx_out")
                for b in (4, 6, 0):
                    split_in(); plain_tok([psum[:, b + t, :] for t in range(NT)], GC)
                event("roped2")
                for y in range(2):
                    for g in range(4):
                        for t in range(NT):
                            a = 4 * y + g
                            src = qq[:, t, a * P:(a + 1) * P]
                            ins = pe.transpose(psum[:, a // 2, (a % 2) * S + t * P:(a % 2) * S + (t + 1) * P], src, ident[:])
                for y in range(2):
                    for t in range(4):
                        ins = pe.transpose(psum[:, 4 + y, t * P:(t + 1) * P], kk[:, t, y * P:(y + 1) * P], ident[:])
                ins.then_inc(sem["qk2_psum"], 1)
                event("qT"); event("kT")
                TILES = [(y, t, v, g) for y in range(2) for t in range(NT) for v in range(2) for g in range(4)]

                def scores(i):
                    y, t, v, g = TILES[i]
                    r = slice(64 * v, 64 * v + 64)
                    pe.matmul(psum[:, i % 2, :], qT[r, 4 * y + g, t * P:(t + 1) * P], kT[r, y, :],
                              start=True, stop=True).then_inc(sem["scores2"], 1)

                scores(0); scores(1)
                for i, (y, t, v, g) in enumerate(TILES):
                    event("probs2")
                    for j in range(4):
                        ins = pe.transpose(psum[:, 2 + i % 2, j * P:(j + 1) * P], prob2[:, i % 2, j * P:(j + 1) * P], ident[:])
                    ins.then_inc(sem["pT2_psum"], 1)
                    if i + 2 < len(TILES):
                        scores(i + 2)
                    event("pT2")
                    h = 4 * v + g
                    for j in range(4):
                        ins = pe.matmul(psum[:, 4 + 2 * y + t, h * 64:(h + 1) * 64], pT2[:, i % 2, j * P:(j + 1) * P],
                                        vk[:, j, y * P + v * 64:y * P + v * 64 + 64], start=j == 0, stop=j == 3)
                    if i % 16 == 15:
                        ins.then_inc(sem["pv2_psum"], 1)
                to_x()
                for c in range(2):
                    split_in(); plain_tok([psum[:, 2 * t + c, :] for t in range(NT)], GC)
                to_x(); ffn("pe_ffn", N1)
                to_x()
                for c, b in enumerate((4, 2, 0, 6, 4, 2)):
                    if c >= 4:
                        event("conv_free")
                    split_in(); plain_tr(halves((b, b + 1)), GC)
                pe.wait_ge(sem["x_lo"], seen("x_lo", 2))
                for c in range(2):
                    split_in(); plain_tok([psum[:, 2 * t + c, :] for t in range(NT)], GC)
                to_x()
                split_in(); plain_tok([MB[:, t * NE:(t + 1) * NE] for t in range(NT)], NE)
                ffn("pe_moe", NM)

        @block.scalar
        def _(act):
            seen = Seen()
            seen.count.update({"a_done": 2, "raw0": 16 * 2 * NADA, "raw1": 16 * 2 * NADA})
            seen.count["y_done"] = 1
            par = [0]

            def go(*a, **k):
                return nc.scalar.activation(*a, **k)

            def link(ins):
                ins.then_inc(sem["act_step"], 1)
                act.wait_ge(sem["act_step"], seen("act_step"))

            def event(name):
                act.wait_ge(sem[name], seen(name))

            def unit():
                act.wait_ge(sem["a_done"], seen("a_done"))

            def unit_skip():
                seen("a_done")

            def split_a(n=PIECE):
                act.wait_ge(sem["a_done"], seen("a_free"))
                for j in range(2):
                    act.wait_ge(sem[f"raw{j}"], seen(f"raw{j}", 16))
                    go(a_hi[:, par[0], j, 0:n], raw[:, j, 0:n], ACT.Copy).then_inc(sem["hi"], 1)
                par[0] ^= 1

            def split_d():
                act.wait_ge(sem["d_done"], seen("d_free"))
                act.wait_ge(sem["raw2"], seen("raw2", 16))
                go(d_hi[:], raw[:, 2, :], ACT.Copy).then_inc(sem["hi"], 1)

            def hidden_hi():
                event("t_psum")
                go(ht_hi[:].rearrange("p b s -> p (b s)"), TB, ACT.Copy).then_inc(sem["ht_hi"], 1)

            def period(u, ahead):
                if u:
                    hidden_hi()
                if ahead:
                    split_a(ahead)
                event("gu0")
                go(sg[:, 0, :], psum[:, 4, 0:FC], ACT.Silu).then_inc(sem["sg0"], 1)
                if u:
                    split_d()
                unit()
                go(sg[:, 1, :], psum[:, 5, 0:FC], ACT.Silu).then_inc(sem["sg1"], 1)

            def ffn(label, n, nxt):
                period(0, PIECE)
                with seen.loop(act, label, (n - 2) // 2):
                    for _ in range(2):
                        period(1, PIECE)
                if n % 2:
                    period(1, PIECE)
                period(1, nxt)
                hidden_hi()
                split_d()

            def norm_rows(src):
                for t in range(NT):
                    ins = go(xn[:, t, :], src(t), ACT.Square, accum_out=st[:, 0, t:t + 1])
                ins.then_inc(sem["ssq"], 1)
                event("ms")
                go(st[:, 1, :], st[:, 0, :], ACT.Sqrt).then_inc(sem["root"], 1)

            def pre_norm(src=lambda t: res[:, t, :], wait="res_ready"):
                if wait:
                    event(wait)
                norm_rows(src)

            def post_norm(wait):
                wait()
                norm_rows(lambda t: Y[:, t, :])

            def y_done(n=1):
                act.wait_ge(sem["d_done"], seen("y_done", n))

            def to_x():
                event("scale")
                for half in range(2):
                    event("xt_psum")
                    for k in range(4 * half, 4 * half + 4):
                        ins = go(mod[:, k, :], psum[:, k // 2, (k % 2) * S:(k % 2) * S + S], ACT.Identity,
                                 bias=gcol[:, 1, k:k + 1], scale=gcol[:, 3, k:k + 1])
                    link(ins)
                    go(x_hi[:, 4 * half:4 * half + 4, :], mod[:, 4 * half:4 * half + 4, :], ACT.Copy).then_inc(sem["x_hi"], 1)

            def mixer():
                def conv_out(name, c0):
                    event(f"taps_{name}")
                    for c in range(c0, c0 + 4):
                        ins = go(cT[:, c, :], cT[:, c, :], ACT.Silu, bias=convb[:, c:c + 1])
                    ins.then_inc(sem[f"conv_{name}"], 1)

                split_a(4 * GC)
                unit()
                act.wait_ge(sem["mix_par"], seen("mix_par", 16 * 9))
                tmp = dts[:, 2 * S:3 * S]
                link(go(tmp, MB[0:8, 0:S], ACT.Abs, bias=dtb))
                link(go(tmp, tmp, ACT.Exp, scale=-1.0))
                link(go(tmp, tmp, ACT.Ln, bias=1.0))
                go(dts[:, 3 * S:3 * S + 1], alog, ACT.Exp).then_inc(sem["soft"], 1)
                split_a(4 * GC)
                unit()
                go(xT[:, 4:8, CPAD:CPAD + S], psum[:, 4:6, :].rearrange("p b (h s) -> p (b h) s", s=S), ACT.Copy).then_inc(sem["bc_out"], 1)
                split_a(4 * GC)
                unit()
                go(xT[:, 0:4, CPAD:CPAD + S], psum[:, 0:2, :].rearrange("p b (h s) -> p (b h) s", s=S), ACT.Copy).then_inc(sem["xs_out"], 1)
                split_a(4 * GC)
                unit()
                go(qk[:, :, 0:256], psum[:, 3, :].rearrange("p (t n) -> p t n", t=NT), ACT.Copy)
                go(uw[0][:, :, PAD:PAD + S], psum[:, 2, :].rearrange("p (c s) -> p c s", s=S), ACT.Copy).then_inc(sem["uq_out"], 1)
                conv_out("bc", 4)
                split_a(4 * GC)
                unit()
                kv = psum[:, 4:6, :]
                go(vv, kv[:, :, 256:512], ACT.Copy)
                go(qk[:, :, 256:512], kv[:, :, 0:256], ACT.Copy).then_inc(sem["kv_out"], 1)
                conv_out("xs", 0)
                split_a(4 * GC)
                unit()
                go(zs, psum[:, 0:2, :], ACT.Silu).then_inc(sem["z_out"], 1)
                split_a(4 * GC)
                event("pool_psum")
                go(xn[:, :, 512:768], MB.rearrange("p (t n) -> p t n", t=NT), ACT.Copy).then_inc(sem["pool_out"], 1)
                for g in range(2):
                    event("arg")
                    go(arg, arg, ACT.Exp).then_inc(sem["decay"], 1)
                event("gated")
                for t in range(NT):
                    ins = go(xsd[:, t, :], xdt[:, t, :], ACT.Square, accum_out=st[:, 0, t:t + 1])
                ins.then_inc(sem["ssq"], 1)
                event("ms")
                go(st[:, 1, :], st[:, 0, :], ACT.Sqrt).then_inc(sem["root"], 1)
                event("qk_psum")
                go(qkT, psum[:, 2:4, :].rearrange("p b (h s) -> p (b h) s", s=S), ACT.Copy).then_inc(sem["qkT"], 1)
                for h in range(4):
                    event("amax")
                    for t in range(NT):
                        ap = prob[:, 0:P] if t == 0 else prob[:, P:3 * P]
                        ins = go(ap, ap, ACT.Exp, bias=qstat[:, 0, h, t:t + 1], accum_out=qstat[:, 1, h, t:t + 1])
                    ins.then_inc(sem["probs"], 1)
                    event("pT_psum")
                    go(pT, TB[:, 0:384], ACT.Copy).then_inc(sem["pT"], 1)
                to_x()

            event("consts_in")
            go(cs[:].rearrange("p k r -> p r k"), small[:, 128:144].rearrange("p (r k) -> p r k", k=KD), ACT.Silu).then_inc(sem["silu_c"], 1)
            split_a()
            with seen.loop(act, "act_layer", DEPTH):
                pre_norm(); to_x(); ffn("act_ff1", N1, 4 * 8)
                post_norm(lambda: y_done(N1))
                pre_norm(); to_x(); mixer()
                unit()
                split_a()
                unit()
                post_norm(lambda: None)
                pre_norm(); to_x(); ffn("act_ff2", N1, None)
                split_a()
                post_norm(lambda: y_done(N1))
            if stop != "first":
                act.wait_ge(sem["att_in"], seen("att_in", 16 * 9))
                pre_norm(lambda t: ctxr[:, t, :], None)
                to_x()
                split_a()
                for y in range(2):
                    unit()
                    go(kk[:, 0:2, y * P:(y + 1) * P], psum[:, 4 + 2 * y:6 + 2 * y, 0:P], ACT.Copy)
                    ins = go(vk[:, 0:2, y * P:(y + 1) * P], psum[:, 4 + 2 * y:6 + 2 * y, P:2 * P], ACT.Copy)
                    split_a()
                go(cs[:, 0, 0:1], epsc[:], ACT.Copy).then_inc(sem["ctx_out"], 1)
                pre_norm(); to_x()
                unit()
                q5 = qq.rearrange("p t (y g v d) -> p t y v g d", y=2, v=2, d=64)

                def heads(ap):
                    return ap.rearrange("p (g d) -> p g d", d=64)
                for t in range(NT):
                    for v in range(2):
                        go(q5[:, t, 0, v], heads(psum[:, 4 + t, v * 256:(v + 1) * 256]), ACT.Copy)
                split_a()
                unit()
                go(kk[:, 2:4, 0:P], psum[:, 6:8, 0:P], ACT.Copy)
                go(vk[:, 2:4, 0:P], psum[:, 6:8, P:2 * P], ACT.Copy)
                for t in range(NT):
                    go(q5[:, t, 1, 0], heads(psum[:, 6 + t, 256:512]), ACT.Copy)
                split_a()
                unit()
                for t in range(NT):
                    go(q5[:, t, 1, 1], heads(psum[:, t, 0:256]), ACT.Copy)
                go(kk[:, 2:4, P:2 * P], psum[:, 0:2, 256:384], ACT.Copy)
                link(go(vk[:, 2:4, P:2 * P], psum[:, 0:2, 384:512], ACT.Copy))
                go(mod[:].rearrange("p k s -> p (k s)"), qq.rearrange("p t n -> p (t n)"), ACT.Square)
                go(xn[:, 0, :], kk.rearrange("p t n -> p (t n)"), ACT.Square).then_inc(sem["squares"], 1)
                event("head_ms")
                go(rms, rms, ACT.Sqrt).then_inc(sem["head_root"], 1)
                split_a()
                event("qk2_psum")
                go(qT, psum[:, 0:4, :].rearrange("p b (h s) -> p (b h) s", s=S), ACT.Copy).then_inc(sem["qT"], 1)
                tiles = [y * 16 + t * 8 + v * 4 + g for y in range(2) for t in range(NT) for v in range(2) for g in range(4)]

                def exps(i):
                    event("amax2")
                    n = tiles[i]
                    go(prob2[:, i % 2, :], psum[:, i % 2, :], ACT.Exp, scale=64.0 ** -0.5, bias=sm2[:, 1, n:n + 1],
                       accum_out=sm2[:, 2, n:n + 1]).then_inc(sem["probs2"], 1)

                exps(0)
                for i in range(32):
                    if i < 31:
                        exps(i + 1)
                    event("pT2_psum")
                    go(pT2[:, i % 2, :], psum[:, 2 + i % 2, :], ACT.Copy).then_inc(sem["pT2"], 1)
                event("sink_arg")
                go(sm2[:, 0, 16:32], sm2[:, 0, 16:32], ACT.Exp).then_inc(sem["sink_exp"], 1)
                to_x()
                unit()
                split_a()
                unit()
                pre_norm(); to_x(); ffn("act_ffn", N1, PIECE)
                pre_norm(); to_x()
                for half in range(2):
                    split_a(); unit()
                    go(cg, psum[:, 4 + 2 * half:6 + 2 * half, :].rearrange("p b (h s) -> p (b h) s", s=S), ACT.Copy).then_inc(sem["cg"], 1)
                    split_a(); unit()
                    split_a(); unit()
                    if half == 0:
                        event("cg_used")
                event("mixed_conv")
                for half in range(2):
                    s4 = slice(4 * half, 4 * half + 4)
                    go(x_hi[:, s4, :], mod[:, s4, :], ACT.Copy).then_inc(sem["x_hi"], 1)
                split_a()
                unit()
                split_a(4 * NE)
                unit()
                pre_norm(); to_x()
                split_a()
                unit()
                event("top2")
                go(lg[:, 6, :, 0:1], lg[:, 6, :, 0:1], ACT.Exp).then_inc(sem["top2_exp"], 1)
                ffn("act_moe", NM, None)

        @block.vector
        def _(dve):
            seen = Seen()
            seen.count.update({"a_done": 2, "y_done": 1, "ada_used1": 1})
            par = [0]
            dve.sem_inc(sem["ada_row"], 2)
            dve.sem_inc(sem["x_lo"], 2)
            for j in range(3):
                dve.sem_inc(sem[f"split{j}"], 1)
            V = nc.vector

            def link(ins):
                ins.then_inc(sem["dve_step"], 1)
                dve.wait_ge(sem["dve_step"], seen("dve_step"))

            def event(name, n=1):
                dve.wait_ge(sem[name], seen(name, n))

            def unit():
                dve.wait_ge(sem["a_done"], seen("a_done"))

            def unit_skip(n=1):
                seen("a_done", n)

            def split_a(n=PIECE):
                for j in range(2):
                    event("hi")
                    V.tensor_tensor(a_lo[:, par[0], j, 0:n], raw[:, j, 0:n], f(a_hi[:, par[0], j, 0:n]),
                                    ALU.subtract).then_inc(sem[f"split{j}"], 1)
                par[0] ^= 1

            def split_d():
                event("hi")
                V.tensor_tensor(d_lo[:], raw[:, 2, :], f(d_hi[:]), ALU.subtract).then_inc(sem["split2"], 1)

            def hidden_lo():
                event("ht_hi")
                V.tensor_tensor(ht_lo[:].rearrange("p b s -> p (b s)"), TB, f(ht_hi[:]).rearrange("p b s -> p (b s)"),
                                ALU.subtract).then_inc(sem["ht"], 1)

            def hidden(t, scale):
                event(f"sg{t}")
                up = psum[:, 4 + t, FC:2 * FC]
                if scale is None:
                    V.tensor_tensor(hb[:, t, :], sg[:, t, :], up, ALU.mult).then_inc(sem[f"h{t}"], 1)
                else:
                    V.scalar_tensor_tensor(hb[:, t, :], sg[:, t, :], scale(t), up, ALU.mult, ALU.mult).then_inc(sem[f"h{t}"], 1)

            def period(u, ahead, scale=None):
                if u:
                    hidden_lo()
                if ahead:
                    split_a(ahead)
                hidden(0, scale)
                if u:
                    split_d()
                hidden(1, scale)

            def ffn(label, n, nxt, scale=None):
                s = scale or (lambda u: None)
                period(0, PIECE, s(0))
                with seen.loop(dve, label, (n - 2) // 2) as i:
                    for q in range(2):
                        period(1, PIECE, s(i * 2 + (1 + q)))
                if n % 2:
                    period(1, PIECE, s(n - 2))
                period(1, nxt, s(n - 1))
                hidden_lo()
                split_d()
                unit_skip(n)

            def roots(width):
                event("ssq")
                V.tensor_scalar(st[:, 0, :], st[:, 0, :], 1.0 / width, EPS, ALU.mult, ALU.add).then_inc(sem["ms"], 1)
                event("root")
                link(V.reciprocal(st[:, 1, :], st[:, 1, :]))

            def pre_norm(src=lambda t: res[:, t, :]):
                roots(D)
                for t in range(NT):
                    ins = V.tensor_scalar(xn[:, t, :], src(t), st[:, 1, t:t + 1], None, ALU.mult)
                ins.then_inc(sem["xn_ready"], 1)

            def to_x(n_gain=1, extra=None):
                event("gain", 16 * n_gain)
                if extra:
                    event(extra)
                V.scalar_tensor_tensor(gcol[:, 3, :], gcol[:, 2, :], 1.0, gcol[:, 0, :], ALU.add, ALU.mult).then_inc(sem["scale"], 1)
                for half in range(2):
                    event("x_hi")
                    s = slice(4 * half, 4 * half + 4)
                    V.tensor_tensor(x_lo[:, s, :], mod[:, s, :], f(x_hi[:, s, :]), ALU.subtract).then_inc(sem["x_lo"], 1)

            def y_done(n=1):
                dve.wait_ge(sem["d_done"], seen("y_done", n))

            def post_norm(wait, factor, normed=True):
                wait()
                if normed:
                    roots(D)
                    if factor != 1.0:
                        link(V.tensor_scalar(st[:, 1, :], st[:, 1, :], factor, None, ALU.mult))
                event("gain_row", 16)
                for t in range(NT):
                    if normed:
                        ins = V.scalar_tensor_tensor(xn[:, t, :], Y[:, t, :], st[:, 1, t:t + 1], gbc[:], ALU.mult, ALU.mult)
                    else:
                        ins = V.tensor_tensor(xn[:, t, :], Y[:, t, :], gbc[:], ALU.mult)
                link(ins)
                for t in range(NT):
                    ins = V.tensor_tensor(res[:, t, :], res[:, t, :], xn[:, t, :], ALU.add)
                ins.then_inc(sem["res_ready"], 1)

            def mixer():
                split_a(4 * GC)
                event("mix_par", 16 * 9)
                event("soft")
                a, b = dts[:, 0:S], dts[:, S:2 * S]
                link(V.tensor_scalar(a, MB[0:8, 0:S], dtb, 0.0, ALU.add, ALU.max))
                link(V.tensor_tensor(a, a, dts[:, 2 * S:3 * S], ALU.add))
                link(V.tensor_scalar(dts[:, 2 * S:3 * S], a, dts[:, 3 * S:3 * S + 1], -1.0, ALU.mult, ALU.mult))
                link(V.memset(dts[:, 3 * S:4 * S], 1.0))
                V.tensor_tensor_scan(b, dts[:, 3 * S:4 * S], dts[:, 2 * S:3 * S], 0.0, ALU.mult, ALU.add).then_inc(sem["acs_rows"], 1)
                split_a(4 * GC)
                link(V.memset(xT[:, :, 0:CPAD], 0.0))
                event("bc_out")

                def taps(name, c0):
                    for j in range(4):
                        for c in range(c0, c0 + 4):
                            src = xT[:, c, j:j + S]
                            w = convw[:, j, c:c + 1]
                            if j == 0:
                                ins = V.tensor_scalar(cT[:, c, :], src, w, None, ALU.mult)
                            else:
                                ins = V.scalar_tensor_tensor(cT[:, c, :], src, w, cT[:, c, :], ALU.mult, ALU.add)
                        if j < 3:
                            link(ins)
                    ins.then_inc(sem[f"taps_{name}"], 1)
                taps("bc", 4)
                split_a(4 * GC)
                event("xs_out")
                taps("xs", 0)
                split_a(4 * GC)
                split_a(4 * GC)
                split_a(4 * GC)
                unit_skip(6)
                event("dt_psum")
                TB3 = TB[:, 0:32].rearrange("p (i t h) -> p i t h", i=2, t=NT)
                V.tensor_copy(dtc, TB3[:, 0])
                V.tensor_scalar(nacs, TB3[:, 1], -1.0, None, ALU.mult).then_inc(sem["dtc"], 1)
                split_a(4 * GC)
                event("kv_out")
                x = qk.rearrange("p t (h d) -> p t h d", d=64)
                r = area(7712, 4, NT, 64).rearrange("p i t (h d) -> p i t h d", d=8)
                for i, (part, trig) in enumerate(((0, 0), (1, 1), (1, 0), (0, 1))):
                    tb = rope[:, :, 8 * trig:8 * trig + 8].unsqueeze(2).broadcast_to([P, NT, 8, 8])
                    for t in range(NT):
                        ins = V.tensor_tensor(r[:, i, t], x[:, t, :, 8 * part:8 * part + 8], tb[:, t], ALU.mult)
                link(ins)
                for t in range(NT):
                    V.tensor_tensor(x[:, t, :, 0:8], r[:, 0, t], r[:, 1, t], ALU.subtract)
                    ins = V.tensor_tensor(x[:, t, :, 8:16], r[:, 2, t], r[:, 3, t], ALU.add)
                ins.then_inc(sem["roped"], 1)
                for g in range(2):
                    event("acs_psum")
                    if g:
                        event("ssd_psum")
                    for h in range(4):
                        ps = psum[:, 2 + h // 2, (h % 2) * S:(h % 2) * S + S]
                        V.scalar_tensor_tensor(arg[:, h, 0:S], ps, nacs[:, 0, 4 * g + h:4 * g + h + 1], cmask[:, 0:S], ALU.add, ALU.add)
                        ins = V.scalar_tensor_tensor(arg[:, h, S:S + P], ps[:, P:S], nacs[:, 1, 4 * g + h:4 * g + h + 1],
                                                     cmask[:, 0:P], ALU.add, ALU.add)
                    ins.then_inc(sem["arg"], 1)
                    if g == 0:
                        event("xs_psum")
                        for t in range(NT):
                            xs = psum[:, t, :].rearrange("p (h d) -> p h d", d=HP)
                            for dst, col in ((xdt, dtc[:, t, :]), (xsd, dskip)):
                                ins = V.tensor_tensor(dst[:, t, :].rearrange("p (h d) -> p h d", d=HP), xs,
                                                      col.unsqueeze(2).broadcast_to([P, HEADS, HP]), ALU.mult)
                        ins.then_inc(sem["xdt"], 1)
                        event("cb_psum")
                    event("decay")
                    cb = (TB, MB)[g][:, 0:384].unsqueeze(1).broadcast_to([P, 4, 384])
                    V.tensor_tensor(arg, arg, cb, ALU.mult).then_inc(sem["seg"], 1)
                event("ssd_psum")
                for t in range(NT):
                    ins = V.tensor_tensor(xdt[:, t, :], psum[:, 4 + t, :], xsd[:, t, :], ALU.add)
                link(ins)
                for t in range(NT):
                    ins = V.tensor_tensor(xdt[:, t, :], xdt[:, t, :], zs[:, t, :], ALU.mult)
                ins.then_inc(sem["gated"], 1)
                roots(SSD_IN)
                for t in range(NT):
                    V.tensor_scalar(xn[:, t, 0:SSD_IN], xdt[:, t, :], st[:, 1, t:t + 1], None, ALU.mult)
                scale = 64.0 ** -0.5
                for h in range(4):
                    event("scores")
                    if h:
                        event("pT_psum")
                    link(V.scalar_tensor_tensor(prob, psum[:, h, 0:384], scale, qmask[:], ALU.mult, ALU.add))
                    V.reduce_max(qstat[:, 0, h, 0:1], prob[:, 0:P], AX)
                    link(V.reduce_max(qstat[:, 0, h, 1:2], prob[:, P:3 * P], AX))
                    V.tensor_scalar(qstat[:, 0, h, :], qstat[:, 0, h, :], -1.0, None, ALU.mult).then_inc(sem["amax"], 1)
                event("pT_psum")
                event("probs", 4)
                link(V.reciprocal(qstat[:, 2], qstat[:, 1]))
                event("pv_psum", 4)
                for t in range(NT):
                    ins = V.tensor_tensor(xn[:, t, 768:D].rearrange("p (h d) -> p h d", d=64),
                                          MB[:, t * 256:(t + 1) * 256].rearrange("p (h d) -> p h d", d=64),
                                          qstat[:, 2, :, t:t + 1].broadcast_to([P, 4, 64]), ALU.mult)
                event("pool_out")
                V.tensor_copy(small[:, 120:121], epsc[:]).then_inc(sem["xn_ready"], 1)
                to_x(2, "gain_one")

            event("consts_in")
            for l in range(DEPTH):
                with seen.loop(dve, f"dve_ada{l}", NADA // 2):
                    for q in range(2):
                        event(f"ada_bias{q}", 16)
                        event("ada_used1")
                        V.tensor_tensor(arena[0:2, 2 * GC + q * GC:3 * GC + q * GC], psum[0:2, q, :],
                                        arena[0:2, q * GC:(q + 1) * GC], ALU.add).then_inc(sem["ada_row"], 1)
            V.tensor_copy(small[:, 120:121], epsc[:]).then_inc(sem["res_ready"], 1)
            split_a()
            with seen.loop(dve, "dve_layer", DEPTH):
                pre_norm(); to_x(); ffn("dve_ff1", N1, 4 * 8)
                post_norm(lambda: y_done(N1), 0.5)
                pre_norm(); to_x(); mixer()
                unit_skip()
                split_a()
                unit()
                post_norm(lambda: None, 1.0)
                pre_norm(); to_x(); ffn("dve_ff2", N1, None)
                split_a()
                post_norm(lambda: y_done(N1), 0.5)
            if stop == "first":
                V.tensor_copy(small[:, 121:122], epsc[:]).then_inc(sem["final"], 1)
            else:
                event("att_in", 16 * 9)
                pre_norm(lambda t: ctxr[:, t, :])
                to_x(3)
                split_a()
                split_a()
                split_a()
                pre_norm(); to_x(3)
                split_a(); split_a()
                unit_skip(5)
                event("squares")
                V.reduce_sum(rms[:, 0:32], mod[:].rearrange("p k (h d) -> p (k h) d", d=64), AX)
                link(V.reduce_sum(rms[:, 32:48], xn[:, 0, :].rearrange("p (h d) -> p h d", d=64), AX))
                V.tensor_scalar(rms, rms, 1.0 / 64, EPS, ALU.mult, ALU.add).then_inc(sem["head_ms"], 1)
                event("head_root")
                link(V.reciprocal(rms, rms))
                q64 = qq.rearrange("p t (h d) -> p (t h) d", d=64)
                k64 = kk.rearrange("p t (h d) -> p (t h) d", d=64)
                V.tensor_tensor(q64, q64, rms[:, 0:32].unsqueeze(2).broadcast_to([P, 32, 64]), ALU.mult)
                link(V.tensor_tensor(k64, k64, rms[:, 32:48].unsqueeze(2).broadcast_to([P, 16, 64]), ALU.mult))
                for y in range(2):
                    for t in range(NT):
                        v = qq[:, t, y * 512:(y + 1) * 512].rearrange("p (h d) -> p h d", d=64)
                        V.tensor_tensor(v, v, qkg[:, y:y + 1, :].broadcast_to([P, 8, 64]), ALU.mult)
                    for t in range(4):
                        v = kk[:, t, y * P:(y + 1) * P].rearrange("p (h d) -> p h d", d=64)
                        ins = V.tensor_tensor(v, v, qkg[:, 2 + y:3 + y, :].broadcast_to([P, 2, 64]), ALU.mult)
                link(ins)
                tmp = mod[:].rearrange("p k s -> p (k s)").rearrange("p (i h d) -> p i h d", i=4, d=32)
                for t in range(NT):
                    for x, nh in ((qq[:, t, :], 16), (kk[:, 2 + t, :], 4)):
                        x = x.rearrange("p (h d two) -> p h d two", d=32, two=2)
                        for i, (side, trig) in enumerate(((0, 0), (1, 1), (0, 1), (1, 0))):
                            tb = rope2[:, t, 32 * trig:32 * trig + 32].unsqueeze(1).broadcast_to([P, nh, 32])
                            ins = V.tensor_tensor(tmp[:, i, 0:nh], x[:, :, :, side], tb, ALU.mult)
                        link(ins)
                        V.tensor_tensor(x[:, :, :, 0], tmp[:, 0, 0:nh], tmp[:, 1, 0:nh], ALU.subtract)
                        link(V.tensor_tensor(x[:, :, :, 1], tmp[:, 2, 0:nh], tmp[:, 3, 0:nh], ALU.add))
                V.tensor_scalar(nsink, nsink, -1.0, None, ALU.mult).then_inc(sem["roped2"], 1)
                split_a()
                event("qk2_psum")
                V.tensor_copy(kT, psum[:, 4:6, :]).then_inc(sem["kT"], 1)
                i = 0
                for y in range(2):
                    for t in range(NT):
                        for h in range(8):
                            n = y * 16 + t * 8 + h
                            event("scores2")
                            if y:
                                link(V.tensor_tensor(psum[:, i % 2, S:2 * S], psum[:, i % 2, S:2 * S], band[:, t, :], ALU.add))
                            link(V.reduce_max(sm2[:, 0, n:n + 1], psum[:, i % 2, :], AX))
                            if y:
                                ins = V.tensor_scalar(sm2[:, 1, n:n + 1], sm2[:, 0, n:n + 1], -(64.0 ** -0.5), nsink[:, h:h + 1], ALU.mult, ALU.min)
                            else:
                                ins = V.tensor_scalar(sm2[:, 1, n:n + 1], sm2[:, 0, n:n + 1], -(64.0 ** -0.5), None, ALU.mult)
                            ins.then_inc(sem["amax2"], 1)
                            i += 1
                event("probs2", 32)
                for t in range(NT):
                    s = slice(16 + 8 * t, 24 + 8 * t)
                    ins = V.tensor_tensor(sm2[:, 0, s], sm2[:, 1, s], nsink, ALU.subtract)
                ins.then_inc(sem["sink_arg"], 1)
                event("sink_exp")
                link(V.tensor_tensor(sm2[:, 2, 16:32], sm2[:, 2, 16:32], sm2[:, 0, 16:32], ALU.add))
                link(V.reciprocal(sm2[:, 3, :], sm2[:, 2, :]))
                event("pv2_psum", 2)
                for y in range(2):
                    for t in range(NT):
                        n = 16 * y + 8 * t
                        ins = V.tensor_tensor(xn[:, t, y * 512:(y + 1) * 512].rearrange("p (h d) -> p h d", d=64),
                                              psum[:, 4 + 2 * y + t, :].rearrange("p (h d) -> p h d", d=64),
                                              sm2[:, 3, n:n + 8].unsqueeze(2).broadcast_to([P, 8, 64]), ALU.mult)
                ins.then_inc(sem["xn_ready"], 1)
                to_x(0, "gain_one")
                unit_skip()
                split_a()
                unit()
                post_norm(lambda: None, 1.0, False)
                pre_norm(); to_x(3); ffn("dve_ffn", N1, PIECE)
                post_norm(lambda: y_done(N1), 1.0, False)
                pre_norm(); to_x(3)
                V.memset(zT[:, :, 0:1], 0.0)
                V.memset(zT[:, :, S + 1:S + 2], 0.0)
                banks = ((4, 2, 0), (6, 4, 2))

                def blocks4(b):
                    return psum[:, b:b + 2, :].rearrange("p b (h s) -> p (b h) s", s=S)
                for half in range(2):
                    split_a()
                    unit()
                    event("cg")
                    if half == 0:
                        V.tensor_copy(small[:, 241:242], epsc[:]).then_inc(sem["conv_free"], 1)
                    split_a()
                    unit()
                    ins = V.tensor_tensor(zT[:, :, 1:S + 1], cg, blocks4(banks[half][1]), ALU.mult)
                    link(ins)
                    if half == 0:
                        V.tensor_copy(small[:, 242:243], epsc[:]).then_inc(sem["conv_free"], 1)
                        V.tensor_copy(small[:, 243:244], epsc[:]).then_inc(sem["cg_used"], 1)
                    split_a()
                    for j in range(3):
                        for c in range(4):
                            w = convw2[:, j, 4 * half + c:4 * half + c + 1]
                            if j == 0:
                                ins = V.tensor_scalar(acc[:, c, :], zT[:, c, 0:S], w, None, ALU.mult)
                            else:
                                ins = V.scalar_tensor_tensor(acc[:, c, :], zT[:, c, j:j + S], w, acc[:, c, :], ALU.mult, ALU.add)
                        link(ins)
                    unit()
                    ins = V.tensor_tensor(mod[:, 4 * half:4 * half + 4, :], acc, blocks4(banks[half][2]), ALU.mult)
                    if half == 1:
                        ins.then_inc(sem["mixed_conv"], 1)
                for half in range(2):
                    event("x_hi")
                    s4 = slice(4 * half, 4 * half + 4)
                    V.tensor_tensor(x_lo[:, s4, :], mod[:, s4, :], f(x_hi[:, s4, :]), ALU.subtract).then_inc(sem["x_lo"], 1)
                split_a()
                unit_skip()
                split_a(4 * NE)
                unit()
                post_norm(lambda: None, 1.0, False)
                pre_norm(); to_x(3)
                split_a()
                unit()
                L, e1, c1, f1, L2, f2, m, g8 = (lg[:, i] for i in range(8))
                link(V.tensor_copy(L, MB[:, 0:2 * NE].rearrange("p (t e) -> p t e", e=NE)))
                ones8 = small[:, 244:252]
                link(V.memset(ones8, 1.0))

                def first_max(src, dst, col):
                    link(V.reduce_max(m[:, :, col:col + 1], src, AX))
                    for t in range(NT):
                        ins = V.tensor_scalar(e1[:, t, :], src[:, t, :], m[:, t, col:col + 1], None, ALU.is_equal)
                    link(ins)
                    for t in range(NT):
                        ins = V.tensor_tensor_scan(c1[:, t, :], ones8, e1[:, t, :], 0.0, ALU.mult, ALU.add)
                    link(ins)
                    link(V.scalar_tensor_tensor(dst, c1, 1.0, e1, ALU.is_equal, ALU.mult))

                first_max(L, f1, 1)
                link(V.scalar_tensor_tensor(L2, f1, NEG, L, ALU.mult, ALU.add))
                first_max(L2, f2, 2)
                V.tensor_tensor(m[:, :, 0:1], m[:, :, 2:3], m[:, :, 1:2], ALU.subtract).then_inc(sem["top2"], 1)
                event("top2_exp")
                link(V.tensor_scalar(m[:, :, 3:4], m[:, :, 0:1], 1.0, None, ALU.add))
                link(V.reciprocal(m[:, :, 3:4], m[:, :, 3:4]))
                link(V.tensor_tensor(m[:, :, 4:5], m[:, :, 0:1], m[:, :, 3:4], ALU.mult))
                for t in range(NT):
                    ins = V.tensor_scalar(g8[:, t, :], f1[:, t, :], m[:, t, 3:4], None, ALU.mult)
                link(ins)
                for t in range(NT):
                    ins = V.scalar_tensor_tensor(g8[:, t, :], f2[:, t, :], m[:, t, 4:5], g8[:, t, :], ALU.mult, ALU.add)
                link(ins)
                for t in range(NT):
                    ins = V.tensor_copy(gexp[:, t, :].rearrange("p (e c) -> p e c", c=NX),
                                        g8[:, t, :].unsqueeze(2).broadcast_to([P, NE, NX]))
                link(ins)
                ffn("dve_moe", NM, None, lambda u: (lambda t: gexp[:, t, bass.ds(u, 1)]))
                post_norm(lambda: y_done(NM), 1.0, False)
                V.tensor_copy(small[:, 121:122], epsc[:]).then_inc(sem["final"], 1)


NAMES = [
    "x", "ff1_norm_pre", "ff1_w_gate", "ff1_w_up", "ff1_w_down", "ff1_norm_post", "mix_norm_pre", "w_in",
    "conv_w", "conv_b", "dt_bias", "a_log", "d_skip", "ssd_norm", "pool_w", "pool_scale", "w_out",
    "mix_norm_post", "ff2_norm_pre", "ff2_w_gate", "ff2_w_up", "ff2_w_down", "ff2_norm_post", "c_2",
    "ctx_2", "c_ctx_2", "ada_w_2", "ada_b_2", "norm1_g_2", "norm2_g_2", "attn_w_in_2", "attn_w_out_2",
    "qnorm_a_2", "knorm_a_2", "qnorm_b_2", "knorm_b_2", "sink_b_2", "ffn_w_gate_2", "ffn_w_up_2",
    "ffn_w_down_2", "conv_w_in_2", "conv_w_2", "conv_w_out_2", "router_w_2", "moe_w_gate_2",
    "moe_w_up_2", "moe_w_down_2"]


def constants():
    f4 = np.float32
    i, j = np.arange(P)[:, None], np.arange(P)[None, :]
    low = np.where(j <= i, 0.0, NEG)
    z = np.zeros((P, P))
    tok = np.arange(S, dtype=f4)
    inv = (f4(500000.0) ** (-np.arange(0, 16, 2, dtype=f4) / f4(16))).astype(f4)
    ang = (tok[:, None] * inv[None, :]).astype(f4)
    rope = np.concatenate([np.cos(ang), np.sin(ang)], -1).reshape(NT, P, 16).transpose(1, 0, 2)
    cnt = np.empty((P, 2, S))
    for g in range(4):
        cnt[64 * (g % 2):64 * (g % 2) + 64, g // 2, :] = 1.0 / np.minimum(np.arange(1, S + 1), 2 ** (g + 1))
    inv2 = (f4(10000.0) ** (-np.arange(0, 32, 2, dtype=f4) / f4(32))).astype(f4)
    row, col = np.divmod(np.arange(S), 64)
    ang2 = np.concatenate([row[:, None].astype(f4) * inv2, col[:, None].astype(f4) * inv2], -1).astype(f4)
    rope2 = np.concatenate([np.cos(ang2), np.sin(ang2)], -1).reshape(NT, P, 64).transpose(1, 0, 2)
    q, k = np.arange(S)[:, None], np.arange(S)[None, :]
    band = np.where(np.abs(q - k) <= 128, 0.0, NEG).reshape(NT, P, S).transpose(1, 0, 2)
    return {k_: np.ascontiguousarray(v, dtype=f4) for k_, v in {
        "c_ident": np.eye(P), "c_cmask": np.concatenate([low.T, z], 1), "c_qmask": np.concatenate([low, z, low], 1),
        "c_rope": rope, "c_rcnt": cnt, "c_rope2": rope2, "c_band": band}.items()}


def kernel(**inputs):
    from concourse import bacc
    from concourse.bass_utils import run_bass_kernel_spmd

    nc = bacc.Bacc("TRN2", target_bir_lowering=False, num_devices=1)
    arrays = {}
    for name in NAMES:
        arrays[name] = np.ascontiguousarray(inputs[name])
    arrays.update(constants())
    T = {}
    for name, a in arrays.items():
        T[name] = nc.dram_tensor(f"in_{name}", a.shape, F32, kind="ExternalInput").ap()
    out = nc.dram_tensor("out_0", (1, S, D), F32, kind="ExternalOutput").ap()
    mods = nc.dram_tensor("mods", (DEPTH, 2, ADA), F32).ap()
    build(nc, T, out, mods)
    r = run_bass_kernel_spmd(nc, [{f"in_{k}": v for k, v in arrays.items()}], core_ids=[0])
    return r.results[0]["out_0"]
```

```python
from contextlib import ExitStack, contextmanager

import numpy as np

import concourse.bass as bass
from concourse import mybir

F32 = mybir.dt.float32
F32R = mybir.dt.float32r
ACT = mybir.ActivationFunctionType
ALU = mybir.AluOpType
AX = mybir.AxisListType.X

P = 128
S = 256
NT = S // P
D = 1024
KD = D // P
DEPTH = 2
F1 = 2816
FE = 3584
NE = 8
FC = 256
FB = FC // P
N1 = F1 // FC
NX = FE // FC
NM = NE * NX
GC = 512
PIECE = 2048
EPS = 1e-6
NEG = -1e30

SSD_IN, HEADS, HP = 512, 8, 64
OFF_XBC, OFF_DT, OFF_U, OFF_Q, OFF_K, OFF_V = 512, 1536, 1544, 1800, 2056, 2312
PAD = 16
CPAD = 3
ADA = 6 * D
AC = ADA // (2 * 8)

PER_TURN = {'act_ff1': {'a_done': 2,
             'a_free': 2,
             'd_free': 2,
             'gu0': 2,
             'raw0': 32,
             'raw1': 32,
             'raw2': 32,
             't_psum': 2},
 'act_ff2': {'a_done': 2,
             'a_free': 2,
             'd_free': 2,
             'gu0': 2,
             'raw0': 32,
             'raw1': 32,
             'raw2': 32,
             't_psum': 2},
 'act_ffn': {'a_done': 2,
             'a_free': 2,
             'd_free': 2,
             'gu0': 2,
             'raw0': 32,
             'raw1': 32,
             'raw2': 32,
             't_psum': 2},
 'act_layer': {'a_done': 30,
               'a_free': 30,
               'act_step': 11,
               'amax': 4,
               'arg': 2,
               'ctx_stored': 16,
               'd_free': 22,
               'gated': 1,
               'gu0': 22,
               'mix_par': 144,
               'ms': 7,
               'pT_psum': 4,
               'pool_psum': 1,
               'qk_psum': 1,
               'raw0': 512,
               'raw1': 512,
               'raw2': 352,
               'res_ready': 3,
               'scale': 4,
               't_psum': 22,
               'taps_bc': 1,
               'taps_xs': 1,
               'xt_psum': 8,
               'y_done': 22},
 'act_moe': {'a_done': 2,
             'a_free': 2,
             'd_free': 2,
             'gu0': 2,
             'raw0': 32,
             'raw1': 32,
             'raw2': 32,
             't_psum': 2},
 'dve_ff1': {'ada_bias0': 16,
             'ada_bias1': 16,
             'ada_in0': 16,
             'ada_in1': 16,
             'ada_sum': 2,
             'dve_step': 14,
             'hi': 6,
             'ht_hi': 2,
             'sg0': 2,
             'sg1': 2},
 'dve_ff2': {'ada_bias0': 16,
             'ada_bias1': 16,
             'ada_in0': 16,
             'ada_in1': 16,
             'ada_sum': 2,
             'dve_step': 14,
             'hi': 6,
             'ht_hi': 2,
             'sg0': 2,
             'sg1': 2},
 'dve_ffn': {'hi': 6, 'ht_hi': 2, 'sg0': 2, 'sg1': 2},
 'dve_layer': {'a_done': 30,
               'acs_psum': 2,
               'ada_bias0': 128,
               'ada_bias1': 128,
               'ada_in0': 128,
               'ada_in1': 128,
               'ada_sum': 16,
               'bc_out': 1,
               'cb_psum': 1,
               'ctx_bias': 16,
               'ctx_used1': 2,
               'decay': 2,
               'dt_psum': 1,
               'dve_step': 146,
               'gain': 80,
               'gain_one': 1,
               'gain_row': 48,
               'hi': 82,
               'ht_hi': 22,
               'kv_out': 1,
               'mix_par': 144,
               'pT_psum': 4,
               'pool_out': 1,
               'probs': 4,
               'pv_psum': 4,
               'root': 7,
               'scores': 4,
               'sg0': 22,
               'sg1': 22,
               'soft': 1,
               'ssd_psum': 2,
               'ssq': 7,
               'x_hi': 8,
               'xs_out': 1,
               'xs_psum': 1,
               'y_done': 22},
 'dve_moe': {'hi': 6, 'ht_hi': 2, 'sg0': 2, 'sg1': 2},
 'pe_ff1': {'ada_acc0': 1,
            'ada_acc1': 1,
            'h0': 2,
            'h1': 2,
            'ht': 2,
            'split0': 2,
            'split1': 2,
            'split2': 2},
 'pe_ff2': {'ada_acc0': 1,
            'ada_acc1': 1,
            'h0': 2,
            'h1': 2,
            'ht': 2,
            'split0': 2,
            'split1': 2,
            'split2': 2},
 'pe_ffn': {'h0': 2, 'h1': 2, 'ht': 2, 'split0': 2, 'split1': 2, 'split2': 2},
 'pe_layer': {'acs_rows': 1,
              'ada_acc0': 8,
              'ada_acc1': 8,
              'arg': 2,
              'bc_out': 1,
              'conv_bc': 1,
              'conv_xs': 1,
              'ctx_row': 1,
              'dtc': 1,
              'h0': 22,
              'h1': 22,
              'ht': 22,
              'kv_out': 1,
              'mix_par': 144,
              'pT': 4,
              'pool_out': 1,
              'pooled': 1,
              'probs': 4,
              'qkT': 1,
              'raw0': 512,
              'raw1': 512,
              'roped': 1,
              'seg': 2,
              'split0': 30,
              'split1': 30,
              'split2': 22,
              'uq_out': 1,
              'x_lo': 8,
              'xdt': 1,
              'xn_ready': 4,
              'xs_out': 1,
              'z_out': 1},
 'pe_moe': {'h0': 2, 'h1': 2, 'ht': 2, 'split0': 2, 'split1': 2, 'split2': 2},
 'pool_ada1': {'ada_bias_free': 2, 'ada_row': 2, 'ada_stored0': 16, 'ada_stored1': 16},
 'pool_ada2': {'ada_bias_free': 2, 'ada_row': 2, 'ada_stored0': 16, 'ada_stored1': 16},
 'pool_layer': {'ada_bias_free': 16,
                'ada_row': 16,
                'ada_stored0': 128,
                'ada_stored1': 128,
                'ctx_row': 1,
                'ctx_stored': 16,
                'pool_step': 9,
                'res_ready': 3,
                'uq_out': 1,
                'x_lo': 8},
 'sp_ff1': {'ada_acc0': 1, 'ada_acc1': 1, 'split0': 2, 'split1': 2, 'split2': 2},
 'sp_ff2': {'ada_acc0': 1, 'ada_acc1': 1, 'split0': 2, 'split1': 2, 'split2': 2},
 'sp_ffn': {'split0': 1, 'split1': 1, 'split2': 1},
 'sp_layer': {'ada_acc0': 8,
              'ada_acc1': 8,
              'ctx_used0': 2,
              'ctx_used1': 2,
              'res_ready': 3,
              'split0': 30,
              'split1': 30,
              'split2': 22},
 'sp_moe': {'split0': 14, 'split1': 14, 'split2': 14},
 'sp_moe0': {'split0': 1, 'split1': 1, 'split2': 1},
 'sp_moec': {'split0': 1, 'split1': 1, 'split2': 1}}
PER_TURN_SEEN = {}


class Seen:

    def __init__(self):
        self.count = {}
        self.loops = []

    def __call__(self, name, events=1):
        self.count[name] = self.count.get(name, 0) + events
        value = self.count[name]
        for turn, label in self.loops:
            per = PER_TURN.get(label, {}).get(name, 0)
            if per:
                value = turn * per + value
        return value

    @contextmanager
    def loop(self, engine, label, turns, start=0):
        before = dict(self.count)
        with engine.Fori(start, start + turns) as i:
            self.loops.append((i - start if start else i, label))
            yield i
            self.loops.pop()
        per = {k: v - before.get(k, 0) for k, v in self.count.items() if v != before.get(k, 0)}
        PER_TURN_SEEN[label] = per
        for k, v in per.items():
            self.count[k] = before.get(k, 0) + v * turns


def build(nc, T, out, mods, stop=None):
    ctx = ExitStack()
    with ctx:
        def sb(name, shape, dt=F32):
            return ctx.enter_context(nc.sbuf_tensor(name, shape, dt))

        sems = {}

        class Sems:
            def __getitem__(self, name):
                if name not in sems:
                    sems[name] = ctx.enter_context(nc.semaphore(name))
                return sems[name]
        sem = Sems()

        raw = sb("raw", [P, 3, PIECE])
        a_hi, a_lo = sb("a_hi", [P, 2, 2, PIECE], F32R), sb("a_lo", [P, 2, 2, PIECE], F32R)
        d_hi, d_lo = sb("d_hi", [P, PIECE], F32R), sb("d_lo", [P, PIECE], F32R)
        x_hi, x_lo = sb("x_hi", [P, KD, S], F32R), sb("x_lo", [P, KD, S], F32R)
        ht_hi, ht_lo = sb("ht_hi", [P, FB, S], F32R), sb("ht_lo", [P, FB, S], F32R)
        res = sb("res", [P, NT, D])
        xn = sb("xn", [P, NT, D])
        mod = sb("mod", [P, KD, S])
        gbc = sb("gbc", [P, D])
        gcol = sb("gcol", [P, 4, KD])
        sg = sb("sg", [P, NT, FC])
        hb = sb("hb", [P, NT, FC])
        st = sb("st", [P, 2, NT])
        ident = sb("ident", [P, P])
        cmask = sb("cmask", [P, 2 * P])
        qmask = sb("qmask", [P, 3 * P])
        epsc = sb("epsc", [P, 1])
        small = sb("small", [P, 256])
        ARENA = 9504
        arena = sb("arena", [P, ARENA])
        psum = ctx.enter_context(nc.psum_tensor("psum", [P, 8, 512], F32))
        Y = psum[:, 0:4, :].rearrange("p (t h) n -> p t (h n)", t=NT)
        TB, MB = psum[:, 6, :], psum[:, 7, :]

        def f(ap):
            return ap.bitcast(F32)

        def area(at, *shape):
            n = int(np.prod(shape))
            assert at + n <= ARENA, (at, n)
            ap = arena[:, at:at + n]
            if len(shape) == 2:
                ap = ap.rearrange("p (a b) -> p a b", b=shape[1])
            if len(shape) == 3:
                ap = ap.rearrange("p (a b c) -> p a b c", b=shape[1], c=shape[2])
            return ap

        ones = sb("ones", [P, 1])
        adaw = area(0, 2, KD, AC)
        adaa = area(2 * KD * AC, 2, AC)
        adar = area(2 * KD * AC + 2 * AC, 2, AC)[0:1]
        crow = area(6688, D)[0:1]
        zs = area(0, NT, SSD_IN)
        xT = area(1024, 8, CPAD + S + 1)
        arg = area(1024, 4, 384)
        cT = mod
        xdt = area(3104, NT, SSD_IN)
        xsd = area(4128, NT, SSD_IN)
        qk = area(5152, NT, 512)
        vv = area(6176, NT, 256)
        qkT = area(6688, 4, S)
        prob = area(7712, 384)
        pT = area(8096, 384)
        dts = area(8480, 4 * S)[0:HEADS]
        uw = [sb(f"uw{i}", [P, 2, PAD + S]) for i in range(2)]
        um, pm = hb, sg
        poolw = sb("poolw", [P, 2, P])
        convw = small[:, 0:32].rearrange("p (j c) -> p j c", c=8)
        convb = small[:, 32:40]
        dskip = small[:, 40:48]
        dtb, alog = small[0:8, 48:49], small[0:8, 49:50]
        dtc = small[:, 52:68].rearrange("p (t h) -> p t h", h=8)
        nacs = small[:, 68:84].rearrange("p (t h) -> p t h", h=8)
        qstat = small[:, 84:108].rearrange("p (c h t) -> p c h t", c=3, t=NT)
        rope = sb("rope", [P, NT, 16])
        rcnt = sb("rcnt", [P, 2, S])

        cs = sb("cs", [P, KD, 2])
        qq = area(0, NT, 1024)
        kk = area(2048, 4, 256)
        vk = area(3072, 4, 256)
        qT = area(4096, 8, S)
        kT = area(6144, 2, 512)
        prob2 = area(7168, 2, 512)
        pT2 = area(8192, 2, 512)
        ctxr = area(4096, NT, D)
        band = hb
        rope2 = sg[:, 0, 0:128].rearrange("p (t n) -> p t n", t=NT)
        qkg = sg[:, 1, :].rearrange("p (i n) -> p i n", n=64)
        rms = small[:, 160:208]
        nsink = small[:, 148:156]
        sm2 = sb("sm2", [P, 4, 32])
        cg = area(0, 4, S)
        zT = area(1024, 4, S + 2)
        acc = area(2056, 4, S)
        convw2 = small[:, 210:234].rearrange("p (j c) -> p j c", c=8)
        lg = area(0, 8, NT, NE)
        gexp = area(256, NT, NM)
        CONV_UNITS = [1024, 2048, 0, 1536, 2560, 512]

        block = ctx.enter_context(nc.Block())

        def colsof(row):
            return row.rearrange("(k p) -> p k", p=P)

        def kview(w):
            return w.rearrange("(k p) n -> p k n", p=P)

        IN_UNITS = [(OFF_DT, 8), (1024, 512), (512, 512), (OFF_U, 512), (OFF_K, 512), (0, 512)]

        @block.sync
        def _(sp):
            seen = Seen()

            def piece(j, src, dst, free=None):
                free = free or f"split{j}"
                sp.wait_ge(sem[free], seen(free))
                sp.sem_inc(sem["sp_past_wait"], 1)
                sp.dma_start(dst, src).then_inc(sem[f"raw{j}"], 16)

            def plain(w, c0, n):
                v = kview(w)
                for j in range(2):
                    dst = raw[:, j, 0:4 * n].rearrange("p (k n) -> p k n", n=n)
                    piece(j, v[:, 4 * j:4 * j + 4, bass.ds(c0, n)], dst)

            def gate_up(wg, wu, c0):
                for j, w in enumerate((wg, wu)):
                    piece(j, kview(w)[:, :, bass.ds(c0, FC)],
                          raw[:, j, :].rearrange("p (k n) -> p k n", n=FC))

            def down(wd, c0):
                piece(2, wd[bass.ds(c0, FC), :].rearrange("(b p) n -> p b n", p=P),
                      raw[:, 2, :].rearrange("p (b n) -> p b n", n=D))

            def ffn(label, wg, wu, wd, after=(), ada=None):
                gate_up(wg, wu, 0)
                gate_up(wg, wu, FC)
                if ada is None:
                    with seen.loop(sp, label, N1 - 2) as i:
                        gate_up(wg, wu, i * FC + 2 * FC)
                        down(wd, i * FC)
                else:
                    sp.wait_ge(sem["res_ready"], seen("res_ready", ada[2]))
                    sp.sem_inc(sem["sp_past_wait"], 1)
                    with seen.loop(sp, label, 4) as i:
                        for q in range(2):
                            sp.wait_ge(sem[f"ada_acc{q}"], seen(f"ada_acc{q}"))
                            sp.sem_inc(sem["sp_past_wait"], 1)
                            sp.dma_start(adaw[:, q], kview(ada[0])[:, :, bass.ds(i * 2 * AC + (ada[1] * 8 + q) * AC, AC)]
                                         ).then_inc(sem[f"ada_in{q}"], 16)
                            gate_up(wg, wu, i * 2 * FC + (2 + q) * FC)
                            down(wd, i * 2 * FC + q * FC)
                    gate_up(wg, wu, (N1 - 1) * FC)
                    down(wd, (N1 - 3) * FC)
                for n in (N1 - 2, N1 - 1):
                    if after:
                        after[n - N1 + 2]()
                    down(wd, n * FC)

            def layer(l):
                W = {k: T[k][l] for k in ("ff1_w_gate", "ff1_w_up", "ff1_w_down", "w_in", "w_out",
                                          "ff2_w_gate", "ff2_w_up", "ff2_w_down")}
                ffn("sp_ff1", W["ff1_w_gate"], W["ff1_w_up"], W["ff1_w_down"],
                    [lambda: plain(W["w_in"], *IN_UNITS[0]), lambda: plain(W["w_in"], *IN_UNITS[1])],
                    ada=(T["ada_w_2"][l], 0, 1))
                for u in IN_UNITS[2:]:
                    plain(W["w_in"], *u)
                for c in range(2):
                    for j in range(2):
                        if c == 0:
                            sp.wait_ge(sem[f"split{j}"], seen(f"split{j}"))
                        else:
                            sp.wait_ge(sem[f"ctx_used{j}"], seen(f"ctx_used{j}"))
                        sp.sem_inc(sem["sp_past_wait"], 1)
                        sp.dma_start(raw[:, j, :].rearrange("p (k n) -> p k n", n=GC),
                                     kview(T["ada_w_2"][0])[:, 4 * j:4 * j + 4, bass.ds(l * D + c * GC, GC)]
                                     ).then_inc(sem[f"raw{j}"], 16)
                for j in range(2):
                    piece(j, kview(W["w_out"])[:, 4 * j:4 * j + 4, 0:GC],
                          raw[:, j, :].rearrange("p (k n) -> p k n", n=GC), f"ctx_used{j}")
                plain(W["w_out"], GC, GC)
                ffn("sp_ff2", W["ff2_w_gate"], W["ff2_w_up"], W["ff2_w_down"],
                    ada=(T["ada_w_2"][l], 1, 2))

            with seen.loop(sp, "sp_layer", DEPTH) as l:
                layer(l)
            wi = T["attn_w_in_2"][0]
            if stop == "first":
                plain(wi, 512, 512)
                sp.wait_ge(sem["final"], 1)
                for t in range(NT):
                    sp.dma_start(out[0, t * P:(t + 1) * P, :], res[:, t, :]).then_inc(sem["stored"], 16)
                sp.wait_ge(sem["stored"], 32)
                return
            plain(wi, 512, 256)
            plain(wi, 1280, 256)
            for c in range(3):
                plain(wi, c * GC, GC)
            for c in range(2):
                plain(T["attn_w_out_2"][0], c * GC, GC)
            ffn("sp_ffn", T["ffn_w_gate_2"][0], T["ffn_w_up_2"][0], T["ffn_w_down_2"][0],
                [lambda: plain(T["conv_w_in_2"][0], CONV_UNITS[0], GC),
                 lambda: plain(T["conv_w_in_2"][0], CONV_UNITS[1], GC)])
            for c0 in CONV_UNITS[2:]:
                plain(T["conv_w_in_2"][0], c0, GC)
            for c in range(2):
                plain(T["conv_w_out_2"][0], c * GC, GC)
            plain(T["router_w_2"][0], 0, NE)
            mg, mu = T["moe_w_gate_2"][0], T["moe_w_up_2"][0]
            md = T["moe_w_down_2"][0].rearrange("e f d -> (e f) d")
            for c in range(2):
                gate_up(mg[0], mu[0], c * FC)
            with seen.loop(sp, "sp_moe0", NX - 2) as c:
                gate_up(mg[0], mu[0], c * FC + 2 * FC)
                down(md, c * FC)
            with seen.loop(sp, "sp_moe", NE - 1) as e:
                for c in range(2):
                    gate_up(mg[e + 1], mu[e + 1], c * FC)
                    down(md, e * FE + (NX - 2 + c) * FC)
                with seen.loop(sp, "sp_moec", NX - 2) as c:
                    gate_up(mg[e + 1], mu[e + 1], c * FC + 2 * FC)
                    down(md, e * FE + (FE + c * FC))
            down(md, (NM - 2) * FC)
            down(md, (NM - 1) * FC)
            sp.wait_ge(sem["final"], 1)
            for t in range(NT):
                sp.dma_start(out[0, t * P:(t + 1) * P, :], res[:, t, :]).then_inc(sem["stored"], 16)
            sp.wait_ge(sem["stored"], 32)

        @block.gpsimd
        def _(pool):
            seen = Seen()
            seen.count["ada_row"] = 2
            M = mods

            def bc(row, n=P):
                return row.unsqueeze(0).broadcast_to([n, row.shape[0]])

            def load(dst, src, name="consts"):
                pool.dma_start(dst, src, allow_slow_non_contiguous=True).then_inc(sem[name], 16)

            nc.gpsimd.memset(uw[0][:], 0.0).then_inc(sem["pool_zero"], 1)
            nc.gpsimd.memset(uw[1][:], 0.0).then_inc(sem["pool_zero"], 1)
            nc.gpsimd.memset(poolw[:], 0.0).then_inc(sem["pool_zero"], 1)
            nc.gpsimd.memset(gcol[:], 0.0).then_inc(sem["pool_zero"], 1)
            nc.gpsimd.memset(epsc[:], EPS).then_inc(sem["pool_zero"], 1)
            nc.gpsimd.memset(ones[:], 1.0).then_inc(sem["pool_zero"], 1)
            CONSTS = [(ident[:], T["c_ident"]), (cmask[:, 0:S], T["c_cmask"]), (qmask[:], T["c_qmask"]),
                      (rope[:], T["c_rope"]), (rcnt[:], T["c_rcnt"]),
                      (res[:], T["x"][0].rearrange("(t p) n -> p t n", p=P)),
                      (small[:, 128:136], colsof(T["c_ctx_2"])), (small[:, 136:144], colsof(T["c_2"][0]))]
            for dst, src in CONSTS:
                load(dst, src)
            pool.wait_ge(sem["consts"], 16 * len(CONSTS))
            pool.wait_ge(sem["pool_zero"], 6)
            pool.sem_inc(sem["consts_in"], 1)

            def modulation(l, label, half):
                with seen.loop(pool, label, 4) as i:
                    for q in range(2):
                        pool.wait_ge(sem["ada_row"], seen("ada_bias_free"))
                        pool.sem_inc(sem["pool_past_wait"], 1)
                        pool.dma_start(adar[:, q, :], T["ada_b_2"][l][bass.ds(i * 2 * AC + (half * 8 + q) * AC, AC)].unsqueeze(0)
                                       ).then_inc(sem[f"ada_bias{q}"], 16)
                    for q in range(2):
                        pool.wait_ge(sem["ada_row"], seen("ada_row"))
                        pool.sem_inc(sem["pool_past_wait"], 1)
                        pool.dma_start(M[l, 1, bass.ds(i * 2 * AC + (half * 8 + q) * AC, AC)].unsqueeze(0), adar[:, q, :]
                                       ).then_inc(sem[f"ada_stored{q}"], 16)
                    for q in range(2):
                        pool.wait_ge(sem[f"ada_stored{q}"], seen(f"ada_stored{q}", 16))

            def gains_in(first=False):
                pool.wait_ge(sem["x_lo"], seen("x_lo", 2))
                pool.sem_inc(sem["pool_past_wait"], 1)

            def columns(cols):
                gains_in()
                for n, (i, src) in enumerate(cols):
                    pool.dma_start(gcol[:, i, 0:src.shape[1]], src, allow_slow_non_contiguous=True).then_inc(sem["gain"], 16)

            def row(src):
                pool.wait_ge(sem["res_ready"], seen("res_ready"))
                pool.sem_inc(sem["pool_past_wait"], 1)
                pool.dma_start(gbc[:], bc(src)).then_inc(sem["gain_row"], 16)

            def pool_branch(l):
                W = T["pool_w"][l]
                pool.wait_ge(sem["uq_out"], seen("uq_out"))
                pool.sem_inc(sem["pool_past_wait"], 1)
                n = PAD + S
                a, b = uw

                def link(ins):
                    ins.then_inc(sem["pool_step"], 1)
                    pool.wait_ge(sem["pool_step"], seen("pool_step"))
                src, dst = a, b
                link(nc.gpsimd.tensor_copy(um[:], a[:, :, PAD:n]))
                for g in range(4):
                    w = 1 << g
                    lo = 2 * w - 1
                    link(nc.gpsimd.tensor_tensor(dst[:, :, lo:n], src[:, :, lo:n], src[:, :, lo - w:n - w], ALU.add))
                    rows = slice(64 * (g % 2), 64 * (g % 2) + 64)
                    c = g // 2
                    link(nc.gpsimd.tensor_tensor(pm[rows, c, :], dst[rows, c, PAD:n],
                                                 rcnt[rows, c, :], ALU.mult))
                    src, dst = dst, src
                nc.gpsimd.tensor_tensor(um[:], pm[:], um[:], ALU.subtract).then_inc(sem["pooled"], 1)

            def mixer_loads(l):
                for dst, src in [(convw, T["conv_w"][l].rearrange("j (c p) -> p j c", p=P)),
                                 (convb, T["conv_b"][l].rearrange("(c p) -> p c", p=P)),
                                 (dskip, bc(T["d_skip"][l])), (dtb, T["dt_bias"][l].unsqueeze(1)),
                                 (alog, T["a_log"][l].unsqueeze(1))] + [
                                 (poolw[64 * (g % 2):64 * (g % 2) + 64, g // 2, 64 * (g % 2):64 * (g % 2) + 64],
                                  T["pool_w"][l, g]) for g in range(4)]:
                    pool.dma_start(dst, src, allow_slow_non_contiguous=True).then_inc(sem["mix_par"], 16)

            with seen.loop(pool, "pool_layer", DEPTH) as l:
                mixer_loads(l)
                columns([(0, colsof(T["ff1_norm_pre"][l]))])
                row(T["ff1_norm_post"][l])
                modulation(l, "pool_ada1", 0)
                columns([(0, colsof(T["mix_norm_pre"][l]))])
                row(T["mix_norm_post"][l])
                pool.dma_start(crow, T["ada_b_2"][0][bass.ds(l * D, D)].unsqueeze(0)).then_inc(sem["ctx_bias"], 16)
                pool_branch(l)
                pool.wait_ge(sem["ctx_row"], seen("ctx_row"))
                pool.sem_inc(sem["pool_past_wait"], 1)
                pool.dma_start(M[0, 0, bass.ds(l * D, D)].unsqueeze(0), crow).then_inc(sem["ctx_stored"], 16)
                gains_in()
                pool.dma_start(gcol[:, 0, 0:4], colsof(T["ssd_norm"][l]), allow_slow_non_contiguous=True).then_inc(sem["gain"], 16)
                pool.dma_start(gcol[:, 0, 4:6], colsof(T["pool_scale"][l]), allow_slow_non_contiguous=True).then_inc(sem["gain"], 16)
                nc.gpsimd.memset(gcol[:, 0, 6:8], 1.0).then_inc(sem["gain_one"], 1)
                columns([(0, colsof(T["ff2_norm_pre"][l]))])
                row(T["ff2_norm_post"][l])
                modulation(l, "pool_ada2", 1)
                pool.wait_ge(sem["ctx_stored"], seen("ctx_stored", 16))
            if stop != "first":
                def part(l, r, i):
                    return M[l, r, i * D:(i + 1) * D]
                G1, G2 = T["norm1_g_2"], T["norm2_g_2"]
                columns([(0, colsof(G1[0])), (1, colsof(part(0, 0, 0))), (2, colsof(part(0, 0, 1)))])
                row(part(0, 1, 2))
                for dst, src in [(ctxr, T["ctx_2"][0].rearrange("(t p) n -> p t n", p=P)), (band[:], T["c_band"]),
                                 (rope2, T["c_rope2"]), (nsink, bc(T["sink_b_2"][0])),
                                 (convw2, T["conv_w_2"][0].rearrange("j (c p) -> p j c", p=P))] + [
                                 (qkg[:, i, :], bc(T[n][0])) for i, n in enumerate(
                                     ("qnorm_a_2", "qnorm_b_2", "knorm_a_2", "knorm_b_2"))]:
                    pool.dma_start(dst, src, allow_slow_non_contiguous=True).then_inc(sem["att_in"], 16)
                columns([(0, colsof(G1[0])), (1, colsof(part(0, 1, 0))), (2, colsof(part(0, 1, 1)))])
                gains_in()
                nc.gpsimd.memset(gcol[:, 1:3, :], 0.0).then_inc(sem["pool_zero"], 1)
                nc.gpsimd.memset(gcol[:, 0, :], 1.0).then_inc(sem["gain_one"], 1)
                for l, i, g in ((0, 3, G2), (1, 0, G1), (1, 3, G2)):
                    columns([(0, colsof(g[l])), (1, colsof(part(l, 1, i))), (2, colsof(part(l, 1, i + 1)))])
                    row(part(l, 1, i + 2))
                    if (l, i) == (1, 0):
                        seen("x_lo", 2)

        @block.tensor
        def _(pe):
            seen = Seen()
            seen.count.update({"split0": 1, "split1": 1, "split2": 1, "x_lo": 2, "ada_acc0": 1, "ada_acc1": 1})
            pe.sem_inc(sem["a_done"], 2)
            pe.sem_inc(sem["d_done"], 1)
            par = [0]

            def mm3(o, xh, xl, wh, wl, start, stop_):
                pe.matmul(o, xh, wh, start=start, stop=False, skip_group_check=True)
                pe.matmul(o, xh, wl, start=False, stop=False, skip_group_check=True)
                return pe.matmul(o, xl, wh, start=False, stop=stop_, skip_group_check=True)

            def split_in():
                for j in range(2):
                    pe.wait_ge(sem[f"split{j}"], seen(f"split{j}"))

            def wview(n):
                b = par[0]
                return [w[:, b, :, 0:4 * n].rearrange("p j (k n) -> p j k n", n=n) for w in (a_hi, a_lo)]

            def plain_tok(outs, n, c0=0, w=None, last=True):
                w = w or n
                wh, wl = wview(n)
                for t in range(NT):
                    for k in range(KD):
                        ins = mm3(outs[t], x_hi[:, k, t * P:(t + 1) * P], x_lo[:, k, t * P:(t + 1) * P],
                                  wh[:, k // 4, k % 4, c0:c0 + w], wl[:, k // 4, k % 4, c0:c0 + w],
                                  k == 0, k == KD - 1)
                if last:
                    ins.then_inc(sem["a_done"], 1)
                    par[0] ^= 1

            def plain_tr(outs, n, last=True):
                wh, wl = wview(n)
                m = min(P, n)
                for c, o in enumerate(outs):
                    for k in range(KD):
                        a, b = (w[:, k // 4, k % 4, c * P:c * P + m] for w in (wh, wl))
                        pe.matmul(o, a, x_hi[:, k, :], start=k == 0, stop=False, skip_group_check=True)
                        pe.matmul(o, b, x_hi[:, k, :], start=False, stop=False, skip_group_check=True)
                        ins = pe.matmul(o, a, x_lo[:, k, :], start=False, stop=k == KD - 1, skip_group_check=True)
                if last:
                    ins.then_inc(sem["a_done"], 1)
                    par[0] ^= 1

            def halves(bank):
                return [psum[:, b, h * S:(h + 1) * S] for b in bank for h in range(2)]

            def gate_up():
                split_in()
                b = par[0]
                for t in range(NT):
                    for k in range(KD):
                        wh, wl = (w[:, b, :, k * FC:(k + 1) * FC] for w in (a_hi, a_lo))
                        ins = mm3(psum[:, 4 + t, :].rearrange("p (a n) -> p a n", n=FC),
                                  x_hi[:, k, t * P:(t + 1) * P], x_lo[:, k, t * P:(t + 1) * P],
                                  wh, wl, k == 0, k == KD - 1)
                    ins.then_inc(sem["a_done"] if t else sem["gu0"], 1)
                par[0] ^= 1

            def down(first, last):
                pe.wait_ge(sem["split2"], seen("split2"))
                pe.wait_ge(sem["ht"], seen("ht"))
                for t in range(NT):
                    for h in range(2):
                        for b in range(FB):
                            wh, wl = (w[:, b * D + h * 512:b * D + h * 512 + 512] for w in (d_hi, d_lo))
                            ins = mm3(psum[:, 2 * t + h, :], ht_hi[:, b, t * P:(t + 1) * P],
                                      ht_lo[:, b, t * P:(t + 1) * P], wh, wl,
                                      first and b == 0, last and b == FB - 1)
                ins.then_inc(sem["d_done"], 1)

            def turn_hidden():
                for t in range(NT):
                    pe.wait_ge(sem[f"h{t}"], seen(f"h{t}"))
                    for b in range(FB):
                        ins = pe.transpose(TB[:, b * S + t * P:b * S + (t + 1) * P], hb[:, t, b * P:(b + 1) * P], ident[:])
                ins.then_inc(sem["t_psum"], 1)

            def column_sum(q):
                pe.wait_ge(sem[f"ada_acc{q}"], seen(f"ada_acc{q}"))
                pe.matmul(MB[0:1, 0:AC], ones[:], adaa[:, q, :], start=True, stop=True).then_inc(sem["ada_sum"], 1)

            def ffn(label, n, ada=False):
                gate_up(); turn_hidden()
                gate_up(); down(True, False)
                if ada:
                    column_sum(0)
                turn_hidden()
                with seen.loop(pe, label, (n - 3) // 2 - ada):
                    for q in range(2):
                        gate_up(); down(False, False)
                        if ada:
                            column_sum(1 - q)
                        turn_hidden()
                if ada:
                    gate_up(); down(False, False); column_sum(1); turn_hidden()
                    gate_up(); down(False, False); turn_hidden()
                for _ in range(1 + (n - 3) % 2):
                    gate_up(); down(False, False); turn_hidden()
                down(False, True)

            def to_x():
                pe.wait_ge(sem["xn_ready"], seen("xn_ready"))
                for k in range(KD):
                    for t in range(NT):
                        ins = pe.transpose(psum[:, k // 2, (k % 2) * S + t * P:(k % 2) * S + (t + 1) * P],
                                           xn[:, t, k * P:(k + 1) * P], ident[:])
                    if k % 4 == 3:
                        ins.then_inc(sem["xt_psum"], 1)
                pe.wait_ge(sem["x_lo"], seen("x_lo", 2))

            def event(name):
                pe.wait_ge(sem[name], seen(name))

            def mixer():
                split_in(); plain_tr([MB[0:8, 0:S]], 8)
                split_in(); plain_tr(halves((4, 5)), GC)
                split_in(); plain_tr(halves((0, 1)), GC)
                split_in(); plain_tr(halves((2,)), GC, last=False)
                plain_tok([psum[:, 3, t * 256:(t + 1) * 256] for t in range(NT)], GC, 256, 256)
                event("bc_out")
                split_in(); plain_tok([psum[:, 4 + t, :] for t in range(NT)], GC)
                event("xs_out")
                split_in(); plain_tok([psum[:, t, :] for t in range(NT)], GC)
                event("uq_out")
                for j in range(2):
                    seen(f"raw{j}", 16 * (N1 + len(IN_UNITS)))
                for c in range(2):
                    for j in range(2):
                        pe.wait_ge(sem[f"raw{j}"], seen(f"raw{j}", 16))
                        for k in range(4):
                            ins = pe.matmul(psum[0:1, 2 + c, :], cs[:, 4 * j + k, 0:1], raw[:, j, k * GC:(k + 1) * GC],
                                            start=4 * j + k == 0, stop=4 * j + k == KD - 1)
                        ins.then_inc(sem[f"ctx_used{j}"], 1)
                for j in range(2):
                    seen(f"raw{j}", 16 * (2 + N1))
                event("acs_rows")
                pe.sem_inc(sem["pe_past_wait"], 1)
                for i in range(2):
                    for t in range(NT):
                        ins = pe.transpose(TB[:, (i * 2 + t) * 8:(i * 2 + t) * 8 + 8],
                                           dts[:, i * S + t * P:i * S + (t + 1) * P], ident[0:8, 0:8])
                ins.then_inc(sem["dt_psum"], 1)
                event("pooled")
                pe.wait_ge(sem["mix_par"], seen("mix_par", 16 * 9))
                for t in range(NT):
                    for c in range(2):
                        ins = pe.matmul(MB[:, t * S + c * P:t * S + (c + 1) * P], um[:, c, t * P:(t + 1) * P],
                                        poolw[:, c, :], start=True, stop=True)
                ins.then_inc(sem["pool_psum"], 1)
                event("conv_bc"); event("dtc"); event("pool_out")
                for g, o in ((0, TB), (1, MB)):
                    pe.matmul(o[:, 0:S], cT[:, 4 + g, 0:P], cT[:, 6 + g, :], start=True, stop=True)
                    ins = pe.matmul(o[:, S:S + P], cT[:, 4 + g, P:S], cT[:, 6 + g, P:S], start=True, stop=True)
                ins.then_inc(sem["cb_psum"], 1)
                event("ctx_row")
                for g in range(2):
                    if g:
                        event("arg")
                    for h in range(4):
                        ins = pe.matmul(psum[:, 2 + h // 2, (h % 2) * S:(h % 2) * S + S], ident[0:8, 4 * g + h:4 * g + h + 1].broadcast_to([8, P]),
                                        dts[:, S:2 * S], start=True, stop=True)
                    ins.then_inc(sem["acs_psum"], 1)
                    if g == 0:
                        event("z_out"); event("conv_xs")
                        for t in range(NT):
                            for c in range(4):
                                ins = pe.transpose(psum[:, t, c * P:(c + 1) * P], cT[:, c, t * P:(t + 1) * P], ident[:])
                        ins.then_inc(sem["xs_psum"], 1)
                        event("kv_out"); event("xdt")
                    event("seg")
                    for h in range(4):
                        o = 64 * (4 * g + h)
                        pe.matmul(psum[:, 4, o:o + 64], arg[:, h, 0:P], xdt[:, 0, o:o + 64], start=True, stop=True)
                        pe.matmul(psum[:, 5, o:o + 64], arg[:, h, P:S], xdt[:, 0, o:o + 64], start=True, stop=False)
                        ins = pe.matmul(psum[:, 5, o:o + 64], arg[:, h, S:S + P], xdt[:, 1, o:o + 64], start=False, stop=True)
                    ins.then_inc(sem["ssd_psum"], 1)
                event("roped"); event("arg")
                for a in range(4):
                    for t in range(NT):
                        ins = pe.transpose(psum[:, 2 + a // 2, (a % 2) * S + t * P:(a % 2) * S + (t + 1) * P],
                                           qk[:, t, a * P:(a + 1) * P], ident[:])
                ins.then_inc(sem["qk_psum"], 1)
                event("qkT")
                for h in range(4):
                    r = slice(64 * (h % 2), 64 * (h % 2) + 64)
                    pe.matmul(psum[:, h, 0:P], qkT[r, h // 2, 0:P], qkT[r, 2 + h // 2, 0:P], start=True, stop=True)
                    ins = pe.matmul(psum[:, h, P:3 * P], qkT[r, h // 2, P:S], qkT[r, 2 + h // 2, :], start=True, stop=True)
                    ins.then_inc(sem["scores"], 1)
                for h in range(4):
                    event("probs")
                    for i in range(3):
                        ins = pe.transpose(TB[:, i * P:(i + 1) * P], prob[:, i * P:(i + 1) * P], ident[:])
                    ins.then_inc(sem["pT_psum"], 1)
                    event("pT")
                    v = vv[:, :, h * 64:h * 64 + 64]
                    pe.matmul(MB[:, h * 64:h * 64 + 64], pT[:, 0:P], v[:, 0], start=True, stop=True)
                    pe.matmul(MB[:, 256 + h * 64:320 + h * 64], pT[:, P:2 * P], v[:, 0], start=True, stop=False)
                    ins = pe.matmul(MB[:, 256 + h * 64:320 + h * 64], pT[:, 2 * P:3 * P], v[:, 1], start=False, stop=True)
                    ins.then_inc(sem["pv_psum"], 1)
                to_x()
                for c in range(2):
                    split_in()
                    plain_tok([psum[:, 2 * t + c, :] for t in range(NT)], GC)

            event("silu_c")
            with seen.loop(pe, "pe_layer", DEPTH):
                to_x(); ffn("pe_ff1", N1, True)
                to_x(); mixer()
                to_x(); ffn("pe_ff2", N1, True)
            if stop != "first":
                tok = [[psum[:, b + t, 0:256] for t in range(NT)] for b in (4, 6)]
                to_x()
                for o in tok:
                    split_in(); plain_tok(o, 256)
                to_x()
                event("ctx_out")
                for b in (4, 6, 0):
                    split_in(); plain_tok([psum[:, b + t, :] for t in range(NT)], GC)
                event("roped2")
                for y in range(2):
                    for g in range(4):
                        for t in range(NT):
                            a = 4 * y + g
                            src = qq[:, t, a * P:(a + 1) * P]
                            ins = pe.transpose(psum[:, a // 2, (a % 2) * S + t * P:(a % 2) * S + (t + 1) * P], src, ident[:])
                for y in range(2):
                    for t in range(4):
                        ins = pe.transpose(psum[:, 4 + y, t * P:(t + 1) * P], kk[:, t, y * P:(y + 1) * P], ident[:])
                ins.then_inc(sem["qk2_psum"], 1)
                event("qT"); event("kT")
                TILES = [(y, t, v, g) for y in range(2) for t in range(NT) for v in range(2) for g in range(4)]

                def scores(i):
                    y, t, v, g = TILES[i]
                    r = slice(64 * v, 64 * v + 64)
                    pe.matmul(psum[:, i % 2, :], qT[r, 4 * y + g, t * P:(t + 1) * P], kT[r, y, :],
                              start=True, stop=True).then_inc(sem["scores2"], 1)

                scores(0); scores(1)
                for i, (y, t, v, g) in enumerate(TILES):
                    event("probs2")
                    for j in range(4):
                        ins = pe.transpose(psum[:, 2 + i % 2, j * P:(j + 1) * P], prob2[:, i % 2, j * P:(j + 1) * P], ident[:])
                    ins.then_inc(sem["pT2_psum"], 1)
                    if i + 2 < len(TILES):
                        scores(i + 2)
                    event("pT2")
                    h = 4 * v + g
                    for j in range(4):
                        ins = pe.matmul(psum[:, 4 + 2 * y + t, h * 64:(h + 1) * 64], pT2[:, i % 2, j * P:(j + 1) * P],
                                        vk[:, j, y * P + v * 64:y * P + v * 64 + 64], start=j == 0, stop=j == 3)
                    if i % 16 == 15:
                        ins.then_inc(sem["pv2_psum"], 1)
                to_x()
                for c in range(2):
                    split_in(); plain_tok([psum[:, 2 * t + c, :] for t in range(NT)], GC)
                to_x(); ffn("pe_ffn", N1)
                to_x()
                for c, b in enumerate((4, 2, 0, 6, 4, 2)):
                    if c >= 4:
                        event("conv_free")
                    split_in(); plain_tr(halves((b, b + 1)), GC)
                pe.wait_ge(sem["x_lo"], seen("x_lo", 2))
                for c in range(2):
                    split_in(); plain_tok([psum[:, 2 * t + c, :] for t in range(NT)], GC)
                to_x()
                split_in(); plain_tok([MB[:, t * NE:(t + 1) * NE] for t in range(NT)], NE)
                ffn("pe_moe", NM)

        @block.scalar
        def _(act):
            seen = Seen()
            seen.count.update({"a_done": 2, "y_done": 1})
            par = [0]

            def go(*a, **k):
                return nc.scalar.activation(*a, **k)

            def link(ins):
                ins.then_inc(sem["act_step"], 1)
                act.wait_ge(sem["act_step"], seen("act_step"))

            def event(name):
                act.wait_ge(sem[name], seen(name))

            def unit():
                act.wait_ge(sem["a_done"], seen("a_done"))

            def unit_skip():
                seen("a_done")

            def split_a(n=PIECE):
                act.wait_ge(sem["a_done"], seen("a_free"))
                for j in range(2):
                    act.wait_ge(sem[f"raw{j}"], seen(f"raw{j}", 16))
                    go(a_hi[:, par[0], j, 0:n], raw[:, j, 0:n], ACT.Copy).then_inc(sem["hi"], 1)
                par[0] ^= 1

            def split_d():
                act.wait_ge(sem["d_done"], seen("d_free"))
                act.wait_ge(sem["raw2"], seen("raw2", 16))
                go(d_hi[:], raw[:, 2, :], ACT.Copy).then_inc(sem["hi"], 1)

            def hidden_hi():
                event("t_psum")
                go(ht_hi[:].rearrange("p b s -> p (b s)"), TB, ACT.Copy).then_inc(sem["ht_hi"], 1)

            def period(u, ahead):
                if u:
                    hidden_hi()
                if ahead:
                    split_a(ahead)
                event("gu0")
                go(sg[:, 0, :], psum[:, 4, 0:FC], ACT.Silu).then_inc(sem["sg0"], 1)
                if u:
                    split_d()
                unit()
                go(sg[:, 1, :], psum[:, 5, 0:FC], ACT.Silu).then_inc(sem["sg1"], 1)

            def ffn(label, n, nxt):
                period(0, PIECE)
                with seen.loop(act, label, (n - 2) // 2):
                    for _ in range(2):
                        period(1, PIECE)
                if n % 2:
                    period(1, PIECE)
                period(1, nxt)
                hidden_hi()
                split_d()

            def norm_rows(src):
                for t in range(NT):
                    ins = go(xn[:, t, :], src(t), ACT.Square, accum_out=st[:, 0, t:t + 1])
                ins.then_inc(sem["ssq"], 1)
                event("ms")
                go(st[:, 1, :], st[:, 0, :], ACT.Sqrt).then_inc(sem["root"], 1)

            def pre_norm(src=lambda t: res[:, t, :], wait="res_ready"):
                if wait:
                    event(wait)
                norm_rows(src)

            def post_norm(wait):
                wait()
                norm_rows(lambda t: Y[:, t, :])

            def y_done(n=1):
                act.wait_ge(sem["d_done"], seen("y_done", n))

            def to_x():
                event("scale")
                for half in range(2):
                    event("xt_psum")
                    for k in range(4 * half, 4 * half + 4):
                        ins = go(mod[:, k, :], psum[:, k // 2, (k % 2) * S:(k % 2) * S + S], ACT.Identity,
                                 bias=gcol[:, 1, k:k + 1], scale=gcol[:, 3, k:k + 1])
                    link(ins)
                    go(x_hi[:, 4 * half:4 * half + 4, :], mod[:, 4 * half:4 * half + 4, :], ACT.Copy).then_inc(sem["x_hi"], 1)

            def mixer():
                def conv_out(name, c0):
                    event(f"taps_{name}")
                    for c in range(c0, c0 + 4):
                        ins = go(cT[:, c, :], cT[:, c, :], ACT.Silu, bias=convb[:, c:c + 1])
                    ins.then_inc(sem[f"conv_{name}"], 1)

                split_a(4 * GC)
                unit()
                act.wait_ge(sem["mix_par"], seen("mix_par", 16 * 9))
                tmp = dts[:, 2 * S:3 * S]
                link(go(tmp, MB[0:8, 0:S], ACT.Abs, bias=dtb))
                link(go(tmp, tmp, ACT.Exp, scale=-1.0))
                link(go(tmp, tmp, ACT.Ln, bias=1.0))
                go(dts[:, 3 * S:3 * S + 1], alog, ACT.Exp).then_inc(sem["soft"], 1)
                split_a(4 * GC)
                unit()
                go(xT[:, 4:8, CPAD:CPAD + S], psum[:, 4:6, :].rearrange("p b (h s) -> p (b h) s", s=S), ACT.Copy).then_inc(sem["bc_out"], 1)
                split_a(4 * GC)
                unit()
                go(xT[:, 0:4, CPAD:CPAD + S], psum[:, 0:2, :].rearrange("p b (h s) -> p (b h) s", s=S), ACT.Copy).then_inc(sem["xs_out"], 1)
                split_a(4 * GC)
                unit()
                go(qk[:, :, 0:256], psum[:, 3, :].rearrange("p (t n) -> p t n", t=NT), ACT.Copy)
                go(uw[0][:, :, PAD:PAD + S], psum[:, 2, :].rearrange("p (c s) -> p c s", s=S), ACT.Copy).then_inc(sem["uq_out"], 1)
                conv_out("bc", 4)
                split_a(4 * GC)
                unit()
                kv = psum[:, 4:6, :]
                go(vv, kv[:, :, 256:512], ACT.Copy)
                go(qk[:, :, 256:512], kv[:, :, 0:256], ACT.Copy).then_inc(sem["kv_out"], 1)
                conv_out("xs", 0)
                unit()
                go(zs, psum[:, 0:2, :], ACT.Silu).then_inc(sem["z_out"], 1)
                for j in range(2):
                    seen(f"raw{j}", 32)
                split_a(4 * GC)
                split_a(4 * GC)
                event("pool_psum")
                go(xn[:, :, 512:768], MB.rearrange("p (t n) -> p t n", t=NT), ACT.Copy).then_inc(sem["pool_out"], 1)
                for g in range(2):
                    event("arg")
                    go(arg, arg, ACT.Exp).then_inc(sem["decay"], 1)
                event("gated")
                for t in range(NT):
                    ins = go(xsd[:, t, :], xdt[:, t, :], ACT.Square, accum_out=st[:, 0, t:t + 1])
                ins.then_inc(sem["ssq"], 1)
                event("ms")
                go(st[:, 1, :], st[:, 0, :], ACT.Sqrt).then_inc(sem["root"], 1)
                event("qk_psum")
                act.wait_ge(sem["ctx_stored"], seen("ctx_stored", 16))
                go(qkT, psum[:, 2:4, :].rearrange("p b (h s) -> p (b h) s", s=S), ACT.Copy).then_inc(sem["qkT"], 1)
                for h in range(4):
                    event("amax")
                    for t in range(NT):
                        ap = prob[:, 0:P] if t == 0 else prob[:, P:3 * P]
                        ins = go(ap, ap, ACT.Exp, bias=qstat[:, 0, h, t:t + 1], accum_out=qstat[:, 1, h, t:t + 1])
                    ins.then_inc(sem["probs"], 1)
                    event("pT_psum")
                    go(pT, TB[:, 0:384], ACT.Copy).then_inc(sem["pT"], 1)
                to_x()

            event("consts_in")
            go(cs[:].rearrange("p k r -> p r k"), small[:, 128:144].rearrange("p (r k) -> p r k", k=KD), ACT.Silu).then_inc(sem["silu_c"], 1)
            split_a()
            with seen.loop(act, "act_layer", DEPTH):
                pre_norm(); to_x(); ffn("act_ff1", N1, 4 * 8)
                post_norm(lambda: y_done(N1))
                pre_norm(); to_x(); mixer()
                unit()
                split_a()
                unit()
                post_norm(lambda: None)
                pre_norm(); to_x(); ffn("act_ff2", N1, None)
                split_a()
                post_norm(lambda: y_done(N1))
            if stop != "first":
                act.wait_ge(sem["att_in"], seen("att_in", 16 * 9))
                pre_norm(lambda t: ctxr[:, t, :], None)
                to_x()
                split_a()
                for y in range(2):
                    unit()
                    go(kk[:, 0:2, y * P:(y + 1) * P], psum[:, 4 + 2 * y:6 + 2 * y, 0:P], ACT.Copy)
                    ins = go(vk[:, 0:2, y * P:(y + 1) * P], psum[:, 4 + 2 * y:6 + 2 * y, P:2 * P], ACT.Copy)
                    split_a()
                go(cs[:, 0, 0:1], epsc[:], ACT.Copy).then_inc(sem["ctx_out"], 1)
                pre_norm(); to_x()
                unit()
                q5 = qq.rearrange("p t (y g v d) -> p t y v g d", y=2, v=2, d=64)

                def heads(ap):
                    return ap.rearrange("p (g d) -> p g d", d=64)
                for t in range(NT):
                    for v in range(2):
                        go(q5[:, t, 0, v], heads(psum[:, 4 + t, v * 256:(v + 1) * 256]), ACT.Copy)
                split_a()
                unit()
                go(kk[:, 2:4, 0:P], psum[:, 6:8, 0:P], ACT.Copy)
                go(vk[:, 2:4, 0:P], psum[:, 6:8, P:2 * P], ACT.Copy)
                for t in range(NT):
                    go(q5[:, t, 1, 0], heads(psum[:, 6 + t, 256:512]), ACT.Copy)
                split_a()
                unit()
                for t in range(NT):
                    go(q5[:, t, 1, 1], heads(psum[:, t, 0:256]), ACT.Copy)
                go(kk[:, 2:4, P:2 * P], psum[:, 0:2, 256:384], ACT.Copy)
                link(go(vk[:, 2:4, P:2 * P], psum[:, 0:2, 384:512], ACT.Copy))
                go(mod[:].rearrange("p k s -> p (k s)"), qq.rearrange("p t n -> p (t n)"), ACT.Square)
                go(xn[:, 0, :], kk.rearrange("p t n -> p (t n)"), ACT.Square).then_inc(sem["squares"], 1)
                event("head_ms")
                go(rms, rms, ACT.Sqrt).then_inc(sem["head_root"], 1)
                split_a()
                event("qk2_psum")
                go(qT, psum[:, 0:4, :].rearrange("p b (h s) -> p (b h) s", s=S), ACT.Copy).then_inc(sem["qT"], 1)
                tiles = [y * 16 + t * 8 + v * 4 + g for y in range(2) for t in range(NT) for v in range(2) for g in range(4)]

                def exps(i):
                    event("amax2")
                    n = tiles[i]
                    go(prob2[:, i % 2, :], psum[:, i % 2, :], ACT.Exp, scale=64.0 ** -0.5, bias=sm2[:, 1, n:n + 1],
                       accum_out=sm2[:, 2, n:n + 1]).then_inc(sem["probs2"], 1)

                exps(0)
                for i in range(32):
                    if i < 31:
                        exps(i + 1)
                    event("pT2_psum")
                    go(pT2[:, i % 2, :], psum[:, 2 + i % 2, :], ACT.Copy).then_inc(sem["pT2"], 1)
                event("sink_arg")
                go(sm2[:, 0, 16:32], sm2[:, 0, 16:32], ACT.Exp).then_inc(sem["sink_exp"], 1)
                to_x()
                unit()
                split_a()
                unit()
                pre_norm(); to_x(); ffn("act_ffn", N1, PIECE)
                pre_norm(); to_x()
                for half in range(2):
                    split_a(); unit()
                    go(cg, psum[:, 4 + 2 * half:6 + 2 * half, :].rearrange("p b (h s) -> p (b h) s", s=S), ACT.Copy).then_inc(sem["cg"], 1)
                    split_a(); unit()
                    split_a(); unit()
                    if half == 0:
                        event("cg_used")
                event("mixed_conv")
                for half in range(2):
                    s4 = slice(4 * half, 4 * half + 4)
                    go(x_hi[:, s4, :], mod[:, s4, :], ACT.Copy).then_inc(sem["x_hi"], 1)
                split_a()
                unit()
                split_a(4 * NE)
                unit()
                pre_norm(); to_x()
                split_a()
                unit()
                event("top2")
                go(lg[:, 6, :, 0:1], lg[:, 6, :, 0:1], ACT.Exp).then_inc(sem["top2_exp"], 1)
                ffn("act_moe", NM, None)

        @block.vector
        def _(dve):
            seen = Seen()
            seen.count.update({"a_done": 2, "y_done": 1})
            par = [0]
            dve.sem_inc(sem["ada_row"], 2)
            dve.sem_inc(sem["x_lo"], 2)
            for q in range(2):
                dve.sem_inc(sem[f"ada_acc{q}"], 1)
            for j in range(3):
                dve.sem_inc(sem[f"split{j}"], 1)
            V = nc.vector

            def link(ins):
                ins.then_inc(sem["dve_step"], 1)
                dve.wait_ge(sem["dve_step"], seen("dve_step"))

            def event(name, n=1):
                dve.wait_ge(sem[name], seen(name, n))

            def unit():
                dve.wait_ge(sem["a_done"], seen("a_done"))

            def unit_skip(n=1):
                seen("a_done", n)

            def split_a(n=PIECE):
                for j in range(2):
                    event("hi")
                    V.tensor_tensor(a_lo[:, par[0], j, 0:n], raw[:, j, 0:n], f(a_hi[:, par[0], j, 0:n]),
                                    ALU.subtract).then_inc(sem[f"split{j}"], 1)
                par[0] ^= 1

            def split_d():
                event("hi")
                V.tensor_tensor(d_lo[:], raw[:, 2, :], f(d_hi[:]), ALU.subtract).then_inc(sem["split2"], 1)

            def hidden_lo():
                event("ht_hi")
                V.tensor_tensor(ht_lo[:].rearrange("p b s -> p (b s)"), TB, f(ht_hi[:]).rearrange("p b s -> p (b s)"),
                                ALU.subtract).then_inc(sem["ht"], 1)

            def hidden(t, scale):
                event(f"sg{t}")
                up = psum[:, 4 + t, FC:2 * FC]
                if scale is None:
                    V.tensor_tensor(hb[:, t, :], sg[:, t, :], up, ALU.mult).then_inc(sem[f"h{t}"], 1)
                else:
                    V.scalar_tensor_tensor(hb[:, t, :], sg[:, t, :], scale(t), up, ALU.mult, ALU.mult).then_inc(sem[f"h{t}"], 1)

            def period(u, ahead, scale=None, ada=None):
                if u:
                    hidden_lo()
                if ahead:
                    split_a(ahead)
                hidden(0, scale)
                if u:
                    split_d()
                if ada is not None:
                    event(f"ada_in{ada}", 16)
                    for k in range(KD):
                        w, a = adaw[:, ada, k, :], adaa[:, ada, :]
                        if k == 0:
                            ins = V.tensor_scalar(a, w, cs[:, k, 1:2], None, ALU.mult)
                        else:
                            ins = V.scalar_tensor_tensor(a, w, cs[:, k, 1:2], a, ALU.mult, ALU.add)
                        if k < KD - 1:
                            link(ins)
                    ins.then_inc(sem[f"ada_acc{ada}"], 1)
                hidden(1, scale)
                if ada is not None:
                    event("ada_sum")
                    event(f"ada_bias{ada}", 16)
                    V.tensor_tensor(adar[:, ada, :], MB[0:1, 0:AC], adar[:, ada, :], ALU.add).then_inc(sem["ada_row"], 1)

            def ffn(label, n, nxt, scale=None, ada=False):
                s = scale or (lambda u: None)
                period(0, PIECE, s(0))
                with seen.loop(dve, label, (n - 2) // 2) as i:
                    for q in range(2):
                        period(1, PIECE, s(i * 2 + (1 + q)), q if ada else None)
                if n % 2:
                    period(1, PIECE, s(n - 2))
                period(1, nxt, s(n - 1))
                hidden_lo()
                split_d()
                unit_skip(n)

            def roots(width):
                event("ssq")
                V.tensor_scalar(st[:, 0, :], st[:, 0, :], 1.0 / width, EPS, ALU.mult, ALU.add).then_inc(sem["ms"], 1)
                event("root")
                link(V.reciprocal(st[:, 1, :], st[:, 1, :]))

            def pre_norm(src=lambda t: res[:, t, :]):
                roots(D)
                for t in range(NT):
                    ins = V.tensor_scalar(xn[:, t, :], src(t), st[:, 1, t:t + 1], None, ALU.mult)
                ins.then_inc(sem["xn_ready"], 1)

            def to_x(n_gain=1, extra=None):
                event("gain", 16 * n_gain)
                if extra:
                    event(extra)
                V.scalar_tensor_tensor(gcol[:, 3, :], gcol[:, 2, :], 1.0, gcol[:, 0, :], ALU.add, ALU.mult).then_inc(sem["scale"], 1)
                for half in range(2):
                    event("x_hi")
                    s = slice(4 * half, 4 * half + 4)
                    V.tensor_tensor(x_lo[:, s, :], mod[:, s, :], f(x_hi[:, s, :]), ALU.subtract).then_inc(sem["x_lo"], 1)

            def y_done(n=1):
                dve.wait_ge(sem["d_done"], seen("y_done", n))

            def post_norm(wait, factor, normed=True):
                wait()
                if normed:
                    roots(D)
                    if factor != 1.0:
                        link(V.tensor_scalar(st[:, 1, :], st[:, 1, :], factor, None, ALU.mult))
                event("gain_row", 16)
                for t in range(NT):
                    if normed:
                        ins = V.scalar_tensor_tensor(xn[:, t, :], Y[:, t, :], st[:, 1, t:t + 1], gbc[:], ALU.mult, ALU.mult)
                    else:
                        ins = V.tensor_tensor(xn[:, t, :], Y[:, t, :], gbc[:], ALU.mult)
                link(ins)
                for t in range(NT):
                    ins = V.tensor_tensor(res[:, t, :], res[:, t, :], xn[:, t, :], ALU.add)
                ins.then_inc(sem["res_ready"], 1)

            def mixer():
                split_a(4 * GC)
                event("mix_par", 16 * 9)
                event("soft")
                a, b = dts[:, 0:S], dts[:, S:2 * S]
                link(V.tensor_scalar(a, MB[0:8, 0:S], dtb, 0.0, ALU.add, ALU.max))
                link(V.tensor_tensor(a, a, dts[:, 2 * S:3 * S], ALU.add))
                link(V.tensor_scalar(dts[:, 2 * S:3 * S], a, dts[:, 3 * S:3 * S + 1], -1.0, ALU.mult, ALU.mult))
                link(V.memset(dts[:, 3 * S:4 * S], 1.0))
                V.tensor_tensor_scan(b, dts[:, 3 * S:4 * S], dts[:, 2 * S:3 * S], 0.0, ALU.mult, ALU.add).then_inc(sem["acs_rows"], 1)
                split_a(4 * GC)
                link(V.memset(xT[:, :, 0:CPAD], 0.0))
                event("bc_out")

                def taps(name, c0):
                    for j in range(4):
                        for c in range(c0, c0 + 4):
                            src = xT[:, c, j:j + S]
                            w = convw[:, j, c:c + 1]
                            if j == 0:
                                ins = V.tensor_scalar(cT[:, c, :], src, w, None, ALU.mult)
                            else:
                                ins = V.scalar_tensor_tensor(cT[:, c, :], src, w, cT[:, c, :], ALU.mult, ALU.add)
                        if j < 3:
                            link(ins)
                    ins.then_inc(sem[f"taps_{name}"], 1)
                taps("bc", 4)
                split_a(4 * GC)
                event("xs_out")
                taps("xs", 0)
                split_a(4 * GC)
                split_a(4 * GC)
                split_a(4 * GC)
                unit_skip(6)
                event("ctx_bias", 16)
                event("ctx_used1", 2)
                V.tensor_tensor(crow.rearrange("p (c n) -> p c n", n=GC), psum[0:1, 2:4, :],
                                crow.rearrange("p (c n) -> p c n", n=GC), ALU.add).then_inc(sem["ctx_row"], 1)
                event("dt_psum")
                TB3 = TB[:, 0:32].rearrange("p (i t h) -> p i t h", i=2, t=NT)
                V.tensor_copy(dtc, TB3[:, 0])
                V.tensor_scalar(nacs, TB3[:, 1], -1.0, None, ALU.mult).then_inc(sem["dtc"], 1)
                split_a(4 * GC)
                event("kv_out")
                x = qk.rearrange("p t (h d) -> p t h d", d=64)
                r = area(7712, 4, NT, 64).rearrange("p i t (h d) -> p i t h d", d=8)
                for i, (part, trig) in enumerate(((0, 0), (1, 1), (1, 0), (0, 1))):
                    tb = rope[:, :, 8 * trig:8 * trig + 8].unsqueeze(2).broadcast_to([P, NT, 8, 8])
                    for t in range(NT):
                        ins = V.tensor_tensor(r[:, i, t], x[:, t, :, 8 * part:8 * part + 8], tb[:, t], ALU.mult)
                link(ins)
                for t in range(NT):
                    V.tensor_tensor(x[:, t, :, 0:8], r[:, 0, t], r[:, 1, t], ALU.subtract)
                    ins = V.tensor_tensor(x[:, t, :, 8:16], r[:, 2, t], r[:, 3, t], ALU.add)
                ins.then_inc(sem["roped"], 1)
                for g in range(2):
                    event("acs_psum")
                    if g:
                        event("ssd_psum")
                    for h in range(4):
                        ps = psum[:, 2 + h // 2, (h % 2) * S:(h % 2) * S + S]
                        V.scalar_tensor_tensor(arg[:, h, 0:S], ps, nacs[:, 0, 4 * g + h:4 * g + h + 1], cmask[:, 0:S], ALU.add, ALU.add)
                        ins = V.scalar_tensor_tensor(arg[:, h, S:S + P], ps[:, P:S], nacs[:, 1, 4 * g + h:4 * g + h + 1],
                                                     cmask[:, 0:P], ALU.add, ALU.add)
                    ins.then_inc(sem["arg"], 1)
                    if g == 0:
                        event("xs_psum")
                        for t in range(NT):
                            xs = psum[:, t, :].rearrange("p (h d) -> p h d", d=HP)
                            for dst, col in ((xdt, dtc[:, t, :]), (xsd, dskip)):
                                ins = V.tensor_tensor(dst[:, t, :].rearrange("p (h d) -> p h d", d=HP), xs,
                                                      col.unsqueeze(2).broadcast_to([P, HEADS, HP]), ALU.mult)
                        ins.then_inc(sem["xdt"], 1)
                        event("cb_psum")
                    event("decay")
                    cb = (TB, MB)[g][:, 0:384].unsqueeze(1).broadcast_to([P, 4, 384])
                    V.tensor_tensor(arg, arg, cb, ALU.mult).then_inc(sem["seg"], 1)
                event("ssd_psum")
                for t in range(NT):
                    ins = V.tensor_tensor(xdt[:, t, :], psum[:, 4 + t, :], xsd[:, t, :], ALU.add)
                link(ins)
                for t in range(NT):
                    ins = V.tensor_tensor(xdt[:, t, :], xdt[:, t, :], zs[:, t, :], ALU.mult)
                ins.then_inc(sem["gated"], 1)
                roots(SSD_IN)
                for t in range(NT):
                    V.tensor_scalar(xn[:, t, 0:SSD_IN], xdt[:, t, :], st[:, 1, t:t + 1], None, ALU.mult)
                scale = 64.0 ** -0.5
                for h in range(4):
                    event("scores")
                    if h:
                        event("pT_psum")
                    link(V.scalar_tensor_tensor(prob, psum[:, h, 0:384], scale, qmask[:], ALU.mult, ALU.add))
                    V.reduce_max(qstat[:, 0, h, 0:1], prob[:, 0:P], AX)
                    link(V.reduce_max(qstat[:, 0, h, 1:2], prob[:, P:3 * P], AX))
                    V.tensor_scalar(qstat[:, 0, h, :], qstat[:, 0, h, :], -1.0, None, ALU.mult).then_inc(sem["amax"], 1)
                event("pT_psum")
                event("probs", 4)
                link(V.reciprocal(qstat[:, 2], qstat[:, 1]))
                event("pv_psum", 4)
                for t in range(NT):
                    ins = V.tensor_tensor(xn[:, t, 768:D].rearrange("p (h d) -> p h d", d=64),
                                          MB[:, t * 256:(t + 1) * 256].rearrange("p (h d) -> p h d", d=64),
                                          qstat[:, 2, :, t:t + 1].broadcast_to([P, 4, 64]), ALU.mult)
                event("pool_out")
                V.tensor_copy(small[:, 120:121], epsc[:]).then_inc(sem["xn_ready"], 1)
                to_x(2, "gain_one")

            event("consts_in")
            event("silu_c")
            V.tensor_copy(small[:, 120:121], epsc[:]).then_inc(sem["res_ready"], 1)
            split_a()
            with seen.loop(dve, "dve_layer", DEPTH):
                pre_norm(); to_x(); ffn("dve_ff1", N1, 4 * 8, ada=True)
                post_norm(lambda: y_done(N1), 0.5)
                pre_norm(); to_x(); mixer()
                unit_skip()
                split_a()
                unit()
                post_norm(lambda: None, 1.0)
                pre_norm(); to_x(); ffn("dve_ff2", N1, None, ada=True)
                split_a()
                post_norm(lambda: y_done(N1), 0.5)
            if stop == "first":
                V.tensor_copy(small[:, 121:122], epsc[:]).then_inc(sem["final"], 1)
            else:
                event("att_in", 16 * 9)
                pre_norm(lambda t: ctxr[:, t, :])
                to_x(3)
                split_a()
                split_a()
                split_a()
                pre_norm(); to_x(3)
                split_a(); split_a()
                unit_skip(5)
                event("squares")
                V.reduce_sum(rms[:, 0:32], mod[:].rearrange("p k (h d) -> p (k h) d", d=64), AX)
                link(V.reduce_sum(rms[:, 32:48], xn[:, 0, :].rearrange("p (h d) -> p h d", d=64), AX))
                V.tensor_scalar(rms, rms, 1.0 / 64, EPS, ALU.mult, ALU.add).then_inc(sem["head_ms"], 1)
                event("head_root")
                link(V.reciprocal(rms, rms))
                q64 = qq.rearrange("p t (h d) -> p (t h) d", d=64)
                k64 = kk.rearrange("p t (h d) -> p (t h) d", d=64)
                V.tensor_tensor(q64, q64, rms[:, 0:32].unsqueeze(2).broadcast_to([P, 32, 64]), ALU.mult)
                link(V.tensor_tensor(k64, k64, rms[:, 32:48].unsqueeze(2).broadcast_to([P, 16, 64]), ALU.mult))
                for y in range(2):
                    for t in range(NT):
                        v = qq[:, t, y * 512:(y + 1) * 512].rearrange("p (h d) -> p h d", d=64)
                        V.tensor_tensor(v, v, qkg[:, y:y + 1, :].broadcast_to([P, 8, 64]), ALU.mult)
                    for t in range(4):
                        v = kk[:, t, y * P:(y + 1) * P].rearrange("p (h d) -> p h d", d=64)
                        ins = V.tensor_tensor(v, v, qkg[:, 2 + y:3 + y, :].broadcast_to([P, 2, 64]), ALU.mult)
                link(ins)
                tmp = mod[:].rearrange("p k s -> p (k s)").rearrange("p (i h d) -> p i h d", i=4, d=32)
                for t in range(NT):
                    for x, nh in ((qq[:, t, :], 16), (kk[:, 2 + t, :], 4)):
                        x = x.rearrange("p (h d two) -> p h d two", d=32, two=2)
                        for i, (side, trig) in enumerate(((0, 0), (1, 1), (0, 1), (1, 0))):
                            tb = rope2[:, t, 32 * trig:32 * trig + 32].unsqueeze(1).broadcast_to([P, nh, 32])
                            ins = V.tensor_tensor(tmp[:, i, 0:nh], x[:, :, :, side], tb, ALU.mult)
                        link(ins)
                        V.tensor_tensor(x[:, :, :, 0], tmp[:, 0, 0:nh], tmp[:, 1, 0:nh], ALU.subtract)
                        link(V.tensor_tensor(x[:, :, :, 1], tmp[:, 2, 0:nh], tmp[:, 3, 0:nh], ALU.add))
                V.tensor_scalar(nsink, nsink, -1.0, None, ALU.mult).then_inc(sem["roped2"], 1)
                split_a()
                event("qk2_psum")
                V.tensor_copy(kT, psum[:, 4:6, :]).then_inc(sem["kT"], 1)
                i = 0
                for y in range(2):
                    for t in range(NT):
                        for h in range(8):
                            n = y * 16 + t * 8 + h
                            event("scores2")
                            if y:
                                link(V.tensor_tensor(psum[:, i % 2, S:2 * S], psum[:, i % 2, S:2 * S], band[:, t, :], ALU.add))
                            link(V.reduce_max(sm2[:, 0, n:n + 1], psum[:, i % 2, :], AX))
                            if y:
                                ins = V.tensor_scalar(sm2[:, 1, n:n + 1], sm2[:, 0, n:n + 1], -(64.0 ** -0.5), nsink[:, h:h + 1], ALU.mult, ALU.min)
                            else:
                                ins = V.tensor_scalar(sm2[:, 1, n:n + 1], sm2[:, 0, n:n + 1], -(64.0 ** -0.5), None, ALU.mult)
                            ins.then_inc(sem["amax2"], 1)
                            i += 1
                event("probs2", 32)
                for t in range(NT):
                    s = slice(16 + 8 * t, 24 + 8 * t)
                    ins = V.tensor_tensor(sm2[:, 0, s], sm2[:, 1, s], nsink, ALU.subtract)
                ins.then_inc(sem["sink_arg"], 1)
                event("sink_exp")
                link(V.tensor_tensor(sm2[:, 2, 16:32], sm2[:, 2, 16:32], sm2[:, 0, 16:32], ALU.add))
                link(V.reciprocal(sm2[:, 3, :], sm2[:, 2, :]))
                event("pv2_psum", 2)
                for y in range(2):
                    for t in range(NT):
                        n = 16 * y + 8 * t
                        ins = V.tensor_tensor(xn[:, t, y * 512:(y + 1) * 512].rearrange("p (h d) -> p h d", d=64),
                                              psum[:, 4 + 2 * y + t, :].rearrange("p (h d) -> p h d", d=64),
                                              sm2[:, 3, n:n + 8].unsqueeze(2).broadcast_to([P, 8, 64]), ALU.mult)
                ins.then_inc(sem["xn_ready"], 1)
                to_x(0, "gain_one")
                unit_skip()
                split_a()
                unit()
                post_norm(lambda: None, 1.0, False)
                pre_norm(); to_x(3); ffn("dve_ffn", N1, PIECE)
                post_norm(lambda: y_done(N1), 1.0, False)
                pre_norm(); to_x(3)
                V.memset(zT[:, :, 0:1], 0.0)
                V.memset(zT[:, :, S + 1:S + 2], 0.0)
                banks = ((4, 2, 0), (6, 4, 2))

                def blocks4(b):
                    return psum[:, b:b + 2, :].rearrange("p b (h s) -> p (b h) s", s=S)
                for half in range(2):
                    split_a()
                    unit()
                    event("cg")
                    if half == 0:
                        V.tensor_copy(small[:, 241:242], epsc[:]).then_inc(sem["conv_free"], 1)
                    split_a()
                    unit()
                    ins = V.tensor_tensor(zT[:, :, 1:S + 1], cg, blocks4(banks[half][1]), ALU.mult)
                    link(ins)
                    if half == 0:
                        V.tensor_copy(small[:, 242:243], epsc[:]).then_inc(sem["conv_free"], 1)
                        V.tensor_copy(small[:, 243:244], epsc[:]).then_inc(sem["cg_used"], 1)
                    split_a()
                    for j in range(3):
                        for c in range(4):
                            w = convw2[:, j, 4 * half + c:4 * half + c + 1]
                            if j == 0:
                                ins = V.tensor_scalar(acc[:, c, :], zT[:, c, 0:S], w, None, ALU.mult)
                            else:
                                ins = V.scalar_tensor_tensor(acc[:, c, :], zT[:, c, j:j + S], w, acc[:, c, :], ALU.mult, ALU.add)
                        link(ins)
                    unit()
                    ins = V.tensor_tensor(mod[:, 4 * half:4 * half + 4, :], acc, blocks4(banks[half][2]), ALU.mult)
                    if half == 1:
                        ins.then_inc(sem["mixed_conv"], 1)
                for half in range(2):
                    event("x_hi")
                    s4 = slice(4 * half, 4 * half + 4)
                    V.tensor_tensor(x_lo[:, s4, :], mod[:, s4, :], f(x_hi[:, s4, :]), ALU.subtract).then_inc(sem["x_lo"], 1)
                split_a()
                unit_skip()
                split_a(4 * NE)
                unit()
                post_norm(lambda: None, 1.0, False)
                pre_norm(); to_x(3)
                split_a()
                unit()
                L, e1, c1, f1, L2, f2, m, g8 = (lg[:, i] for i in range(8))
                link(V.tensor_copy(L, MB[:, 0:2 * NE].rearrange("p (t e) -> p t e", e=NE)))
                ones8 = small[:, 244:252]
                link(V.memset(ones8, 1.0))

                def first_max(src, dst, col):
                    link(V.reduce_max(m[:, :, col:col + 1], src, AX))
                    for t in range(NT):
                        ins = V.tensor_scalar(e1[:, t, :], src[:, t, :], m[:, t, col:col + 1], None, ALU.is_equal)
                    link(ins)
                    for t in range(NT):
                        ins = V.tensor_tensor_scan(c1[:, t, :], ones8, e1[:, t, :], 0.0, ALU.mult, ALU.add)
                    link(ins)
                    link(V.scalar_tensor_tensor(dst, c1, 1.0, e1, ALU.is_equal, ALU.mult))

                first_max(L, f1, 1)
                link(V.scalar_tensor_tensor(L2, f1, NEG, L, ALU.mult, ALU.add))
                first_max(L2, f2, 2)
                V.tensor_tensor(m[:, :, 0:1], m[:, :, 2:3], m[:, :, 1:2], ALU.subtract).then_inc(sem["top2"], 1)
                event("top2_exp")
                link(V.tensor_scalar(m[:, :, 3:4], m[:, :, 0:1], 1.0, None, ALU.add))
                link(V.reciprocal(m[:, :, 3:4], m[:, :, 3:4]))
                link(V.tensor_tensor(m[:, :, 4:5], m[:, :, 0:1], m[:, :, 3:4], ALU.mult))
                for t in range(NT):
                    ins = V.tensor_scalar(g8[:, t, :], f1[:, t, :], m[:, t, 3:4], None, ALU.mult)
                link(ins)
                for t in range(NT):
                    ins = V.scalar_tensor_tensor(g8[:, t, :], f2[:, t, :], m[:, t, 4:5], g8[:, t, :], ALU.mult, ALU.add)
                link(ins)
                for t in range(NT):
                    ins = V.tensor_copy(gexp[:, t, :].rearrange("p (e c) -> p e c", c=NX),
                                        g8[:, t, :].unsqueeze(2).broadcast_to([P, NE, NX]))
                link(ins)
                ffn("dve_moe", NM, None, lambda u: (lambda t: gexp[:, t, bass.ds(u, 1)]))
                post_norm(lambda: y_done(NM), 1.0, False)
                V.tensor_copy(small[:, 121:122], epsc[:]).then_inc(sem["final"], 1)


NAMES = [
    "x", "ff1_norm_pre", "ff1_w_gate", "ff1_w_up", "ff1_w_down", "ff1_norm_post", "mix_norm_pre", "w_in",
    "conv_w", "conv_b", "dt_bias", "a_log", "d_skip", "ssd_norm", "pool_w", "pool_scale", "w_out",
    "mix_norm_post", "ff2_norm_pre", "ff2_w_gate", "ff2_w_up", "ff2_w_down", "ff2_norm_post", "c_2",
    "ctx_2", "c_ctx_2", "ada_w_2", "ada_b_2", "norm1_g_2", "norm2_g_2", "attn_w_in_2", "attn_w_out_2",
    "qnorm_a_2", "knorm_a_2", "qnorm_b_2", "knorm_b_2", "sink_b_2", "ffn_w_gate_2", "ffn_w_up_2",
    "ffn_w_down_2", "conv_w_in_2", "conv_w_2", "conv_w_out_2", "router_w_2", "moe_w_gate_2",
    "moe_w_up_2", "moe_w_down_2"]


def constants():
    f4 = np.float32
    i, j = np.arange(P)[:, None], np.arange(P)[None, :]
    low = np.where(j <= i, 0.0, NEG)
    z = np.zeros((P, P))
    tok = np.arange(S, dtype=f4)
    inv = (f4(500000.0) ** (-np.arange(0, 16, 2, dtype=f4) / f4(16))).astype(f4)
    ang = (tok[:, None] * inv[None, :]).astype(f4)
    rope = np.concatenate([np.cos(ang), np.sin(ang)], -1).reshape(NT, P, 16).transpose(1, 0, 2)
    cnt = np.empty((P, 2, S))
    for g in range(4):
        cnt[64 * (g % 2):64 * (g % 2) + 64, g // 2, :] = 1.0 / np.minimum(np.arange(1, S + 1), 2 ** (g + 1))
    inv2 = (f4(10000.0) ** (-np.arange(0, 32, 2, dtype=f4) / f4(32))).astype(f4)
    row, col = np.divmod(np.arange(S), 64)
    ang2 = np.concatenate([row[:, None].astype(f4) * inv2, col[:, None].astype(f4) * inv2], -1).astype(f4)
    rope2 = np.concatenate([np.cos(ang2), np.sin(ang2)], -1).reshape(NT, P, 64).transpose(1, 0, 2)
    q, k = np.arange(S)[:, None], np.arange(S)[None, :]
    band = np.where(np.abs(q - k) <= 128, 0.0, NEG).reshape(NT, P, S).transpose(1, 0, 2)
    return {k_: np.ascontiguousarray(v, dtype=f4) for k_, v in {
        "c_ident": np.eye(P), "c_cmask": np.concatenate([low.T, z], 1), "c_qmask": np.concatenate([low, z, low], 1),
        "c_rope": rope, "c_rcnt": cnt, "c_rope2": rope2, "c_band": band}.items()}


def kernel(**inputs):
    from concourse import bacc
    from concourse.bass_utils import run_bass_kernel_spmd

    nc = bacc.Bacc("TRN2", target_bir_lowering=False, num_devices=1)
    arrays = {}
    for name in NAMES:
        arrays[name] = np.ascontiguousarray(inputs[name])
    arrays.update(constants())
    T = {}
    for name, a in arrays.items():
        T[name] = nc.dram_tensor(f"in_{name}", a.shape, F32, kind="ExternalInput").ap()
    out = nc.dram_tensor("out_0", (1, S, D), F32, kind="ExternalOutput").ap()
    mods = nc.dram_tensor("mods", (DEPTH, 2, ADA), F32).ap()
    build(nc, T, out, mods)
    r = run_bass_kernel_spmd(nc, [{f"in_{k}": v for k, v in arrays.items()}], core_ids=[0])
    return r.results[0]["out_0"]
```

```python
from contextlib import ExitStack, contextmanager

import numpy as np

import concourse.bass as bass
from concourse import mybir

F32 = mybir.dt.float32
F32R = mybir.dt.float32r
ACT = mybir.ActivationFunctionType
ALU = mybir.AluOpType
AX = mybir.AxisListType.X

P = 128
S = 256
NT = S // P
D = 1024
KD = D // P
DEPTH = 2
F1 = 2816
FE = 3584
NE = 8
FC = 256
FB = FC // P
N1 = F1 // FC
NX = FE // FC
NM = NE * NX
GC = 512
PIECE = 2048
EPS = 1e-6
NEG = -1e30

SSD_IN, HEADS, HP = 512, 8, 64
OFF_XBC, OFF_DT, OFF_U, OFF_Q, OFF_K, OFF_V = 512, 1536, 1544, 1800, 2056, 2312
PAD = 16
CPAD = 3
ADA = 6 * D
AC = ADA // (2 * 8)

PER_TURN = {'act_ff1': {'a_done': 2,
             'a_free': 2,
             'd_free': 2,
             'gu0': 2,
             'raw0': 32,
             'raw1': 32,
             'raw2': 32,
             't_psum': 2},
 'act_ff2': {'a_done': 2,
             'a_free': 2,
             'd_free': 2,
             'gu0': 2,
             'raw0': 32,
             'raw1': 32,
             'raw2': 32,
             't_psum': 2},
 'act_ffn': {'a_done': 2,
             'a_free': 2,
             'd_free': 2,
             'gu0': 2,
             'raw0': 32,
             'raw1': 32,
             'raw2': 32,
             't_psum': 2},
 'act_layer': {'a_done': 30,
               'a_free': 30,
               'act_step': 16,
               'amax': 4,
               'arg': 2,
               'ctx_stored': 32,
               'd_free': 22,
               'gated': 1,
               'gu0': 22,
               'mix_par': 144,
               'pT_psum': 4,
               'pool_psum': 1,
               'qk_psum': 1,
               'raw0': 512,
               'raw1': 512,
               'raw2': 352,
               'res_ready': 6,
               'scale': 4,
               't_psum': 22,
               'taps_bc': 1,
               'taps_xs': 1,
               'xt_psum': 16,
               'y0': 2,
               'y_done': 22},
 'act_moe': {'a_done': 2,
             'a_free': 2,
             'd_free': 2,
             'gu0': 2,
             'raw0': 32,
             'raw1': 32,
             'raw2': 32,
             't_psum': 2},
 'dve_ff1': {'ada_bias0': 16,
             'ada_bias1': 16,
             'ada_in0': 16,
             'ada_in1': 16,
             'ada_sum': 2,
             'dve_step': 14,
             'hi': 6,
             'ht_hi': 2,
             'sg0': 2,
             'sg1': 2},
 'dve_ff2': {'ada_bias0': 16,
             'ada_bias1': 16,
             'ada_in0': 16,
             'ada_in1': 16,
             'ada_sum': 2,
             'dve_step': 14,
             'hi': 6,
             'ht_hi': 2,
             'sg0': 2,
             'sg1': 2},
 'dve_ffn': {'hi': 6, 'ht_hi': 2, 'sg0': 2, 'sg1': 2},
 'dve_layer': {'a_done': 30,
               'acs_psum': 2,
               'ada_bias0': 128,
               'ada_bias1': 128,
               'ada_in0': 128,
               'ada_in1': 128,
               'ada_sum': 16,
               'bc_out': 1,
               'cb_psum': 1,
               'ctx_bias': 32,
               'ctx_used1': 2,
               'decay': 2,
               'dt_psum': 1,
               'dve_step': 186,
               'gain': 80,
               'gain_one': 1,
               'gain_row': 48,
               'hi': 84,
               'ht_hi': 22,
               'kv_out': 1,
               'mix_par': 144,
               'pT_psum': 4,
               'pool_out': 1,
               'probs': 4,
               'pv_psum': 4,
               'root': 14,
               'scores': 4,
               'sg0': 22,
               'sg1': 22,
               'soft': 1,
               'ssd_psum': 2,
               'x_hi': 32,
               'xs_out': 1,
               'xs_psum': 1,
               'y0': 2,
               'y_done': 22},
 'dve_moe': {'hi': 6, 'ht_hi': 2, 'sg0': 2, 'sg1': 2},
 'pe_ff1': {'ada_acc0': 1,
            'ada_acc1': 1,
            'h0': 2,
            'h1': 2,
            'ht': 2,
            'split0': 2,
            'split1': 2,
            'split2': 2},
 'pe_ff2': {'ada_acc0': 1,
            'ada_acc1': 1,
            'h0': 2,
            'h1': 2,
            'ht': 2,
            'split0': 2,
            'split1': 2,
            'split2': 2},
 'pe_ffn': {'h0': 2, 'h1': 2, 'ht': 2, 'split0': 2, 'split1': 2, 'split2': 2},
 'pe_layer': {'acs_rows': 1,
              'ada_acc0': 8,
              'ada_acc1': 8,
              'arg': 2,
              'bc_out': 1,
              'conv_bc': 1,
              'conv_xs': 1,
              'ctx_row': 2,
              'd_half': 2,
              'dtc': 1,
              'h0': 22,
              'h1': 22,
              'ht': 22,
              'kv_out': 1,
              'mix_par': 144,
              'pT': 4,
              'pool_out': 1,
              'pooled': 1,
              'probs': 4,
              'qkT': 1,
              'raw0': 512,
              'raw1': 512,
              'roped': 1,
              'seg': 2,
              'split0': 30,
              'split1': 30,
              'split2': 22,
              'uq_out': 1,
              'x_lo': 32,
              'xdt': 1,
              'xn_ready': 12,
              'xs_out': 1,
              'z_out': 1},
 'pe_moe': {'h0': 2, 'h1': 2, 'ht': 2, 'split0': 2, 'split1': 2, 'split2': 2},
 'pool_ada1': {'ada_bias_free': 2, 'ada_row': 2, 'ada_stored0': 16, 'ada_stored1': 16},
 'pool_ada2': {'ada_bias_free': 2, 'ada_row': 2, 'ada_stored0': 16, 'ada_stored1': 16},
 'pool_layer': {'ada_bias_free': 16,
                'ada_row': 16,
                'ada_stored0': 128,
                'ada_stored1': 128,
                'ctx_row': 2,
                'ctx_stored': 32,
                'pool_step': 9,
                'res_ready': 6,
                'uq_out': 1,
                'x_lo': 32},
 'sp_ff1': {'ada_acc0': 1, 'ada_acc1': 1, 'split0': 2, 'split1': 2, 'split2': 2},
 'sp_ff2': {'ada_acc0': 1, 'ada_acc1': 1, 'split0': 2, 'split1': 2, 'split2': 2},
 'sp_ffn': {'split0': 1, 'split1': 1, 'split2': 1},
 'sp_layer': {'ada_acc0': 8,
              'ada_acc1': 8,
              'ctx_used0': 2,
              'ctx_used1': 2,
              'res_ready': 6,
              'split0': 30,
              'split1': 30,
              'split2': 22},
 'sp_moe': {'split0': 14, 'split1': 14, 'split2': 14},
 'sp_moe0': {'split0': 1, 'split1': 1, 'split2': 1},
 'sp_moec': {'split0': 1, 'split1': 1, 'split2': 1}}
PER_TURN_SEEN = {}


class Seen:

    def __init__(self):
        self.count = {}
        self.loops = []

    def __call__(self, name, events=1):
        self.count[name] = self.count.get(name, 0) + events
        value = self.count[name]
        for turn, label in self.loops:
            per = PER_TURN.get(label, {}).get(name, 0)
            if per:
                value = turn * per + value
        return value

    @contextmanager
    def loop(self, engine, label, turns, start=0):
        before = dict(self.count)
        with engine.Fori(start, start + turns) as i:
            self.loops.append((i - start if start else i, label))
            yield i
            self.loops.pop()
        per = {k: v - before.get(k, 0) for k, v in self.count.items() if v != before.get(k, 0)}
        PER_TURN_SEEN[label] = per
        for k, v in per.items():
            self.count[k] = before.get(k, 0) + v * turns


def build(nc, T, out, mods, stop=None):
    ctx = ExitStack()
    with ctx:
        def sb(name, shape, dt=F32):
            return ctx.enter_context(nc.sbuf_tensor(name, shape, dt))

        sems = {}

        class Sems:
            def __getitem__(self, name):
                if name not in sems:
                    sems[name] = ctx.enter_context(nc.semaphore(name))
                return sems[name]
        sem = Sems()

        raw = sb("raw", [P, 3, PIECE])
        a_hi, a_lo = sb("a_hi", [P, 2, 2, PIECE], F32R), sb("a_lo", [P, 2, 2, PIECE], F32R)
        d_hi, d_lo = sb("d_hi", [P, PIECE], F32R), sb("d_lo", [P, PIECE], F32R)
        x_hi, x_lo = sb("x_hi", [P, KD, S], F32R), sb("x_lo", [P, KD, S], F32R)
        ht_hi, ht_lo = sb("ht_hi", [P, FB, S], F32R), sb("ht_lo", [P, FB, S], F32R)
        res = sb("res", [P, NT, D])
        xn = sb("xn", [P, NT, D])
        mod = sb("mod", [P, KD, S])
        gbc = sb("gbc", [P, D])
        gcol = sb("gcol", [P, 4, KD])
        sg = sb("sg", [P, NT, FC])
        hb = sb("hb", [P, NT, FC])
        st = sb("st", [P, 2, NT])
        ident = sb("ident", [P, P])
        cmask = sb("cmask", [P, 2 * P])
        qmask = sb("qmask", [P, 3 * P])
        epsc = sb("epsc", [P, 2])
        small = sb("small", [P, 256])
        warm = sb("warm", [P, 4])
        ARENA = 9504
        arena = sb("arena", [P, ARENA])
        psum = ctx.enter_context(nc.psum_tensor("psum", [P, 8, 512], F32))
        Y = psum[:, 0:4, :].rearrange("p (t h) n -> p t (h n)", t=NT)
        TB, MB = psum[:, 6, :], psum[:, 7, :]

        def f(ap):
            return ap.bitcast(F32)

        def area(at, *shape):
            n = int(np.prod(shape))
            assert at + n <= ARENA, (at, n)
            ap = arena[:, at:at + n]
            if len(shape) == 2:
                ap = ap.rearrange("p (a b) -> p a b", b=shape[1])
            if len(shape) == 3:
                ap = ap.rearrange("p (a b c) -> p a b c", b=shape[1], c=shape[2])
            return ap

        ones = sb("ones", [P, 1])
        adaw = area(0, 2, KD, AC)
        adaa = area(2 * KD * AC, 2, AC)
        adar = area(2 * KD * AC + 2 * AC, 2, AC)[0:1]
        crow = [raw[0:1, 2, c * GC:(c + 1) * GC] for c in range(2)]
        zs = area(0, NT, SSD_IN)
        xT = area(1024, 8, CPAD + S + 1)
        arg = [area(1024, 4, 384), mod[:].rearrange("p k s -> p (k s)")[:, 0:1536].rearrange("p (h n) -> p h n", n=384)]
        cT = mod
        xdt = area(3104, NT, SSD_IN)
        xsd = area(4128, NT, SSD_IN)
        qk = area(5152, NT, 512)
        vv = area(6176, NT, 256)
        qkT = area(6688, 4, S)
        prob = [area(7712, 384), area(5152, 384)]
        pT = [area(8096, 384), area(5536, 384)]
        dts = area(8480, 4 * S)[0:HEADS]
        uw = [sb(f"uw{i}", [P, 2, PAD + S]) for i in range(2)]
        um, pm = hb, sg
        poolw = sb("poolw", [P, 2, P])
        convw = small[:, 0:32].rearrange("p (j c) -> p j c", c=8)
        convb = small[:, 32:40]
        dskip = small[:, 40:48]
        dtb, alog = small[0:8, 48:49], small[0:8, 49:50]
        dtc = small[:, 52:68].rearrange("p (t h) -> p t h", h=8)
        nacs = small[:, 68:84].rearrange("p (t h) -> p t h", h=8)
        qstat = small[:, 84:108].rearrange("p (c h t) -> p c h t", c=3, t=NT)
        rope = sb("rope", [P, NT, 16])
        rcnt = sb("rcnt", [P, 2, S])

        cs = sb("cs", [P, KD, 2])
        qq = area(0, NT, 1024)
        kk = area(2048, 4, 256)
        vk = area(3072, 4, 256)
        k_hi, k_lo = (d[:, 0:1024].rearrange("p (y n) -> p y n", n=512) for d in (d_hi, d_lo))
        qsq, ksq = area(6144, NT * 1024), area(8192, 1024)
        prob2 = area(7168, 2, 512)
        pT2 = area(8192, 2, 512)
        ctxr = area(4096, NT, D)
        band = hb
        rope2 = sg[:, 0, 0:128].rearrange("p (t n) -> p t n", t=NT)
        qkg = sg[:, 1, :].rearrange("p (i n) -> p i n", n=64)
        rms = small[:, 160:208]
        head_rms = rms
        ctx_rms = rms[:, 32:40]
        nsink = small[:, 148:156]
        sm2 = sb("sm2", [P, 4, 32])
        cg = area(0, 4, S)
        zT = area(1024, 4, S + 2)
        acc = area(2056, 4, S)
        convw2 = small[:, 210:234].rearrange("p (j c) -> p j c", c=8)
        lg = area(0, 8, NT, NE)
        gexp = area(256, NT, NM)
        CONV_UNITS = [1024, 2048, 0, 1536, 2560, 512]

        block = ctx.enter_context(nc.Block())

        def colsof(row):
            return row.rearrange("(k p) -> p k", p=P)

        def kview(w):
            return w.rearrange("(k p) n -> p k n", p=P)

        IN_UNITS = [(OFF_DT, 8), (1024, 512), (512, 512), (OFF_U, 512), (OFF_K, 512), (0, 512)]

        @block.sync
        def _(sp):
            seen = Seen()

            def piece(j, src, dst, free=None):
                free = free or f"split{j}"
                sp.wait_ge(sem[free], seen(free))
                sp.sem_inc(sem["sp_past_wait"], 1)
                sp.dma_start(dst, src).then_inc(sem[f"raw{j}"], 16)

            def plain(w, c0, n):
                v = kview(w)
                for j in range(2):
                    dst = raw[:, j, 0:4 * n].rearrange("p (k n) -> p k n", n=n)
                    piece(j, v[:, 4 * j:4 * j + 4, bass.ds(c0, n)], dst)

            def gate_up(wg, wu, c0):
                for j, w in enumerate((wg, wu)):
                    piece(j, kview(w)[:, :, bass.ds(c0, FC)],
                          raw[:, j, :].rearrange("p (k n) -> p k n", n=FC))

            def down(wd, c0):
                piece(2, wd[bass.ds(c0, FC), :].rearrange("(b p) n -> p b n", p=P),
                      raw[:, 2, :].rearrange("p (b n) -> p b n", n=D))

            def ffn(label, wg, wu, wd, after=(), ada=None):
                gate_up(wg, wu, 0)
                gate_up(wg, wu, FC)
                if ada is None:
                    with seen.loop(sp, label, N1 - 2) as i:
                        gate_up(wg, wu, i * FC + 2 * FC)
                        down(wd, i * FC)
                else:
                    sp.wait_ge(sem["res_ready"], seen("res_ready", ada[2] * NT))
                    sp.sem_inc(sem["sp_past_wait"], 1)
                    with seen.loop(sp, label, 4) as i:
                        for q in range(2):
                            sp.wait_ge(sem[f"ada_acc{q}"], seen(f"ada_acc{q}"))
                            sp.sem_inc(sem["sp_past_wait"], 1)
                            sp.dma_start(adaw[:, q], kview(ada[0])[:, :, bass.ds(i * 2 * AC + (ada[1] * 8 + q) * AC, AC)]
                                         ).then_inc(sem[f"ada_in{q}"], 16)
                            gate_up(wg, wu, i * 2 * FC + (2 + q) * FC)
                            down(wd, i * 2 * FC + q * FC)
                    gate_up(wg, wu, (N1 - 1) * FC)
                    down(wd, (N1 - 3) * FC)
                for n in (N1 - 2, N1 - 1):
                    if after:
                        after[n - N1 + 2]()
                    down(wd, n * FC)

            def layer(l):
                W = {k: T[k][l] for k in ("ff1_w_gate", "ff1_w_up", "ff1_w_down", "w_in", "w_out",
                                          "ff2_w_gate", "ff2_w_up", "ff2_w_down")}
                ffn("sp_ff1", W["ff1_w_gate"], W["ff1_w_up"], W["ff1_w_down"],
                    [lambda: plain(W["w_in"], *IN_UNITS[0]), lambda: plain(W["w_in"], *IN_UNITS[1])],
                    ada=(T["ada_w_2"][l], 0, 1))
                for u in IN_UNITS[2:]:
                    plain(W["w_in"], *u)
                for c in range(2):
                    for j in range(2):
                        if c == 0:
                            sp.wait_ge(sem[f"split{j}"], seen(f"split{j}"))
                        else:
                            sp.wait_ge(sem[f"ctx_used{j}"], seen(f"ctx_used{j}"))
                        sp.sem_inc(sem["sp_past_wait"], 1)
                        sp.dma_start(raw[:, j, :].rearrange("p (k n) -> p k n", n=GC),
                                     kview(T["ada_w_2"][0])[:, 4 * j:4 * j + 4, bass.ds(l * D + c * GC, GC)]
                                     ).then_inc(sem[f"raw{j}"], 16)
                for j in range(2):
                    piece(j, kview(W["w_out"])[:, 4 * j:4 * j + 4, 0:GC],
                          raw[:, j, :].rearrange("p (k n) -> p k n", n=GC), f"ctx_used{j}")
                plain(W["w_out"], GC, GC)
                ffn("sp_ff2", W["ff2_w_gate"], W["ff2_w_up"], W["ff2_w_down"],
                    ada=(T["ada_w_2"][l], 1, 2))

            with seen.loop(sp, "sp_layer", DEPTH) as l:
                layer(l)
            wi = T["attn_w_in_2"][0]
            if stop == "first":
                plain(wi, 512, 512)
                sp.wait_ge(sem["final"], 1)
                for t in range(NT):
                    sp.dma_start(out[0, t * P:(t + 1) * P, :], res[:, t, :]).then_inc(sem["stored"], 16)
                sp.wait_ge(sem["stored"], 32)
                return
            for c in range(3):
                plain(wi, c * GC, GC)
            plain(wi, 512, 256)
            plain(wi, 1280, 256)
            for c in range(2):
                plain(T["attn_w_out_2"][0], c * GC, GC)
            ffn("sp_ffn", T["ffn_w_gate_2"][0], T["ffn_w_up_2"][0], T["ffn_w_down_2"][0],
                [lambda: plain(T["conv_w_in_2"][0], CONV_UNITS[0], GC),
                 lambda: plain(T["conv_w_in_2"][0], CONV_UNITS[1], GC)])
            for c0 in CONV_UNITS[2:]:
                plain(T["conv_w_in_2"][0], c0, GC)
            for c in range(2):
                plain(T["conv_w_out_2"][0], c * GC, GC)
            plain(T["router_w_2"][0], 0, NE)
            mg, mu = T["moe_w_gate_2"][0], T["moe_w_up_2"][0]
            md = T["moe_w_down_2"][0].rearrange("e f d -> (e f) d")
            for c in range(2):
                gate_up(mg[0], mu[0], c * FC)
            with seen.loop(sp, "sp_moe0", NX - 2) as c:
                gate_up(mg[0], mu[0], c * FC + 2 * FC)
                down(md, c * FC)
            with seen.loop(sp, "sp_moe", NE - 1) as e:
                for c in range(2):
                    gate_up(mg[e + 1], mu[e + 1], c * FC)
                    down(md, e * FE + (NX - 2 + c) * FC)
                with seen.loop(sp, "sp_moec", NX - 2) as c:
                    gate_up(mg[e + 1], mu[e + 1], c * FC + 2 * FC)
                    down(md, e * FE + (FE + c * FC))
            down(md, (NM - 2) * FC)
            down(md, (NM - 1) * FC)
            sp.wait_ge(sem["final"], 1)
            for t in range(NT):
                sp.dma_start(out[0, t * P:(t + 1) * P, :], res[:, t, :]).then_inc(sem["stored"], 16)
            sp.wait_ge(sem["stored"], 32)

        @block.gpsimd
        def _(pool):
            seen = Seen()
            seen.count["ada_row"] = 2
            M = mods

            def bc(row, n=P):
                return row.unsqueeze(0).broadcast_to([n, row.shape[0]])

            def load(dst, src, name="consts"):
                pool.dma_start(dst, src, allow_slow_non_contiguous=True).then_inc(sem[name], 16)

            nc.gpsimd.memset(uw[0][:], 0.0).then_inc(sem["pool_zero"], 1)
            nc.gpsimd.memset(uw[1][:], 0.0).then_inc(sem["pool_zero"], 1)
            nc.gpsimd.memset(poolw[:], 0.0).then_inc(sem["pool_zero"], 1)
            nc.gpsimd.memset(gcol[:], 0.0).then_inc(sem["pool_zero"], 1)
            nc.gpsimd.memset(epsc[:, 0:1], EPS).then_inc(sem["pool_zero"], 1)
            nc.gpsimd.memset(epsc[:, 1:2], 4 * EPS).then_inc(sem["pool_zero"], 1)
            nc.gpsimd.memset(ones[:], 1.0).then_inc(sem["pool_zero"], 1)
            nc.gpsimd.memset(warm[:], 1.0).then_inc(sem["pool_zero"], 1)
            CONSTS = [(ident[:], T["c_ident"]), (cmask[:, 0:S], T["c_cmask"]), (qmask[:], T["c_qmask"]),
                      (rope[:], T["c_rope"]), (rcnt[:], T["c_rcnt"]),
                      (res[:], T["x"][0].rearrange("(t p) n -> p t n", p=P)),
                      (small[:, 128:136], colsof(T["c_ctx_2"])), (small[:, 136:144], colsof(T["c_2"][0]))]
            for dst, src in CONSTS:
                load(dst, src)
            pool.wait_ge(sem["consts"], 16 * len(CONSTS))
            pool.wait_ge(sem["pool_zero"], 8)
            pool.sem_inc(sem["consts_in"], 1)

            def modulation(l, label, half):
                with seen.loop(pool, label, 4) as i:
                    for q in range(2):
                        pool.wait_ge(sem["ada_row"], seen("ada_bias_free"))
                        pool.sem_inc(sem["pool_past_wait"], 1)
                        pool.dma_start(adar[:, q, :], T["ada_b_2"][l][bass.ds(i * 2 * AC + (half * 8 + q) * AC, AC)].unsqueeze(0)
                                       ).then_inc(sem[f"ada_bias{q}"], 16)
                    for q in range(2):
                        pool.wait_ge(sem["ada_row"], seen("ada_row"))
                        pool.sem_inc(sem["pool_past_wait"], 1)
                        pool.dma_start(M[l, 1, bass.ds(i * 2 * AC + (half * 8 + q) * AC, AC)].unsqueeze(0), adar[:, q, :]
                                       ).then_inc(sem[f"ada_stored{q}"], 16)
                    for q in range(2):
                        pool.wait_ge(sem[f"ada_stored{q}"], seen(f"ada_stored{q}", 16))

            def link(ins):
                ins.then_inc(sem["pool_step"], 1)
                pool.wait_ge(sem["pool_step"], seen("pool_step"))

            def gains_in(first=False):
                pool.wait_ge(sem["x_lo"], seen("x_lo", KD))
                pool.sem_inc(sem["pool_past_wait"], 1)

            def columns(cols):
                gains_in()
                for n, (i, src) in enumerate(cols):
                    pool.dma_start(gcol[:, i, 0:src.shape[1]], src, allow_slow_non_contiguous=True).then_inc(sem["gain"], 16)

            def row(src):
                pool.wait_ge(sem["res_ready"], seen("res_ready", NT))
                pool.sem_inc(sem["pool_past_wait"], 1)
                pool.dma_start(gbc[:], bc(src)).then_inc(sem["gain_row"], 16)

            def pool_branch(l):
                W = T["pool_w"][l]
                pool.wait_ge(sem["uq_out"], seen("uq_out"))
                pool.sem_inc(sem["pool_past_wait"], 1)
                n = PAD + S
                a, b = uw

                src, dst = a, b
                link(nc.gpsimd.tensor_copy(um[:], a[:, :, PAD:n]))
                for g in range(4):
                    w = 1 << g
                    lo = 2 * w - 1
                    link(nc.gpsimd.tensor_tensor(dst[:, :, lo:n], src[:, :, lo:n], src[:, :, lo - w:n - w], ALU.add))
                    rows = slice(64 * (g % 2), 64 * (g % 2) + 64)
                    c = g // 2
                    link(nc.gpsimd.tensor_tensor(pm[rows, c, :], dst[rows, c, PAD:n],
                                                 rcnt[rows, c, :], ALU.mult))
                    src, dst = dst, src
                nc.gpsimd.tensor_tensor(um[:], pm[:], um[:], ALU.subtract).then_inc(sem["pooled"], 1)

            def mixer_loads(l):
                for dst, src in [(convw, T["conv_w"][l].rearrange("j (c p) -> p j c", p=P)),
                                 (convb, T["conv_b"][l].rearrange("(c p) -> p c", p=P)),
                                 (dskip, bc(T["d_skip"][l])), (dtb, T["dt_bias"][l].unsqueeze(1)),
                                 (alog, T["a_log"][l].unsqueeze(1))] + [
                                 (poolw[64 * (g % 2):64 * (g % 2) + 64, g // 2, 64 * (g % 2):64 * (g % 2) + 64],
                                  T["pool_w"][l, g]) for g in range(4)]:
                    pool.dma_start(dst, src, allow_slow_non_contiguous=True).then_inc(sem["mix_par"], 16)

            with seen.loop(pool, "pool_layer", DEPTH) as l:
                columns([(0, colsof(T["ff1_norm_pre"][l]))])
                row(T["ff1_norm_post"][l])
                mixer_loads(l)
                modulation(l, "pool_ada1", 0)
                columns([(0, colsof(T["mix_norm_pre"][l]))])
                row(T["mix_norm_post"][l])
                for c in range(2):
                    pool.dma_start(crow[c], T["ada_b_2"][0][bass.ds(l * D + c * GC, GC)].unsqueeze(0)).then_inc(sem["ctx_bias"], 16)
                pool_branch(l)
                for c in range(2):
                    pool.wait_ge(sem["ctx_row"], seen("ctx_row"))
                    pool.sem_inc(sem["pool_past_wait"], 1)
                    pool.dma_start(M[0, 0, bass.ds(l * D + c * GC, GC)].unsqueeze(0), crow[c]).then_inc(sem["ctx_stored"], 16)
                gains_in()
                pool.dma_start(gcol[:, 0, 0:4], colsof(T["ssd_norm"][l]), allow_slow_non_contiguous=True).then_inc(sem["gain"], 16)
                pool.dma_start(gcol[:, 0, 4:6], colsof(T["pool_scale"][l]), allow_slow_non_contiguous=True).then_inc(sem["gain"], 16)
                nc.gpsimd.memset(gcol[:, 0, 6:8], 1.0).then_inc(sem["gain_one"], 1)
                columns([(0, colsof(T["ff2_norm_pre"][l]))])
                row(T["ff2_norm_post"][l])
                modulation(l, "pool_ada2", 1)
                pool.wait_ge(sem["ctx_stored"], seen("ctx_stored", 32))
            if stop != "first":
                def part(l, r, i):
                    return M[l, r, i * D:(i + 1) * D]
                G1, G2 = T["norm1_g_2"], T["norm2_g_2"]
                columns([(0, colsof(G1[0])), (1, colsof(part(0, 1, 0))), (2, colsof(part(0, 1, 1)))])
                row(part(0, 1, 2))
                load(ctxr, T["ctx_2"][0].rearrange("(t p) n -> p t n", p=P), "ctx_in")
                for dst, src in [(band[:], T["c_band"]),
                                 (rope2, T["c_rope2"]), (nsink, bc(T["sink_b_2"][0])),
                                 (convw2, T["conv_w_2"][0].rearrange("j (c p) -> p j c", p=P))] + [
                                 (qkg[:, i, :], bc(T[n][0])) for i, n in enumerate(
                                     ("qnorm_a_2", "qnorm_b_2", "knorm_a_2", "knorm_b_2"))]:
                    load(dst, src, "att_in")
                columns([(0, colsof(G1[0])), (1, colsof(part(0, 0, 0))), (2, colsof(part(0, 0, 1)))])
                gains_in()
                nc.gpsimd.memset(gcol[:, 1:3, :], 0.0).then_inc(sem["pool_zero"], 1)
                nc.gpsimd.memset(gcol[:, 0, :], 1.0).then_inc(sem["gain_one"], 1)
                for l, i, g in ((0, 3, G2), (1, 0, G1), (1, 3, G2)):
                    columns([(0, colsof(g[l])), (1, colsof(part(l, 1, i))), (2, colsof(part(l, 1, i + 1)))])
                    row(part(l, 1, i + 2))
                    if (l, i) == (1, 0):
                        seen("x_lo", KD)

        @block.tensor
        def _(pe):
            seen = Seen()
            seen.count.update({"split0": 1, "split1": 1, "split2": 1, "x_lo": 8, "ada_acc0": 1, "ada_acc1": 1})
            pe.sem_inc(sem["a_done"], 2)
            pe.sem_inc(sem["d_done"], 1)
            par = [0]

            def mm3(o, xh, xl, wh, wl, start, stop_):
                pe.matmul(o, xh, wh, start=start, stop=False, skip_group_check=True)
                pe.matmul(o, xh, wl, start=False, stop=False, skip_group_check=True)
                return pe.matmul(o, xl, wh, start=False, stop=stop_, skip_group_check=True)

            def split_in():
                for j in range(2):
                    pe.wait_ge(sem[f"split{j}"], seen(f"split{j}"))

            def wview(n):
                b = par[0]
                return [w[:, b, :, 0:4 * n].rearrange("p j (k n) -> p j k n", n=n) for w in (a_hi, a_lo)]

            fresh = [False]

            def x_in(k):
                if fresh[0]:
                    pe.wait_ge(sem["x_lo"], seen("x_lo"))
                    fresh[0] = k < KD - 1

            def plain_tok(outs, n, c0=0, w=None, last=True):
                w = w or n
                wh, wl = wview(n)
                for t in range(NT):
                    for k in range(KD):
                        x_in(k)
                        ins = mm3(outs[t], x_hi[:, k, t * P:(t + 1) * P], x_lo[:, k, t * P:(t + 1) * P],
                                  wh[:, k // 4, k % 4, c0:c0 + w], wl[:, k // 4, k % 4, c0:c0 + w],
                                  k == 0, k == KD - 1)
                if last:
                    ins.then_inc(sem["a_done"], 1)
                    par[0] ^= 1

            def plain_tr(outs, n, last=True):
                wh, wl = wview(n)
                m = min(P, n)
                for c, o in enumerate(outs):
                    for k in range(KD):
                        x_in(k)
                        a, b = (w[:, k // 4, k % 4, c * P:c * P + m] for w in (wh, wl))
                        pe.matmul(o, a, x_hi[:, k, :], start=k == 0, stop=False, skip_group_check=True)
                        pe.matmul(o, b, x_hi[:, k, :], start=False, stop=False, skip_group_check=True)
                        ins = pe.matmul(o, a, x_lo[:, k, :], start=False, stop=k == KD - 1, skip_group_check=True)
                if last:
                    ins.then_inc(sem["a_done"], 1)
                    par[0] ^= 1

            def halves(bank):
                return [psum[:, b, h * S:(h + 1) * S] for b in bank for h in range(2)]

            def gate_up():
                split_in()
                b = par[0]
                for t in range(NT):
                    for k in range(KD):
                        x_in(k)
                        wh, wl = (w[:, b, :, k * FC:(k + 1) * FC] for w in (a_hi, a_lo))
                        ins = mm3(psum[:, 4 + t, :].rearrange("p (a n) -> p a n", n=FC),
                                  x_hi[:, k, t * P:(t + 1) * P], x_lo[:, k, t * P:(t + 1) * P],
                                  wh, wl, k == 0, k == KD - 1)
                    ins.then_inc(sem["a_done"] if t else sem["gu0"], 1)
                par[0] ^= 1

            def down(first, last):
                if last:
                    pe.wait_ge(sem["d_half"], seen("d_half"))
                else:
                    pe.wait_ge(sem["split2"], seen("split2"))
                pe.wait_ge(sem["ht"], seen("ht"))
                order = ([(b, t, h) for b in range(FB) for t in range(NT) for h in range(2)] if last else
                         [(b, t, h) for t in range(NT) for h in range(2) for b in range(FB)])
                for b, t, h in order:
                    if last and (b, t, h) == (1, 0, 0):
                        pe.wait_ge(sem["split2"], seen("split2"))
                    wh, wl = (w[:, b * D + h * 512:b * D + h * 512 + 512] for w in (d_hi, d_lo))
                    ins = mm3(psum[:, 2 * t + h, :], ht_hi[:, b, t * P:(t + 1) * P],
                              ht_lo[:, b, t * P:(t + 1) * P], wh, wl, first and b == 0, last and b == FB - 1)
                    if last and (b, t, h) == (1, 0, 1):
                        ins.then_inc(sem["y0"], 1)
                ins.then_inc(sem["d_done"], 1)

            def turn_hidden():
                for t in range(NT):
                    pe.wait_ge(sem[f"h{t}"], seen(f"h{t}"))
                    for b in range(FB):
                        ins = pe.transpose(TB[:, b * S + t * P:b * S + (t + 1) * P], hb[:, t, b * P:(b + 1) * P], ident[:])
                ins.then_inc(sem["t_psum"], 1)

            def column_sum(q):
                pe.wait_ge(sem[f"ada_acc{q}"], seen(f"ada_acc{q}"))
                pe.matmul(MB[0:1, 0:AC], ones[:], adaa[:, q, :], start=True, stop=True).then_inc(sem["ada_sum"], 1)

            def ffn(label, n, ada=False):
                gate_up(); turn_hidden()
                gate_up(); down(True, False)
                if ada:
                    column_sum(0)
                turn_hidden()
                with seen.loop(pe, label, (n - 3) // 2 - ada):
                    for q in range(2):
                        gate_up(); down(False, False)
                        if ada:
                            column_sum(1 - q)
                        turn_hidden()
                if ada:
                    gate_up(); down(False, False); column_sum(1); turn_hidden()
                    gate_up(); down(False, False); turn_hidden()
                for _ in range(1 + (n - 3) % 2):
                    gate_up(); down(False, False); turn_hidden()
                down(False, True)

            def to_x():
                for t in range(NT):
                    pe.wait_ge(sem["xn_ready"], seen("xn_ready"))
                    for k in range(KD):
                        if t and k == KD // 2:
                            pe.wait_ge(sem["xn_ready"], seen("xn_ready"))
                        ins = pe.transpose(psum[:, k // 2, (k % 2) * S + t * P:(k % 2) * S + (t + 1) * P],
                                           xn[:, t, k * P:(k + 1) * P], ident[:])
                        if t and k % 2:
                            ins.then_inc(sem["xt_psum"], 1)
                fresh[0] = True

            def event(name):
                pe.wait_ge(sem[name], seen(name))

            def mixer():
                split_in(); plain_tr([MB[0:8, 0:S]], 8)
                split_in(); plain_tr(halves((4, 5)), GC)
                split_in(); plain_tr(halves((0, 1)), GC)
                split_in(); plain_tr(halves((2,)), GC, last=False)
                plain_tok([psum[:, 3, t * 256:(t + 1) * 256] for t in range(NT)], GC, 256, 256)
                event("bc_out")
                split_in(); plain_tok([psum[:, 4 + t, :] for t in range(NT)], GC)
                event("acs_rows")
                pe.sem_inc(sem["pe_past_wait"], 1)
                for i in range(2):
                    for t in range(NT):
                        ins = pe.transpose(TB[:, (i * 2 + t) * 8:(i * 2 + t) * 8 + 8],
                                           dts[:, i * S + t * P:i * S + (t + 1) * P], ident[0:8, 0:8])
                ins.then_inc(sem["dt_psum"], 1)
                event("xs_out")
                split_in(); plain_tok([psum[:, t, :] for t in range(NT)], GC)
                def context(c, bank):
                    if c == 0:
                        for j in range(2):
                            seen(f"raw{j}", 16 * (N1 + len(IN_UNITS)))
                    for j in range(2):
                        pe.wait_ge(sem[f"raw{j}"], seen(f"raw{j}", 16))
                        for k in range(4):
                            ins = pe.matmul(bank[0:1, :], cs[:, 4 * j + k, 0:1], raw[:, j, k * GC:(k + 1) * GC],
                                            start=4 * j + k == 0, stop=4 * j + k == KD - 1)
                        ins.then_inc(sem[f"ctx_used{j}"], 1)
                    if c:
                        for j in range(2):
                            seen(f"raw{j}", 16 * (2 + N1))

                def running(g):
                    for h in range(4):
                        ins = pe.matmul(psum[:, 2 + h // 2, (h % 2) * S:(h % 2) * S + S], ident[0:8, 4 * g + h:4 * g + h + 1].broadcast_to([8, P]),
                                        dts[:, S:2 * S], start=True, stop=True)
                    ins.then_inc(sem["acs_psum"], 1)

                def ssd(g):
                    event("seg")
                    for h in range(4):
                        o = 64 * (4 * g + h)
                        pe.matmul(psum[:, 4, o:o + 64], arg[g][:, h, 0:P], xdt[:, 0, o:o + 64], start=True, stop=True)
                        pe.matmul(psum[:, 5, o:o + 64], arg[g][:, h, P:S], xdt[:, 0, o:o + 64], start=True, stop=False)
                        ins = pe.matmul(psum[:, 5, o:o + 64], arg[g][:, h, S:S + P], xdt[:, 1, o:o + 64], start=False, stop=True)
                    ins.then_inc(sem["ssd_psum"], 1)

                event("uq_out")
                running(0)
                event("conv_bc"); event("dtc")
                for g, o in ((0, TB), (1, MB)):
                    pe.matmul(o[:, 0:S], cT[:, 4 + g, 0:P], cT[:, 6 + g, :], start=True, stop=True)
                    ins = pe.matmul(o[:, S:S + P], cT[:, 4 + g, P:S], cT[:, 6 + g, P:S], start=True, stop=True)
                ins.then_inc(sem["cb_psum"], 1)
                event("z_out"); event("conv_xs")
                for t in range(NT):
                    for c in range(4):
                        ins = pe.transpose(psum[:, t, c * P:(c + 1) * P], cT[:, c, t * P:(t + 1) * P], ident[:])
                ins.then_inc(sem["xs_psum"], 1)
                event("arg")
                running(1)
                event("kv_out")
                context(0, psum[:, 4, :])
                event("xdt"); event("ctx_row")
                ssd(0)
                event("roped"); event("arg")
                for a in range(4):
                    for t in range(NT):
                        ins = pe.transpose(psum[:, 2 + a // 2, (a % 2) * S + t * P:(a % 2) * S + (t + 1) * P],
                                           qk[:, t, a * P:(a + 1) * P], ident[:])
                ins.then_inc(sem["qk_psum"], 1)
                ssd(1)
                event("pooled")
                pe.wait_ge(sem["mix_par"], seen("mix_par", 16 * 9))
                for t in range(NT):
                    for c in range(2):
                        ins = pe.matmul(MB[:, t * S + c * P:t * S + (c + 1) * P], um[:, c, t * P:(t + 1) * P],
                                        poolw[:, c, :], start=True, stop=True)
                ins.then_inc(sem["pool_psum"], 1)
                context(1, TB)
                event("qkT")
                for h in range(4):
                    r = slice(64 * (h % 2), 64 * (h % 2) + 64)
                    pe.matmul(psum[:, h, 0:P], qkT[r, h // 2, 0:P], qkT[r, 2 + h // 2, 0:P], start=True, stop=True)
                    ins = pe.matmul(psum[:, h, P:3 * P], qkT[r, h // 2, P:S], qkT[r, 2 + h // 2, :], start=True, stop=True)
                    ins.then_inc(sem["scores"], 1)
                event("pool_out")
                for h in range(5):
                    if h < 4:
                        event("probs")
                        for i in range(3):
                            ins = pe.transpose(psum[:, h, i * P:(i + 1) * P], prob[h % 2][:, i * P:(i + 1) * P], ident[:])
                        ins.then_inc(sem["pT_psum"], 1)
                    if h:
                        event("pT")
                        o, p, v = (h - 1) * 64, pT[(h - 1) % 2], vv[:, :, (h - 1) * 64:h * 64]
                        pe.matmul(MB[:, o:o + 64], p[:, 0:P], v[:, 0], start=True, stop=True)
                        pe.matmul(MB[:, 256 + o:320 + o], p[:, P:2 * P], v[:, 0], start=True, stop=False)
                        ins = pe.matmul(MB[:, 256 + o:320 + o], p[:, 2 * P:3 * P], v[:, 1], start=False, stop=True)
                        ins.then_inc(sem["pv_psum"], 1)
                event("ctx_row")
                to_x()
                for c in range(2):
                    split_in()
                    plain_tok([psum[:, 2 * t + c, :] for t in range(NT)], GC)

            event("silu_c")
            with seen.loop(pe, "pe_layer", DEPTH):
                to_x(); ffn("pe_ff1", N1, True)
                to_x(); mixer()
                to_x(); ffn("pe_ff2", N1, True)
            if stop != "first":
                to_x()
                for n, b in enumerate((4, 6, 4)):
                    if n == 2:
                        event("heads_out")
                    split_in(); plain_tok([psum[:, b + t, :] for t in range(NT)], GC)
                to_x()
                event("heads_out")
                for b in (6, 0):
                    split_in(); plain_tok([psum[:, b + t, 0:256] for t in range(NT)], 256)
                event("heads_out"); event("heads_out")
                event("roped2")
                for y in range(2):
                    for g in range(4):
                        for t in range(NT):
                            a = 4 * y + g
                            ins = pe.transpose(psum[:, a // 2, (a % 2) * S + t * P:(a % 2) * S + (t + 1) * P],
                                               qq[:, t, a * P:(a + 1) * P], ident[:])
                ins.then_inc(sem["qk2_psum"], 1)
                event("k_roped2")
                for y in range(2):
                    for t in range(4):
                        ins = pe.transpose(psum[:, 4 + y, t * P:(t + 1) * P], kk[:, t, y * P:(y + 1) * P], ident[:])
                ins.then_inc(sem["qk2_psum"], 1)
                TILES = [(y, t, v, g) for y in range(2) for t in range(NT) for v in range(2) for g in range(4)]

                def scores(i):
                    y, t, v, g = TILES[i]
                    r = slice(64 * v, 64 * v + 64)
                    mm3(psum[:, i % 2, :], x_hi[r, 4 * y + g, t * P:(t + 1) * P], x_lo[r, 4 * y + g, t * P:(t + 1) * P],
                        k_hi[r, y, :], k_lo[r, y, :], True, True).then_inc(sem["scores2"], 1)

                event("k_split2"); event("q_split2"); event("q_split2")
                scores(0); scores(1)
                for i, (y, t, v, g) in enumerate(TILES):
                    event("probs2")
                    for j in range(4):
                        ins = pe.transpose(psum[:, 2 + i % 2, j * P:(j + 1) * P], prob2[:, i % 2, j * P:(j + 1) * P], ident[:])
                    ins.then_inc(sem["pT2_psum"], 1)
                    if i + 2 < len(TILES):
                        scores(i + 2)
                    event("pT2")
                    h = 4 * v + g
                    for j in range(4):
                        ins = pe.matmul(psum[:, 4 + 2 * y + t, h * 64:(h + 1) * 64], pT2[:, i % 2, j * P:(j + 1) * P],
                                        vk[:, j, y * P + v * 64:y * P + v * 64 + 64], start=j == 0, stop=j == 3)
                    if i % 16 == 15:
                        ins.then_inc(sem["pv2_psum"], 1)
                to_x()
                for c in range(2):
                    split_in(); plain_tok([psum[:, 2 * t + c, :] for t in range(NT)], GC)
                to_x(); ffn("pe_ffn", N1)
                to_x()
                for c, b in enumerate((4, 2, 0, 6, 4, 2)):
                    if c >= 4:
                        event("conv_free")
                    split_in(); plain_tr(halves((b, b + 1)), GC)
                fresh[0] = True
                for c in range(2):
                    split_in(); plain_tok([psum[:, 2 * t + c, :] for t in range(NT)], GC)
                to_x()
                split_in(); plain_tok([MB[:, t * NE:(t + 1) * NE] for t in range(NT)], NE)
                ffn("pe_moe", NM)

        @block.scalar
        def _(act):
            seen = Seen()
            seen.count.update({"a_done": 2, "y_done": 1})
            par = [0]

            def go(*a, **k):
                return nc.scalar.activation(*a, **k)

            def link(ins):
                ins.then_inc(sem["act_step"], 1)
                act.wait_ge(sem["act_step"], seen("act_step"))

            def event(name):
                act.wait_ge(sem[name], seen(name))

            def unit():
                act.wait_ge(sem["a_done"], seen("a_done"))

            def unit_skip():
                seen("a_done")

            def split_piece(j, n=PIECE):
                if j == 0:
                    act.wait_ge(sem["a_done"], seen("a_free"))
                act.wait_ge(sem[f"raw{j}"], seen(f"raw{j}", 16))
                go(a_hi[:, par[0], j, 0:n], raw[:, j, 0:n], ACT.Copy).then_inc(sem["hi"], 1)
                par[0] ^= j

            def split_a(n=PIECE):
                split_piece(0, n)
                split_piece(1, n)

            def split_d():
                act.wait_ge(sem["d_done"], seen("d_free"))
                act.wait_ge(sem["raw2"], seen("raw2", 16))
                go(d_hi[:], raw[:, 2, :], ACT.Copy).then_inc(sem["hi"], 1)

            def hidden_hi():
                event("t_psum")
                go(ht_hi[:].rearrange("p b s -> p (b s)"), TB, ACT.Copy).then_inc(sem["ht_hi"], 1)

            def period(u, ahead):
                if u:
                    hidden_hi()
                if ahead:
                    split_a(ahead)
                event("gu0")
                go(sg[:, 0, :], psum[:, 4, 0:FC], ACT.Silu).then_inc(sem["sg0"], 1)
                if u:
                    split_d()
                unit()
                go(sg[:, 1, :], psum[:, 5, 0:FC], ACT.Silu).then_inc(sem["sg1"], 1)

            def ffn(label, n, nxt):
                period(0, PIECE)
                with seen.loop(act, label, (n - 2) // 2):
                    for _ in range(2):
                        period(1, PIECE)
                if n % 2:
                    period(1, PIECE)
                period(1, nxt)
                act.wait_ge(sem["d_done"], seen("d_free"))
                act.wait_ge(sem["raw2"], seen("raw2", 16))
                go(d_hi[:, 0:D], raw[:, 2, 0:D], ACT.Copy).then_inc(sem["hi"], 1)
                hidden_hi()
                go(d_hi[:, D:2 * D], raw[:, 2, D:2 * D], ACT.Copy).then_inc(sem["hi"], 1)
                table(ACT.Sqrt)

            def table(func):
                c = 1 + (ACT.Sqrt, ACT.Silu, ACT.Exp).index(func)
                go(warm[:, c:c + 1], warm[:, 0:1], func)

            def root(t, width, double):
                go(st[:, 1, t:t + 1], st[:, 0, t:t + 1], ACT.Sqrt, scale=(4.0 if double else 1.0) / width,
                   bias=epsc[:, 1:2] if double else epsc[:, 0:1]).then_inc(sem["root"], 1)

            def norm_rows(src, wait, double=False):
                for t in range(NT):
                    wait(t)
                    link(go(xn[:, t, :], src(t), ACT.Square, accum_out=st[:, 0, t:t + 1]))
                    root(t, D, double)

            def pre_norm(src=lambda t: res[:, t, :], wait=lambda t: event("res_ready")):
                norm_rows(src, wait)

            def post_norm(wait=lambda t: None, double=False):
                norm_rows(lambda t: Y[:, t, :], wait, double)

            def ffn_done(n):
                def wait(t):
                    if t == 0:
                        event("y0")
                    else:
                        act.wait_ge(sem["d_done"], seen("y_done", n))
                return wait

            def to_x():
                event("scale")
                for k in range(KD):
                    if k % 2 == 0:
                        event("xt_psum")
                    go(x_hi[:, k, :], psum[:, k // 2, (k % 2) * S:(k % 2) * S + S], ACT.Identity,
                       bias=gcol[:, 1, k:k + 1], scale=gcol[:, 3, k:k + 1]).then_inc(sem["x_hi"], 1)

            def mixer():
                def conv_out(name, c0):
                    event(f"taps_{name}")
                    for c in range(c0, c0 + 4):
                        ins = go(cT[:, c, :], cT[:, c, :], ACT.Silu, bias=convb[:, c:c + 1])
                    ins.then_inc(sem[f"conv_{name}"], 1)

                split_a(4 * GC)
                unit()
                act.wait_ge(sem["mix_par"], seen("mix_par", 16 * 9))
                tmp = dts[:, 2 * S:3 * S]
                link(go(tmp, MB[0:8, 0:S], ACT.Abs, bias=dtb))
                link(go(tmp, tmp, ACT.Exp, scale=-1.0))
                link(go(tmp, tmp, ACT.Ln, bias=1.0))
                go(dts[:, 3 * S:3 * S + 1], alog, ACT.Exp).then_inc(sem["soft"], 1)
                split_a(4 * GC)
                unit()
                go(xT[:, 4:8, CPAD:CPAD + S], psum[:, 4:6, :].rearrange("p b (h s) -> p (b h) s", s=S), ACT.Copy).then_inc(sem["bc_out"], 1)
                split_a(4 * GC)
                unit()
                go(xT[:, 0:4, CPAD:CPAD + S], psum[:, 0:2, :].rearrange("p b (h s) -> p (b h) s", s=S), ACT.Copy).then_inc(sem["xs_out"], 1)
                split_a(4 * GC)
                unit()
                go(qk[:, :, 0:256], psum[:, 3, :].rearrange("p (t n) -> p t n", t=NT), ACT.Copy)
                go(uw[0][:, :, PAD:PAD + S], psum[:, 2, :].rearrange("p (c s) -> p c s", s=S), ACT.Copy).then_inc(sem["uq_out"], 1)
                conv_out("bc", 4)
                split_a(4 * GC)
                unit()
                kv = psum[:, 4:6, :]
                go(vv, kv[:, :, 256:512], ACT.Copy)
                go(qk[:, :, 256:512], kv[:, :, 0:256], ACT.Copy).then_inc(sem["kv_out"], 1)
                conv_out("xs", 0)
                unit()
                go(zs, psum[:, 0:2, :], ACT.Silu).then_inc(sem["z_out"], 1)
                for g in range(2):
                    event("arg")
                    go(arg[g], arg[g], ACT.Exp).then_inc(sem["decay"], 1)
                event("qk_psum")
                go(qkT, psum[:, 2:4, :].rearrange("p b (h s) -> p (b h) s", s=S), ACT.Copy).then_inc(sem["qkT"], 1)
                event("pool_psum")
                go(xn[:, :, 512:768], MB.rearrange("p (t n) -> p t n", t=NT), ACT.Copy).then_inc(sem["pool_out"], 1)
                event("gated")
                for t in range(NT):
                    ins = go(xsd[:, t, :], xdt[:, t, :], ACT.Square, accum_out=st[:, 0, t:t + 1])
                link(ins)
                for j in range(2):
                    seen(f"raw{j}", 32)

                def exps(h):
                    event("amax")
                    for t in range(NT):
                        ap = prob[h % 2][:, 0:P] if t == 0 else prob[h % 2][:, P:3 * P]
                        ins = go(ap, ap, ACT.Exp, bias=qstat[:, 0, h, t:t + 1], accum_out=qstat[:, 1, h, t:t + 1])
                    ins.then_inc(sem["probs"], 1)

                def pT_out(h):
                    event("pT_psum")
                    go(pT[h % 2], psum[:, h, 0:384], ACT.Copy).then_inc(sem["pT"], 1)
                exps(0); exps(1); pT_out(0)
                split_piece(0)
                exps(2); pT_out(1); exps(3)
                split_piece(1)
                pT_out(2); pT_out(3)
                for t in range(NT):
                    root(t, SSD_IN, False)
                act.wait_ge(sem["ctx_stored"], seen("ctx_stored", 32))
                to_x()
                split_a()

            event("consts_in")
            go(cs[:].rearrange("p k r -> p r k"), small[:, 128:144].rearrange("p (r k) -> p r k", k=KD), ACT.Silu).then_inc(sem["silu_c"], 1)
            split_a()
            with seen.loop(act, "act_layer", DEPTH):
                pre_norm(); to_x(); table(ACT.Silu); ffn("act_ff1", N1, 4 * 8)
                post_norm(ffn_done(N1), True)
                pre_norm(); to_x(); mixer()
                unit()
                split_a()
                unit()
                post_norm()
                pre_norm(); to_x(); table(ACT.Silu); ffn("act_ff2", N1, None)
                split_a()
                post_norm(ffn_done(N1), True)
            if stop != "first":
                q5 = qq.rearrange("p t (y g v d) -> p t y v g d", y=2, v=2, d=64)

                def heads(ap):
                    return ap.rearrange("p (g d) -> p g d", d=64)
                pre_norm(); to_x()
                split_a()
                act.wait_ge(sem["ctx_in"], 16)
                pre_norm(lambda t: ctxr[:, t, :], lambda t: None)
                unit()
                for t in range(NT):
                    for v in range(2):
                        ins = go(q5[:, t, 0, v], heads(psum[:, 4 + t, v * 256:(v + 1) * 256]), ACT.Copy)
                ins.then_inc(sem["heads_out"], 1)
                split_a()
                unit()
                go(kk[:, 2:4, 0:P], psum[:, 6:8, 0:P], ACT.Copy)
                go(vk[:, 2:4, 0:P], psum[:, 6:8, P:2 * P], ACT.Copy)
                for t in range(NT):
                    ins = go(q5[:, t, 1, 0], heads(psum[:, 6 + t, 256:512]), ACT.Copy)
                ins.then_inc(sem["heads_out"], 1)
                split_a(4 * 256)
                unit()
                to_x()
                split_a(4 * 256)
                for t in range(NT):
                    go(q5[:, t, 1, 1], heads(psum[:, 4 + t, 0:256]), ACT.Copy)
                go(vk[:, 2:4, P:2 * P], psum[:, 4:6, 384:512], ACT.Copy)
                link(go(kk[:, 2:4, P:2 * P], psum[:, 4:6, 256:384], ACT.Copy))
                go(qsq, qq.rearrange("p t n -> p (t n)"), ACT.Square)
                go(ksq[:, 512:1024], kk[:, 2:4, :].rearrange("p t n -> p (t n)"), ACT.Square).then_inc(sem["squares"], 1)
                event("head_ssq")
                go(head_rms, head_rms, ACT.Sqrt, scale=1.0 / 64, bias=epsc[:, 0:1]).then_inc(sem["head_root"], 1)
                for y, b in ((0, 6), (1, 0)):
                    unit()
                    ins = go(kk[:, 0:2, y * P:(y + 1) * P], psum[:, b:b + 2, 0:P], ACT.Copy)
                    go(vk[:, 0:2, y * P:(y + 1) * P], psum[:, b:b + 2, P:2 * P], ACT.Copy).then_inc(sem["heads_out"], 1)
                link(ins)
                go(ksq[:, 0:512], kk[:, 0:2, :].rearrange("p t n -> p (t n)"), ACT.Square).then_inc(sem["squares"], 1)
                event("head_ssq")
                go(ctx_rms, ctx_rms, ACT.Sqrt, scale=1.0 / 64, bias=epsc[:, 0:1]).then_inc(sem["head_root"], 1)
                table(ACT.Exp)
                event("qk2_psum")
                blocks = psum[:, 0:4, :].rearrange("p b (h s) -> p (b h) s", s=S)
                go(x_hi[:, 0:4, :], blocks[:, 0:4], ACT.Copy).then_inc(sem["qk_hi2"], 1)
                go(x_hi[:, 4:8, :], blocks[:, 4:8], ACT.Copy).then_inc(sem["qk_hi2"], 1)
                event("qk2_psum")
                go(k_hi, psum[:, 4:6, :], ACT.Copy).then_inc(sem["qk_hi2"], 1)
                tiles = [y * 16 + t * 8 + v * 4 + g for y in range(2) for t in range(NT) for v in range(2) for g in range(4)]

                def exps(i):
                    event("amax2")
                    n = tiles[i]
                    go(prob2[:, i % 2, :], psum[:, i % 2, :], ACT.Exp, scale=64.0 ** -0.5, bias=sm2[:, 1, n:n + 1],
                       accum_out=sm2[:, 2, n:n + 1]).then_inc(sem["probs2"], 1)

                exps(0)
                for i in range(32):
                    if i < 31:
                        exps(i + 1)
                    if i in (2, 6, 12, 16):
                        split_piece(int(i in (6, 16)))
                    event("pT2_psum")
                    go(pT2[:, i % 2, :], psum[:, 2 + i % 2, :], ACT.Copy).then_inc(sem["pT2"], 1)
                event("sink_arg")
                go(sm2[:, 0, 16:32], sm2[:, 0, 16:32], ACT.Exp).then_inc(sem["sink_exp"], 1)
                to_x()
                unit()
                split_a()
                unit()
                pre_norm(); to_x(); table(ACT.Silu); ffn("act_ffn", N1, PIECE)
                pre_norm(); to_x()
                for half in range(2):
                    split_a(); unit()
                    go(cg, psum[:, 4 + 2 * half:6 + 2 * half, :].rearrange("p b (h s) -> p (b h) s", s=S), ACT.Copy).then_inc(sem["cg"], 1)
                    split_a(); unit()
                    split_a(); unit()
                    if half == 0:
                        event("cg_used")
                event("mixed_conv")
                for k in range(KD):
                    go(x_hi[:, k, :], mod[:, k, :], ACT.Copy).then_inc(sem["x_hi"], 1)
                split_a()
                unit()
                split_a(4 * NE)
                unit()
                pre_norm(); to_x()
                split_a()
                unit()
                event("top2")
                go(lg[:, 6, :, 0:1], lg[:, 6, :, 0:1], ACT.Exp).then_inc(sem["top2_exp"], 1)
                ffn("act_moe", NM, None)

        @block.vector
        def _(dve):
            seen = Seen()
            seen.count.update({"a_done": 2, "y_done": 1})
            par = [0]
            dve.sem_inc(sem["ada_row"], 2)
            dve.sem_inc(sem["x_lo"], KD)
            for q in range(2):
                dve.sem_inc(sem[f"ada_acc{q}"], 1)
            for j in range(3):
                dve.sem_inc(sem[f"split{j}"], 1)
            V = nc.vector

            def link(ins):
                ins.then_inc(sem["dve_step"], 1)
                dve.wait_ge(sem["dve_step"], seen("dve_step"))

            def event(name, n=1):
                dve.wait_ge(sem[name], seen(name, n))

            def unit():
                dve.wait_ge(sem["a_done"], seen("a_done"))

            def unit_skip(n=1):
                seen("a_done", n)

            def split_piece(j, n=PIECE):
                event("hi")
                V.tensor_tensor(a_lo[:, par[0], j, 0:n], raw[:, j, 0:n], f(a_hi[:, par[0], j, 0:n]),
                                ALU.subtract).then_inc(sem[f"split{j}"], 1)
                par[0] ^= j

            def split_a(n=PIECE):
                split_piece(0, n)
                split_piece(1, n)

            def split_d():
                event("hi")
                V.tensor_tensor(d_lo[:], raw[:, 2, :], f(d_hi[:]), ALU.subtract).then_inc(sem["split2"], 1)

            def hidden_lo():
                event("ht_hi")
                V.tensor_tensor(ht_lo[:].rearrange("p b s -> p (b s)"), TB, f(ht_hi[:]).rearrange("p b s -> p (b s)"),
                                ALU.subtract).then_inc(sem["ht"], 1)

            def hidden(t, scale):
                event(f"sg{t}")
                up = psum[:, 4 + t, FC:2 * FC]
                if scale is None:
                    V.tensor_tensor(hb[:, t, :], sg[:, t, :], up, ALU.mult).then_inc(sem[f"h{t}"], 1)
                else:
                    V.scalar_tensor_tensor(hb[:, t, :], sg[:, t, :], scale(t), up, ALU.mult, ALU.mult).then_inc(sem[f"h{t}"], 1)

            def period(u, ahead, scale=None, ada=None):
                if u:
                    hidden_lo()
                if ahead:
                    split_a(ahead)
                hidden(0, scale)
                if u:
                    split_d()
                if ada is not None:
                    event(f"ada_in{ada}", 16)
                    for k in range(KD):
                        w, a = adaw[:, ada, k, :], adaa[:, ada, :]
                        if k == 0:
                            ins = V.tensor_scalar(a, w, cs[:, k, 1:2], None, ALU.mult)
                        else:
                            ins = V.scalar_tensor_tensor(a, w, cs[:, k, 1:2], a, ALU.mult, ALU.add)
                        if k < KD - 1:
                            link(ins)
                    ins.then_inc(sem[f"ada_acc{ada}"], 1)
                hidden(1, scale)
                if ada is not None:
                    event("ada_sum")
                    event(f"ada_bias{ada}", 16)
                    V.tensor_tensor(adar[:, ada, :], MB[0:1, 0:AC], adar[:, ada, :], ALU.add).then_inc(sem["ada_row"], 1)

            def ffn(label, n, nxt, scale=None, ada=False):
                s = scale or (lambda u: None)
                period(0, PIECE, s(0))
                with seen.loop(dve, label, (n - 2) // 2) as i:
                    for q in range(2):
                        period(1, PIECE, s(i * 2 + (1 + q)), q if ada else None)
                if n % 2:
                    period(1, PIECE, s(n - 2))
                period(1, nxt, s(n - 1))
                event("hi")
                V.tensor_tensor(d_lo[:, 0:D], raw[:, 2, 0:D], f(d_hi[:, 0:D]), ALU.subtract).then_inc(sem["d_half"], 1)
                hidden_lo()
                event("hi")
                V.tensor_tensor(d_lo[:, D:2 * D], raw[:, 2, D:2 * D], f(d_hi[:, D:2 * D]), ALU.subtract).then_inc(sem["split2"], 1)
                unit_skip(n)

            def pre_norm(src=lambda t: res[:, t, :]):
                for t in range(NT):
                    event("root")
                    link(V.reciprocal(st[:, 1, t:t + 1], st[:, 1, t:t + 1]))
                    for c in (slice(0, D),) if t == 0 else (slice(0, D // 2), slice(D // 2, D)):
                        V.tensor_scalar(xn[:, t, c], src(t)[:, c], st[:, 1, t:t + 1], None, ALU.mult).then_inc(sem["xn_ready"], 1)

            def to_x(n_gain=1, extra=None):
                event("gain", 16 * n_gain)
                if extra:
                    event(extra)
                V.scalar_tensor_tensor(gcol[:, 3, :], gcol[:, 2, :], 1.0, gcol[:, 0, :], ALU.add, ALU.mult).then_inc(sem["scale"], 1)
                for pair in range(KD // 2):
                    event("x_hi", 2)
                    for k in (2 * pair, 2 * pair + 1):
                        V.tensor_scalar(mod[:, k, :], psum[:, k // 2, (k % 2) * S:(k % 2) * S + S], gcol[:, 3, k:k + 1],
                                        gcol[:, 1, k:k + 1], ALU.mult, ALU.add).then_inc(sem["dve_step"], 1)
                    for k in (2 * pair, 2 * pair + 1):
                        event("dve_step")
                        V.tensor_tensor(x_lo[:, k, :], mod[:, k, :], f(x_hi[:, k, :]), ALU.subtract).then_inc(sem["x_lo"], 1)

            def ffn_done(n):
                def wait(t):
                    if t == 0:
                        event("y0")
                    else:
                        dve.wait_ge(sem["d_done"], seen("y_done", n))
                return wait

            def post_norm(wait=lambda t: None, normed=True):
                event("gain_row", 16)
                for t in range(NT):
                    wait(t)
                    if normed:
                        event("root")
                        link(V.reciprocal(st[:, 1, t:t + 1], st[:, 1, t:t + 1]))
                        ins = V.scalar_tensor_tensor(xn[:, t, :], Y[:, t, :], st[:, 1, t:t + 1], gbc[:], ALU.mult, ALU.mult)
                    else:
                        ins = V.tensor_tensor(xn[:, t, :], Y[:, t, :], gbc[:], ALU.mult)
                    link(ins)
                    V.tensor_tensor(res[:, t, :], res[:, t, :], xn[:, t, :], ALU.add).then_inc(sem["res_ready"], 1)

            def mixer():
                split_a(4 * GC)
                event("mix_par", 16 * 9)
                event("soft")
                a, b = dts[:, 0:S], dts[:, S:2 * S]
                link(V.tensor_scalar(a, MB[0:8, 0:S], dtb, 0.0, ALU.add, ALU.max))
                link(V.tensor_tensor(a, a, dts[:, 2 * S:3 * S], ALU.add))
                link(V.tensor_scalar(dts[:, 2 * S:3 * S], a, dts[:, 3 * S:3 * S + 1], -1.0, ALU.mult, ALU.mult))
                link(V.memset(dts[:, 3 * S:4 * S], 1.0))
                V.tensor_tensor_scan(b, dts[:, 3 * S:4 * S], dts[:, 2 * S:3 * S], 0.0, ALU.mult, ALU.add).then_inc(sem["acs_rows"], 1)
                split_a(4 * GC)
                link(V.memset(xT[:, :, 0:CPAD], 0.0))
                event("bc_out")

                def taps(name, c0):
                    for j in range(4):
                        for c in range(c0, c0 + 4):
                            src = xT[:, c, j:j + S]
                            w = convw[:, j, c:c + 1]
                            if j == 0:
                                ins = V.tensor_scalar(cT[:, c, :], src, w, None, ALU.mult)
                            else:
                                ins = V.scalar_tensor_tensor(cT[:, c, :], src, w, cT[:, c, :], ALU.mult, ALU.add)
                        if j < 3:
                            link(ins)
                    ins.then_inc(sem[f"taps_{name}"], 1)
                taps("bc", 4)
                split_a(4 * GC)
                event("xs_out")
                taps("xs", 0)
                split_a(4 * GC)
                split_a(4 * GC)
                unit_skip(6)
                def context_row(c, bank):
                    if c == 0:
                        event("ctx_bias", 32)
                    event("ctx_used1")
                    V.tensor_tensor(crow[c], bank[0:1, :], crow[c], ALU.add).then_inc(sem["ctx_row"], 1)

                event("dt_psum")
                TB3 = TB[:, 0:32].rearrange("p (i t h) -> p i t h", i=2, t=NT)
                V.tensor_copy(dtc, TB3[:, 0])
                V.tensor_scalar(nacs, TB3[:, 1], -1.0, None, ALU.mult).then_inc(sem["dtc"], 1)
                event("kv_out")
                x = qk.rearrange("p t (h d) -> p t h d", d=64)
                r = area(7712, 4, NT, 64).rearrange("p i t (h d) -> p i t h d", d=8)
                for i, (part, trig) in enumerate(((0, 0), (1, 1), (1, 0), (0, 1))):
                    tb = rope[:, :, 8 * trig:8 * trig + 8].unsqueeze(2).broadcast_to([P, NT, 8, 8])
                    for t in range(NT):
                        ins = V.tensor_tensor(r[:, i, t], x[:, t, :, 8 * part:8 * part + 8], tb[:, t], ALU.mult)
                link(ins)
                for t in range(NT):
                    V.tensor_tensor(x[:, t, :, 0:8], r[:, 0, t], r[:, 1, t], ALU.subtract)
                    ins = V.tensor_tensor(x[:, t, :, 8:16], r[:, 2, t], r[:, 3, t], ALU.add)
                ins.then_inc(sem["roped"], 1)
                def decay(g):
                    event("acs_psum")
                    for h in range(4):
                        ps = psum[:, 2 + h // 2, (h % 2) * S:(h % 2) * S + S]
                        V.scalar_tensor_tensor(arg[g][:, h, 0:S], ps, nacs[:, 0, 4 * g + h:4 * g + h + 1], cmask[:, 0:S], ALU.add, ALU.add)
                        ins = V.scalar_tensor_tensor(arg[g][:, h, S:S + P], ps[:, P:S], nacs[:, 1, 4 * g + h:4 * g + h + 1],
                                                     cmask[:, 0:P], ALU.add, ALU.add)
                    ins.then_inc(sem["arg"], 1)

                def segment(g):
                    event("decay")
                    cb = (TB, MB)[g][:, 0:384].unsqueeze(1).broadcast_to([P, 4, 384])
                    V.tensor_tensor(arg[g], arg[g], cb, ALU.mult).then_inc(sem["seg"], 1)

                decay(0)
                event("xs_psum")
                for t in range(NT):
                    xs = psum[:, t, :].rearrange("p (h d) -> p h d", d=HP)
                    for dst, col in ((xdt, dtc[:, t, :]), (xsd, dskip)):
                        ins = V.tensor_tensor(dst[:, t, :].rearrange("p (h d) -> p h d", d=HP), xs,
                                              col.unsqueeze(2).broadcast_to([P, HEADS, HP]), ALU.mult)
                ins.then_inc(sem["xdt"], 1)
                event("cb_psum")
                segment(0)
                decay(1)
                segment(1)
                context_row(0, psum[:, 4, :])
                event("ssd_psum")
                event("ssd_psum")
                for t in range(NT):
                    ins = V.tensor_tensor(xdt[:, t, :], psum[:, 4 + t, :], xsd[:, t, :], ALU.add)
                link(ins)
                for t in range(NT):
                    ins = V.tensor_tensor(xdt[:, t, :], xdt[:, t, :], zs[:, t, :], ALU.mult)
                ins.then_inc(sem["gated"], 1)
                scale = 64.0 ** -0.5

                def head(h):
                    event("scores")
                    if h >= 2:
                        event("pT_psum")
                    p = prob[h % 2]
                    link(V.scalar_tensor_tensor(p, psum[:, h, 0:384], scale, qmask[:], ALU.mult, ALU.add))
                    V.reduce_max(qstat[:, 0, h, 0:1], p[:, 0:P], AX)
                    link(V.reduce_max(qstat[:, 0, h, 1:2], p[:, P:3 * P], AX))
                    V.tensor_scalar(qstat[:, 0, h, :], qstat[:, 0, h, :], -1.0, None, ALU.mult).then_inc(sem["amax"], 1)
                head(0); head(1)
                context_row(1, TB)
                head(2)
                split_piece(0)
                head(3)
                split_piece(1)
                for t in range(NT):
                    event("root")
                    link(V.reciprocal(st[:, 1, t:t + 1], st[:, 1, t:t + 1]))
                    V.tensor_scalar(xn[:, t, 0:SSD_IN], xdt[:, t, :], st[:, 1, t:t + 1], None, ALU.mult)
                event("pT_psum", 2)
                event("probs", 4)
                link(V.reciprocal(qstat[:, 2], qstat[:, 1]))
                event("pv_psum", 4)
                for t in range(NT):
                    ins = V.tensor_tensor(xn[:, t, 768:D].rearrange("p (h d) -> p h d", d=64),
                                          MB[:, t * 256:(t + 1) * 256].rearrange("p (h d) -> p h d", d=64),
                                          qstat[:, 2, :, t:t + 1].broadcast_to([P, 4, 64]), ALU.mult)
                event("pool_out")
                V.tensor_copy(small[:, 120:121], epsc[:, 0:1]).then_inc(sem["xn_ready"], 3)
                to_x(2, "gain_one")
                split_a()

            event("consts_in")
            event("silu_c")
            V.tensor_copy(small[:, 120:121], epsc[:, 0:1]).then_inc(sem["res_ready"], 2)
            split_a()
            with seen.loop(dve, "dve_layer", DEPTH):
                pre_norm(); to_x(); ffn("dve_ff1", N1, 4 * 8, ada=True)
                post_norm(ffn_done(N1))
                pre_norm(); to_x(); mixer()
                unit_skip()
                split_a()
                unit()
                post_norm()
                pre_norm(); to_x(); ffn("dve_ff2", N1, None, ada=True)
                split_a()
                post_norm(ffn_done(N1))
            if stop == "first":
                V.tensor_copy(small[:, 121:122], epsc[:, 0:1]).then_inc(sem["final"], 1)
            else:
                pre_norm(); to_x(3)
                split_a()
                pre_norm(lambda t: ctxr[:, t, :])
                event("att_in", 16 * 8)
                split_a()
                V.tensor_scalar(nsink, nsink, -1.0, None, ALU.mult)
                split_a(4 * 256)
                to_x(3)
                split_a(4 * 256)
                unit_skip(5)

                def scaled(x, n, c):
                    x = x.rearrange("p t (h d) -> p (t h) d", d=64)
                    return V.tensor_tensor(x, x, rms[:, c:c + n].unsqueeze(2).broadcast_to([P, n, 64]), ALU.mult)

                def gained(t, y, q):
                    x = qq[:, t, y * 512:(y + 1) * 512] if q else kk[:, t, y * P:(y + 1) * P]
                    x = x.rearrange("p (h d) -> p h d", d=64)
                    g = qkg[:, y:y + 1, :] if q else qkg[:, 2 + y:3 + y, :]
                    return V.tensor_tensor(x, x, g.broadcast_to(list(x.shape)), ALU.mult)

                tmp = mod[:].rearrange("p k s -> p (k s)").rearrange("p (i h d) -> p i h d", i=4, d=32)

                def turned(x, t, nh):
                    x = x.rearrange("p (h d two) -> p h d two", d=32, two=2)
                    for i, (side, trig) in enumerate(((0, 0), (1, 1), (0, 1), (1, 0))):
                        tb = rope2[:, t, 32 * trig:32 * trig + 32].unsqueeze(1).broadcast_to([P, nh, 32])
                        ins = V.tensor_tensor(tmp[:, i, 0:nh], x[:, :, :, side], tb, ALU.mult)
                    link(ins)
                    V.tensor_tensor(x[:, :, :, 0], tmp[:, 0, 0:nh], tmp[:, 1, 0:nh], ALU.subtract)
                    return V.tensor_tensor(x[:, :, :, 1], tmp[:, 2, 0:nh], tmp[:, 3, 0:nh], ALU.add)

                link(V.memset(rms[:, 32:40], 1.0))
                event("squares")
                V.reduce_sum(rms[:, 0:32], qsq.rearrange("p (h d) -> p h d", d=64), AX)
                V.reduce_sum(rms[:, 40:48], ksq[:, 512:1024].rearrange("p (h d) -> p h d", d=64), AX).then_inc(sem["head_ssq"], 1)
                event("head_root")
                link(V.reciprocal(rms, rms))
                scaled(kk[:, 2:4, :], 8, 40)
                link(scaled(qq, 32, 0))
                for t in range(NT):
                    for y in range(2):
                        gained(t, y, True)
                        ins = gained(2 + t, y, False)
                link(ins)
                for t in range(NT):
                    link(turned(qq[:, t, :], t, 16))
                V.tensor_copy(small[:, 239:240], epsc[:, 0:1]).then_inc(sem["roped2"], 1)
                for t in range(NT):
                    link(turned(kk[:, 2 + t, :], t, 4))
                event("squares")
                V.reduce_sum(ctx_rms, ksq[:, 0:512].rearrange("p (h d) -> p h d", d=64), AX).then_inc(sem["head_ssq"], 1)
                event("head_root")
                link(V.reciprocal(ctx_rms, ctx_rms))
                link(scaled(kk[:, 0:2, :], 8, 32))
                for t in range(NT):
                    for y in range(2):
                        ins = gained(t, y, False)
                ins.then_inc(sem["k_roped2"], 1)
                blocks = psum[:, 0:4, :].rearrange("p b (h s) -> p (b h) s", s=S)
                for y in range(2):
                    event("qk_hi2")
                    V.tensor_tensor(x_lo[:, 4 * y:4 * y + 4, :], blocks[:, 4 * y:4 * y + 4], f(x_hi[:, 4 * y:4 * y + 4, :]),
                                    ALU.subtract).then_inc(sem["q_split2"], 1)
                event("qk_hi2")
                V.tensor_tensor(k_lo, psum[:, 4:6, :], f(k_hi), ALU.subtract).then_inc(sem["k_split2"], 1)
                i = 0
                for y in range(2):
                    for t in range(NT):
                        for h in range(8):
                            n = y * 16 + t * 8 + h
                            event("scores2")
                            if y:
                                link(V.tensor_tensor(psum[:, i % 2, S:2 * S], psum[:, i % 2, S:2 * S], band[:, t, :], ALU.add))
                            link(V.reduce_max(sm2[:, 0, n:n + 1], psum[:, i % 2, :], AX))
                            if y:
                                ins = V.tensor_scalar(sm2[:, 1, n:n + 1], sm2[:, 0, n:n + 1], -(64.0 ** -0.5), nsink[:, h:h + 1], ALU.mult, ALU.min)
                            else:
                                ins = V.tensor_scalar(sm2[:, 1, n:n + 1], sm2[:, 0, n:n + 1], -(64.0 ** -0.5), None, ALU.mult)
                            ins.then_inc(sem["amax2"], 1)
                            if i in (4, 8, 14, 18):
                                split_piece(int(i in (8, 18)))
                            i += 1
                event("probs2", 32)
                for t in range(NT):
                    s = slice(16 + 8 * t, 24 + 8 * t)
                    ins = V.tensor_tensor(sm2[:, 0, s], sm2[:, 1, s], nsink, ALU.subtract)
                ins.then_inc(sem["sink_arg"], 1)
                event("sink_exp")
                link(V.tensor_tensor(sm2[:, 2, 16:32], sm2[:, 2, 16:32], sm2[:, 0, 16:32], ALU.add))
                link(V.reciprocal(sm2[:, 3, :], sm2[:, 2, :]))
                event("pv2_psum", 2)
                for y in range(2):
                    for t in range(NT):
                        n = 16 * y + 8 * t
                        ins = V.tensor_tensor(xn[:, t, y * 512:(y + 1) * 512].rearrange("p (h d) -> p h d", d=64),
                                              psum[:, 4 + 2 * y + t, :].rearrange("p (h d) -> p h d", d=64),
                                              sm2[:, 3, n:n + 8].unsqueeze(2).broadcast_to([P, 8, 64]), ALU.mult)
                ins.then_inc(sem["xn_ready"], 3)
                to_x(0, "gain_one")
                unit_skip()
                split_a()
                unit()
                post_norm(lambda t: None, False)
                pre_norm(); to_x(3); ffn("dve_ffn", N1, PIECE)
                post_norm(ffn_done(N1), False)
                pre_norm(); to_x(3)
                V.memset(zT[:, :, 0:1], 0.0)
                V.memset(zT[:, :, S + 1:S + 2], 0.0)
                banks = ((4, 2, 0), (6, 4, 2))

                def blocks4(b):
                    return psum[:, b:b + 2, :].rearrange("p b (h s) -> p (b h) s", s=S)
                for half in range(2):
                    split_a()
                    unit()
                    event("cg")
                    if half == 0:
                        V.tensor_copy(small[:, 241:242], epsc[:, 0:1]).then_inc(sem["conv_free"], 1)
                    split_a()
                    unit()
                    ins = V.tensor_tensor(zT[:, :, 1:S + 1], cg, blocks4(banks[half][1]), ALU.mult)
                    link(ins)
                    if half == 0:
                        V.tensor_copy(small[:, 242:243], epsc[:, 0:1]).then_inc(sem["conv_free"], 1)
                        V.tensor_copy(small[:, 243:244], epsc[:, 0:1]).then_inc(sem["cg_used"], 1)
                    split_a()
                    for j in range(3):
                        for c in range(4):
                            w = convw2[:, j, 4 * half + c:4 * half + c + 1]
                            if j == 0:
                                ins = V.tensor_scalar(acc[:, c, :], zT[:, c, 0:S], w, None, ALU.mult)
                            else:
                                ins = V.scalar_tensor_tensor(acc[:, c, :], zT[:, c, j:j + S], w, acc[:, c, :], ALU.mult, ALU.add)
                        link(ins)
                    unit()
                    ins = V.tensor_tensor(mod[:, 4 * half:4 * half + 4, :], acc, blocks4(banks[half][2]), ALU.mult)
                    if half == 1:
                        ins.then_inc(sem["mixed_conv"], 1)
                for k in range(KD):
                    event("x_hi")
                    V.tensor_tensor(x_lo[:, k, :], mod[:, k, :], f(x_hi[:, k, :]), ALU.subtract).then_inc(sem["x_lo"], 1)
                split_a()
                unit_skip()
                split_a(4 * NE)
                unit()
                post_norm(lambda t: None, False)
                pre_norm(); to_x(3)
                split_a()
                unit()
                L, e1, c1, f1, L2, f2, m, g8 = (lg[:, i] for i in range(8))
                link(V.tensor_copy(L, MB[:, 0:2 * NE].rearrange("p (t e) -> p t e", e=NE)))
                ones8 = small[:, 244:252]
                link(V.memset(ones8, 1.0))

                def first_max(src, dst, col):
                    link(V.reduce_max(m[:, :, col:col + 1], src, AX))
                    for t in range(NT):
                        ins = V.tensor_scalar(e1[:, t, :], src[:, t, :], m[:, t, col:col + 1], None, ALU.is_equal)
                    link(ins)
                    for t in range(NT):
                        ins = V.tensor_tensor_scan(c1[:, t, :], ones8, e1[:, t, :], 0.0, ALU.mult, ALU.add)
                    link(ins)
                    link(V.scalar_tensor_tensor(dst, c1, 1.0, e1, ALU.is_equal, ALU.mult))

                first_max(L, f1, 1)
                link(V.scalar_tensor_tensor(L2, f1, NEG, L, ALU.mult, ALU.add))
                first_max(L2, f2, 2)
                V.tensor_tensor(m[:, :, 0:1], m[:, :, 2:3], m[:, :, 1:2], ALU.subtract).then_inc(sem["top2"], 1)
                event("top2_exp")
                link(V.tensor_scalar(m[:, :, 3:4], m[:, :, 0:1], 1.0, None, ALU.add))
                link(V.reciprocal(m[:, :, 3:4], m[:, :, 3:4]))
                link(V.tensor_tensor(m[:, :, 4:5], m[:, :, 0:1], m[:, :, 3:4], ALU.mult))
                for t in range(NT):
                    ins = V.tensor_scalar(g8[:, t, :], f1[:, t, :], m[:, t, 3:4], None, ALU.mult)
                link(ins)
                for t in range(NT):
                    ins = V.scalar_tensor_tensor(g8[:, t, :], f2[:, t, :], m[:, t, 4:5], g8[:, t, :], ALU.mult, ALU.add)
                link(ins)
                for t in range(NT):
                    ins = V.tensor_copy(gexp[:, t, :].rearrange("p (e c) -> p e c", c=NX),
                                        g8[:, t, :].unsqueeze(2).broadcast_to([P, NE, NX]))
                link(ins)
                ffn("dve_moe", NM, None, lambda u: (lambda t: gexp[:, t, bass.ds(u, 1)]))
                post_norm(ffn_done(NM), False)
                V.tensor_copy(small[:, 121:122], epsc[:, 0:1]).then_inc(sem["final"], 1)


NAMES = [
    "x", "ff1_norm_pre", "ff1_w_gate", "ff1_w_up", "ff1_w_down", "ff1_norm_post", "mix_norm_pre", "w_in",
    "conv_w", "conv_b", "dt_bias", "a_log", "d_skip", "ssd_norm", "pool_w", "pool_scale", "w_out",
    "mix_norm_post", "ff2_norm_pre", "ff2_w_gate", "ff2_w_up", "ff2_w_down", "ff2_norm_post", "c_2",
    "ctx_2", "c_ctx_2", "ada_w_2", "ada_b_2", "norm1_g_2", "norm2_g_2", "attn_w_in_2", "attn_w_out_2",
    "qnorm_a_2", "knorm_a_2", "qnorm_b_2", "knorm_b_2", "sink_b_2", "ffn_w_gate_2", "ffn_w_up_2",
    "ffn_w_down_2", "conv_w_in_2", "conv_w_2", "conv_w_out_2", "router_w_2", "moe_w_gate_2",
    "moe_w_up_2", "moe_w_down_2"]


def constants():
    f4 = np.float32
    i, j = np.arange(P)[:, None], np.arange(P)[None, :]
    low = np.where(j <= i, 0.0, NEG)
    z = np.zeros((P, P))
    tok = np.arange(S, dtype=f4)
    inv = (f4(500000.0) ** (-np.arange(0, 16, 2, dtype=f4) / f4(16))).astype(f4)
    ang = (tok[:, None] * inv[None, :]).astype(f4)
    rope = np.concatenate([np.cos(ang), np.sin(ang)], -1).reshape(NT, P, 16).transpose(1, 0, 2)
    cnt = np.empty((P, 2, S))
    for g in range(4):
        cnt[64 * (g % 2):64 * (g % 2) + 64, g // 2, :] = 1.0 / np.minimum(np.arange(1, S + 1), 2 ** (g + 1))
    inv2 = (f4(10000.0) ** (-np.arange(0, 32, 2, dtype=f4) / f4(32))).astype(f4)
    row, col = np.divmod(np.arange(S), 64)
    ang2 = np.concatenate([row[:, None].astype(f4) * inv2, col[:, None].astype(f4) * inv2], -1).astype(f4)
    rope2 = np.concatenate([np.cos(ang2), np.sin(ang2)], -1).reshape(NT, P, 64).transpose(1, 0, 2)
    q, k = np.arange(S)[:, None], np.arange(S)[None, :]
    band = np.where(np.abs(q - k) <= 128, 0.0, NEG).reshape(NT, P, S).transpose(1, 0, 2)
    return {k_: np.ascontiguousarray(v, dtype=f4) for k_, v in {
        "c_ident": np.eye(P), "c_cmask": np.concatenate([low.T, z], 1), "c_qmask": np.concatenate([low, z, low], 1),
        "c_rope": rope, "c_rcnt": cnt, "c_rope2": rope2, "c_band": band}.items()}


def kernel(**inputs):
    from concourse import bacc
    from concourse.bass_utils import run_bass_kernel_spmd

    nc = bacc.Bacc("TRN2", target_bir_lowering=False, num_devices=1)
    arrays = {}
    for name in NAMES:
        arrays[name] = np.ascontiguousarray(inputs[name])
    arrays.update(constants())
    T = {}
    for name, a in arrays.items():
        T[name] = nc.dram_tensor(f"in_{name}", a.shape, F32, kind="ExternalInput").ap()
    out = nc.dram_tensor("out_0", (1, S, D), F32, kind="ExternalOutput").ap()
    mods = nc.dram_tensor("mods", (DEPTH, 2, ADA), F32).ap()
    build(nc, T, out, mods)
    r = run_bass_kernel_spmd(nc, [{f"in_{k}": v for k, v in arrays.items()}], core_ids=[0])
    return r.results[0]["out_0"]
```
